# Optimizing a Trainium2 kernel written in Bass

```python
import math
import jax, jax.numpy as jnp
from jax import lax
import numpy as np

D_MODEL = 2048
BATCH = 1
SEQ = 256
DEPTH = 1

GRID_W = 64
CTX_LEN = 256
MIX_WIDTH = D_MODEL
DA_HEADS = 8
DA_QK_DIM = 64
DA_V_DIM = 2 * DA_QK_DIM
DA_WIDTH = DA_HEADS * DA_V_DIM
NA_HEADS = 8
NA_HEAD_DIM = 128
NA_WIDTH = NA_HEADS * NA_HEAD_DIM
NA_WIN_ROWS = 8
NA_WIN_COLS = 16
Q_BLOCK = 128
ROPE_BASE = 10000.0
NORM_EPS = 1e-6
SUBLN_EPS = 1e-5
IN_COLS = 4 * DA_WIDTH + 4 * NA_WIDTH
NA_OFF = 4 * DA_WIDTH


def rmsnorm(x, g, eps=NORM_EPS):
    xf = x.astype(jnp.float32)
    y = xf * lax.rsqrt(jnp.mean(xf * xf, axis=-1, keepdims=True) + eps)
    return (y * g.astype(jnp.float32)).astype(x.dtype)

def rope_1d(x, pos):
    half = x.shape[-1] // 2
    inv_freq = ROPE_BASE ** (-jnp.arange(half, dtype=jnp.float32) / half)
    ang = pos.astype(jnp.float32)[:, None] * inv_freq[None, :]
    cos = jnp.cos(ang).astype(x.dtype)
    sin = jnp.sin(ang).astype(x.dtype)
    x1, x2 = x[..., :half], x[..., half:]
    return jnp.concatenate([x1 * cos - x2 * sin, x2 * cos + x1 * sin], axis=-1)

def axial_rope(x, row_pos, col_pos):
    a = x.shape[-1] // 2
    return jnp.concatenate([rope_1d(x[..., :a], row_pos), rope_1d(x[..., a:], col_pos)], axis=-1)

def diff_attention(q, k, v, k_ctx, v_ctx, row_pos, col_pos, lam, subln_g, lambda_init):
    B, S, _ = q.shape
    n_ctx = k_ctx.shape[1]
    split_qk = lambda t, n: t.reshape(B, n, DA_HEADS, 2, DA_QK_DIM).transpose(0, 2, 3, 1, 4)
    split_v = lambda t, n: t.reshape(B, n, DA_HEADS, DA_V_DIM).transpose(0, 2, 1, 3)
    qh = axial_rope(split_qk(q, S), row_pos, col_pos) * (DA_QK_DIM ** -0.5)
    kh = axial_rope(split_qk(k, S), row_pos, col_pos)
    k_all = jnp.concatenate([kh, split_qk(k_ctx, n_ctx)], axis=3)
    v_all = jnp.concatenate([split_v(v, S), split_v(v_ctx, n_ctx)], axis=2)
    nb = S // Q_BLOCK
    q_blocks = jnp.moveaxis(qh.reshape(B, DA_HEADS, 2, nb, Q_BLOCK, DA_QK_DIM), 3, 0)

    def block(qb):
        s = jnp.einsum('bhiqd,bhikd->bhiqk', qb, k_all).astype(jnp.float32)
        p = jax.nn.softmax(s, axis=-1)
        attn = p[:, :, 0] - lam * p[:, :, 1]
        return jnp.einsum('bhqk,bhkd->bhqd', attn.astype(v_all.dtype), v_all)

    out = lax.map(block, q_blocks)
    out = out.transpose(1, 0, 3, 2, 4).reshape(B, S, DA_HEADS, DA_V_DIM)
    out = rmsnorm(out, subln_g, SUBLN_EPS) * (1.0 - lambda_init)
    return out.reshape(B, S, DA_WIDTH)

def neighbourhood_attention(q, k, v, k_ctx, v_ctx, rpb_l, rows):
    B, S, _ = q.shape
    n_ctx = k_ctx.shape[1]
    kr = min(NA_WIN_ROWS, rows)
    kc = min(NA_WIN_COLS, GRID_W)
    grid = lambda t: t.reshape(B, rows, GRID_W, NA_HEADS, NA_HEAD_DIM).transpose(0, 3, 1, 2, 4)
    qg = grid(q) * (NA_HEAD_DIM ** -0.5)
    kg = grid(k)
    vg = grid(v)
    kcx = k_ctx.reshape(B, n_ctx, NA_HEADS, NA_HEAD_DIM).transpose(0, 2, 1, 3)
    vcx = v_ctx.reshape(B, n_ctx, NA_HEADS, NA_HEAD_DIM).transpose(0, 2, 1, 3)
    j = np.arange(GRID_W)
    c0 = np.clip(j - kc // 2, 0, GRID_W - kc)
    col_idx_np = c0[:, None] + np.arange(kc)[None, :]
    col_off_np = col_idx_np - j[:, None] + (NA_WIN_COLS - 1)
    col_idx = jnp.asarray(col_idx_np, dtype=jnp.int32)
    bias_cols = rpb_l[:, :, jnp.asarray(col_off_np, dtype=jnp.int32)]
    n_win = kr * kc

    def row_block(args):
        r, q_row = args
        r0 = jnp.clip(r - kr // 2, 0, rows - kr)
        k_band = lax.dynamic_slice_in_dim(kg, r0, kr, axis=2)
        v_band = lax.dynamic_slice_in_dim(vg, r0, kr, axis=2)
        k_win = k_band[:, :, :, col_idx]
        v_win = v_band[:, :, :, col_idx]
        row_off = r0 + jnp.arange(kr, dtype=jnp.int32) - r + (NA_WIN_ROWS - 1)
        bias = jnp.transpose(bias_cols[:, row_off], (0, 2, 1, 3))
        s_win = jnp.einsum('bhqd,bhrqcd->bhqrc', q_row, k_win).astype(jnp.float32) + bias.astype(jnp.float32)
        s_ctx = jnp.einsum('bhqd,bhcd->bhqc', q_row, kcx).astype(jnp.float32)
        s = jnp.concatenate([s_win.reshape(B, NA_HEADS, GRID_W, n_win), s_ctx], axis=-1)
        p = jax.nn.softmax(s, axis=-1).astype(v.dtype)
        p_win = p[..., :n_win].reshape(B, NA_HEADS, GRID_W, kr, kc)
        return (jnp.einsum('bhqrc,bhrqcd->bhqd', p_win, v_win)
                + jnp.einsum('bhqc,bhcd->bhqd', p[..., n_win:], vcx))

    out = lax.map(row_block, (jnp.arange(rows, dtype=jnp.int32), jnp.moveaxis(qg, 2, 0)))
    return out.transpose(1, 0, 3, 2, 4).reshape(B, S, NA_WIDTH)

def first_inputs(seed: int = 0) -> dict:
    key = jax.random.key(seed)
    ks = jax.random.split(key, 16)
    f32 = jnp.float32
    nrm = lambda k, shape, s: jax.random.normal(k, shape, f32) * s
    return {
        "x": nrm(ks[0], (BATCH, SEQ, D_MODEL), 1.0),
        "c": nrm(ks[1], (BATCH, D_MODEL), 1.0),
        "ctx": nrm(ks[2], (BATCH, CTX_LEN, D_MODEL), 1.0),
        "c_ctx": nrm(ks[3], (D_MODEL,), 1.0),
        "norm_g": 1.0 + nrm(ks[4], (DEPTH, D_MODEL), 0.02),
        "w_mod": nrm(ks[5], (DEPTH, D_MODEL, 3 * D_MODEL), 0.5 * D_MODEL ** -0.5),
        "b_mod": nrm(ks[6], (DEPTH, 3 * D_MODEL), 0.02),
        "w_in": nrm(ks[7], (DEPTH, D_MODEL, IN_COLS), D_MODEL ** -0.5),
        "w_out": nrm(ks[8], (DEPTH, MIX_WIDTH, D_MODEL), MIX_WIDTH ** -0.5),
        "lam_q1": nrm(ks[9], (DEPTH, DA_QK_DIM), 0.1),
        "lam_k1": nrm(ks[10], (DEPTH, DA_QK_DIM), 0.1),
        "lam_q2": nrm(ks[11], (DEPTH, DA_QK_DIM), 0.1),
        "lam_k2": nrm(ks[12], (DEPTH, DA_QK_DIM), 0.1),
        "subln_g": 1.0 + nrm(ks[13], (DEPTH, DA_V_DIM), 0.02),
        "rpb": nrm(ks[14], (DEPTH, NA_HEADS, 2 * NA_WIN_ROWS - 1, 2 * NA_WIN_COLS - 1), 0.1),
        "final_g": 1.0 + nrm(ks[15], (D_MODEL,), 0.02),
    }

def first_block(x, c, ctx, c_ctx, norm_g, w_mod, b_mod, w_in, w_out, lam_q1, lam_k1, lam_q2, lam_k2, subln_g, rpb, final_g):
    B, S, _ = x.shape
    rows = S // GRID_W
    t = jnp.arange(S, dtype=jnp.int32)
    row_pos = t // GRID_W
    col_pos = t % GRID_W
    h = x
    for layer in range(DEPTH):
        lambda_init = 0.8 - 0.6 * math.exp(-0.3 * layer)
        wm, bm, wi = w_mod[layer], b_mod[layer], w_in[layer]
        shift, scale, gate = jnp.split(jax.nn.silu(c) @ wm + bm, 3, axis=-1)
        shift_c, scale_c = jnp.split(jax.nn.silu(c_ctx) @ wm[:, :2 * D_MODEL] + bm[:2 * D_MODEL], 2, axis=-1)
        hx = rmsnorm(h, norm_g[layer]) * (1.0 + scale[:, None]) + shift[:, None]
        hc = rmsnorm(ctx, norm_g[layer]) * (1.0 + scale_c) + shift_c
        proj = hx @ wi
        qa, ka, va, ga, qb, kb, vb, gb = jnp.split(proj, 8, axis=-1)
        ka_c, va_c = jnp.split(hc @ wi[:, DA_WIDTH:3 * DA_WIDTH], 2, axis=-1)
        kb_c, vb_c = jnp.split(hc @ wi[:, NA_OFF + NA_WIDTH:NA_OFF + 3 * NA_WIDTH], 2, axis=-1)
        lq1, lk1 = lam_q1[layer].astype(jnp.float32), lam_k1[layer].astype(jnp.float32)
        lq2, lk2 = lam_q2[layer].astype(jnp.float32), lam_k2[layer].astype(jnp.float32)
        lam = jnp.exp(jnp.sum(lq1 * lk1)) - jnp.exp(jnp.sum(lq2 * lk2)) + lambda_init
        oa = diff_attention(qa, ka, va, ka_c, va_c, row_pos, col_pos, lam, subln_g[layer], lambda_init)
        oa = oa * jax.nn.silu(ga)
        ob = neighbourhood_attention(qb, kb, vb, kb_c, vb_c, rpb[layer], rows) * jax.nn.silu(gb)
        mixed = jnp.concatenate([oa, ob], axis=-1) @ w_out[layer]
        h = h + gate[:, None] * mixed
    return rmsnorm(h, final_g)


CHUNK = 64
D_MIX = D_MODEL
D_CONV = D_MIX // 2
D_MLSTM = D_MIX - D_CONV
CONV_K = 3
M_HEADS = 8
M_HEAD_DIM = D_MLSTM // M_HEADS
D_IN = 3 * D_CONV + 4 * D_MLSTM + 2 * M_HEADS
PEER_HEADS = 8
N_KEYS = 128
N_EXPERTS = N_KEYS * N_KEYS
PEER_TOPK = 16
PEER_QDIM = 256
PEER_HALF = PEER_QDIM // 2
PEER_BLOCK = 128
ALPHA = (2 * DEPTH) ** 0.25
BETA = (8 * DEPTH) ** -0.25
LN_EPS = 1e-5


def layernorm(x, g, b):
    xf = x.astype(jnp.float32)
    mu = jnp.mean(xf, axis=-1, keepdims=True)
    xc = xf - mu
    var = jnp.mean(xc * xc, axis=-1, keepdims=True)
    y = xc * lax.rsqrt(var + LN_EPS) * g.astype(jnp.float32) + b.astype(jnp.float32)
    return y.astype(x.dtype)

def causal_dwconv(z, w, b):
    S = z.shape[1]
    zp = jnp.pad(z, ((0, 0), (CONV_K - 1, 0), (0, 0)))
    y = b
    for j in range(CONV_K):
        y = y + w[j] * zp[:, j:j + S]
    return y

def mlstm_chunkwise(q, k, v, logi, logf):
    Bn, S, H, dh = q.shape
    L = CHUNK
    NC = S // L
    f32 = jnp.float32
    def to_chunks(t):
        return t.astype(f32).reshape(Bn, NC, L, H, dh).transpose(1, 0, 3, 2, 4)
    qc = to_chunks(q)
    kc = to_chunks(k) * (dh ** -0.5)
    vc = to_chunks(v)
    li = logi.astype(f32).reshape(Bn, NC, L, H).transpose(1, 0, 3, 2)
    lf = logf.astype(f32).reshape(Bn, NC, L, H).transpose(1, 0, 3, 2)
    mask = jnp.tril(jnp.ones((L, L), dtype=bool))

    def step(carry, inp):
        C, n, m = carry
        qb, kb, vb, lib, lfb = inp
        bcum = jnp.cumsum(lfb, axis=-1)
        Dm = bcum[..., :, None] - bcum[..., None, :] + lib[..., None, :]
        Dm = jnp.where(mask, Dm, -jnp.inf)
        inter = bcum + m[..., None]
        m_t = jnp.maximum(inter, jnp.max(Dm, axis=-1))
        w_intra = jnp.exp(Dm - m_t[..., None])
        w_inter = jnp.exp(inter - m_t)
        s = jnp.einsum('bhld,bhjd->bhlj', qb, kb) * w_intra
        num = (jnp.einsum('bhlj,bhjd->bhld', s, vb)
               + w_inter[..., None] * jnp.einsum('bhed,bhld->bhle', C, qb))
        den = jnp.sum(s, axis=-1) + w_inter * jnp.einsum('bhd,bhld->bhl', n, qb)
        h = num / jnp.maximum(jnp.abs(den), jnp.exp(-m_t))[..., None]
        bL = bcum[..., -1]
        g = bL[..., None] - bcum + lib
        m_new = jnp.maximum(bL + m, jnp.max(g, axis=-1))
        wk = jnp.exp(g - m_new[..., None])
        decay = jnp.exp(bL + m - m_new)
        C_new = decay[..., None, None] * C + jnp.einsum('bhl,bhle,bhld->bhed', wk, vb, kb)
        n_new = decay[..., None] * n + jnp.einsum('bhl,bhld->bhd', wk, kb)
        return (C_new, n_new, m_new), h

    init = (jnp.zeros((Bn, H, dh, dh), f32), jnp.zeros((Bn, H, dh), f32),
            jnp.zeros((Bn, H), f32))
    _, hs = lax.scan(step, init, (qc, kc, vc, li, lf))
    return hs.transpose(1, 0, 3, 2, 4).reshape(Bn, S, H, dh).astype(q.dtype)

def peer_ffn(h, wq, keys, u, v):
    Bn, S, D = h.shape
    xb = h.reshape(-1, PEER_BLOCK, D)

    def block(xt):
        q = (xt @ wq).reshape(-1, PEER_HEADS, 2, PEER_HALF)
        s = jnp.einsum('thpc,hpnc->thpn', q, keys)
        sv, si = lax.top_k(s, PEER_TOPK)
        cand = (sv[:, :, 0, :, None] + sv[:, :, 1, None, :]).reshape(-1, PEER_HEADS, PEER_TOPK * PEER_TOPK)
        cid = (si[:, :, 0, :, None] * N_KEYS + si[:, :, 1, None, :]).reshape(-1, PEER_HEADS, PEER_TOPK * PEER_TOPK)
        top_s, top_j = lax.top_k(cand, PEER_TOPK)
        eid = jnp.take_along_axis(cid, top_j, axis=-1)
        gate = jax.nn.softmax(top_s.astype(jnp.float32), axis=-1)
        ue = jnp.take(u, eid, axis=0)
        act = jax.nn.gelu(jnp.einsum('thkd,td->thk', ue, xt).astype(jnp.float32), approximate=False)
        ve = jnp.take(v, eid, axis=0)
        return jnp.einsum('thk,thkd->td', (gate * act).astype(xt.dtype), ve)

    return lax.map(block, xb).reshape(Bn, S, D)

def second_inputs(seed: int = 0) -> dict:
    key = jax.random.key(seed)
    ks = jax.random.split(key, 20)
    f32 = jnp.float32
    nrm = lambda k, shape: jax.random.normal(k, shape, f32)
    x = nrm(ks[0], (BATCH, SEQ, D_MODEL))
    ln_in_g = 1.0 + 0.05 * nrm(ks[1], (D_MODEL,))
    ln_in_b = 0.01 * nrm(ks[2], (D_MODEL,))
    col_scale = jnp.concatenate([
        jnp.ones((2 * D_CONV,), f32), jnp.full((D_CONV,), BETA, f32),
        jnp.ones((2 * D_MLSTM,), f32), jnp.full((D_MLSTM,), BETA, f32),
        jnp.ones((D_MLSTM + 2 * M_HEADS,), f32)])
    w_in = nrm(ks[3], (DEPTH, D_MODEL, D_IN)) * (D_MODEL ** -0.5) * col_scale
    b_i = 0.1 * nrm(ks[4], (DEPTH, M_HEADS))
    b_f = jnp.linspace(3.0, 6.0, M_HEADS, dtype=f32) + 0.1 * nrm(ks[5], (DEPTH, M_HEADS))
    b_gate = jnp.concatenate([b_i, b_f], axis=-1)
    conv_w = nrm(ks[6], (DEPTH, CONV_K, D_CONV)) * (CONV_K ** -0.5)
    conv_b = 0.01 * nrm(ks[7], (DEPTH, D_CONV))
    mh_norm_g = 1.0 + 0.05 * nrm(ks[8], (DEPTH, D_MLSTM))
    w_out = nrm(ks[9], (DEPTH, D_MIX, D_MODEL)) * (D_MIX ** -0.5) * BETA
    ln1_g = 1.0 + 0.05 * nrm(ks[10], (DEPTH, D_MODEL))
    ln1_b = 0.01 * nrm(ks[11], (DEPTH, D_MODEL))
    peer_wq = nrm(ks[12], (DEPTH, D_MODEL, PEER_HEADS * PEER_QDIM)) * (D_MODEL ** -0.5)
    peer_keys = nrm(ks[13], (DEPTH, PEER_HEADS, 2, N_KEYS, PEER_HALF)) * (PEER_HALF ** -0.5)
    peer_u = nrm(ks[14], (DEPTH, N_EXPERTS, D_MODEL)) * (D_MODEL ** -0.5) * BETA
    peer_v = nrm(ks[15], (DEPTH, N_EXPERTS, D_MODEL)) * (PEER_HEADS ** -0.5) * BETA
    ln2_g = 1.0 + 0.05 * nrm(ks[16], (DEPTH, D_MODEL))
    ln2_b = 0.01 * nrm(ks[17], (DEPTH, D_MODEL))
    return {"x": x, "ln_in_g": ln_in_g, "ln_in_b": ln_in_b, "w_in": w_in, "b_gate": b_gate,
            "conv_w": conv_w, "conv_b": conv_b, "mh_norm_g": mh_norm_g, "w_out": w_out,
            "ln1_g": ln1_g, "ln1_b": ln1_b, "peer_wq": peer_wq, "peer_keys": peer_keys,
            "peer_u": peer_u, "peer_v": peer_v, "ln2_g": ln2_g, "ln2_b": ln2_b}

def second_block(x, ln_in_g, ln_in_b, w_in, b_gate, conv_w, conv_b, mh_norm_g, w_out,
              ln1_g, ln1_b, peer_wq, peer_keys, peer_u, peer_v, ln2_g, ln2_b):
    Bn, S, D = x.shape
    split_at = np.cumsum([D_CONV, D_CONV, D_CONV, D_MLSTM, D_MLSTM, D_MLSTM, D_MLSTM, M_HEADS]).tolist()
    h = layernorm(x, ln_in_g, ln_in_b)
    for l in range(DEPTH):
        proj = h @ w_in[l]
        cB, cC, ch, q, k, v, o, gi, gf = jnp.split(proj, split_at, axis=-1)
        y_conv = cB * causal_dwconv(cC * ch, conv_w[l], conv_b[l])
        gates = (jnp.concatenate([gi, gf], axis=-1) + b_gate[l]).astype(jnp.float32)
        logi = gates[..., :M_HEADS]
        logf = jax.nn.log_sigmoid(gates[..., M_HEADS:])
        hd = lambda t: t.reshape(Bn, S, M_HEADS, M_HEAD_DIM)
        hm = mlstm_chunkwise(hd(q), hd(k), hd(v), logi, logf)
        hm = layernorm(hm, mh_norm_g[l].reshape(M_HEADS, M_HEAD_DIM),
                       jnp.zeros((M_HEADS, M_HEAD_DIM), hm.dtype))
        y_m = jax.nn.sigmoid(o) * hm.reshape(Bn, S, D_MLSTM)
        mix = jnp.concatenate([y_conv, y_m], axis=-1) @ w_out[l]
        h = layernorm(ALPHA * h + mix, ln1_g[l], ln1_b[l])
        ff = peer_ffn(h, peer_wq[l], peer_keys[l], peer_u[l], peer_v[l])
        h = layernorm(ALPHA * h + ff, ln2_g[l], ln2_b[l])
    return h


def setup_inputs(seed=0):
    out = dict(first_inputs(seed))
    for name, value in second_inputs(seed + 1).items():
        if name != "x":
            out[name + "_2"] = value
    return out


def reference(
    x, c, ctx, c_ctx, norm_g, w_mod, b_mod, w_in, w_out, lam_q1, lam_k1, lam_q2, lam_k2,
    subln_g, rpb, final_g, ln_in_g_2, ln_in_b_2, w_in_2, b_gate_2, conv_w_2, conv_b_2,
    mh_norm_g_2, w_out_2, ln1_g_2, ln1_b_2, peer_wq_2, peer_keys_2, peer_u_2, peer_v_2, ln2_g_2,
    ln2_b_2,
):
    x = first_block(
        x, c, ctx, c_ctx, norm_g, w_mod, b_mod, w_in, w_out, lam_q1, lam_k1, lam_q2, lam_k2,
        subln_g, rpb, final_g,
    )
    return second_block(
        x, ln_in_g_2, ln_in_b_2, w_in_2, b_gate_2, conv_w_2, conv_b_2, mh_norm_g_2, w_out_2,
        ln1_g_2, ln1_b_2, peer_wq_2, peer_keys_2, peer_u_2, peer_v_2, ln2_g_2, ln2_b_2,
    )


_drawn_inputs = setup_inputs


def setup_inputs(seed=0):
    import zlib

    import numpy as np

    out = dict(_drawn_inputs(seed))
    spreads = {}
    factors = {'norm_g': 8.0,
     'b_mod': 3.572,
     'lam_q1': 8.0,
     'lam_k1': 8.0,
     'lam_q2': 3.851,
     'lam_k2': 8.0,
     'subln_g': 8.0,
     'rpb': 8.0,
     'ln_in_b_2': 4.67,
     'conv_b_2': 8.0,
     'mh_norm_g_2': 5.159,
     'ln1_b_2': 5.065,
     'ln2_b_2': 5.616}
    for name, (base, spread) in spreads.items():
        noise = np.random.default_rng([zlib.crc32(name.encode()), seed]).standard_normal(out[name].shape)
        drawn = base * np.exp(spread * noise) if base else spread * noise
        out[name] = __import__('jax').numpy.asarray(drawn.astype(out[name].dtype))
    for name, factor in factors.items():
        out[name] = (out[name] * factor).astype(out[name].dtype)
    return out
```

```python
import concourse.bass as bass
from concourse import mybir
from contextlib import ExitStack, contextmanager

T = 256
D = 2048
P = 128
KT = D // P
TT = T // P
WA = 1024
HEADS = 8
SLAB = 1024
LAMBDA_INIT = 0.2
MASKED = -1e30
ALPHA = 2 ** 0.25
N_KEYS = 128
TOPK = 16

N_MOD, N_WIN_A, N_WIN_B, N_OUT, N_WIN2, N_OUT2, N_WQ, N_U, N_V = 96, 64, 64, 32, 112, 32, 32, 256, 256
NRAW = 4

C_IDENT, C_ONES, C_TRI, C_IOTA = 0, 128, 256, 384
C_PERM, C_COS, C_SIN, C_NAMASK, C_EYE8 = 512, 640, 896, 1152, 1216
C_KEEP, C_ALL = 512, 1224
H_OFFSET = 212960


@contextmanager
def loop(eng, count, step=1):
    with eng.Fori(0, count // step) as i:
        yield i * step if step > 1 else i


def peer_block_kernel(nc, io):
    F, R = mybir.dt.float32, mybir.dt.float32r
    U32 = mybir.dt.uint32
    ALU = mybir.AluOpType
    ACT = mybir.ActivationFunctionType
    X = mybir.AxisListType.X
    ds = bass.ds
    ctx = ExitStack()

    def lasting_sem(name):
        return ctx.enter_context(nc.semaphore(name))

    used, to_clear = [], []

    def sem(name):
        used.append(nc.alloc_semaphore(name=name))
        return used[-1]

    def clear_last_stage(pool):
        for s in to_clear:
            pool.sem_clear(s)

    @contextmanager
    def stage():
        with nc.Block() as block:
            yield block
        for s in to_clear:
            nc.release_semaphore(s)
        to_clear[:] = used
        used.clear()

    with ctx:
        def keep(name, shape, dt=F):
            return ctx.enter_context(nc.sbuf_tensor(name, shape, dt))

        raw = keep("raw", [P, NRAW, SLAB])
        w_hi = [keep(f"w_hi{i}", [P, SLAB], R) for i in range(2)]
        w_lo = [keep(f"w_lo{i}", [P, SLAB], R) for i in range(2)]
        raw_ready = [lasting_sem(f"raw_ready{i}") for i in range(NRAW)]
        mod_used = lasting_sem("mod_used")
        hi_ready = lasting_sem("hi_ready")
        lo_ready = lasting_sem("lo_ready")
        multiplied = lasting_sem("multiplied")

        passed = lasting_sem("passed")

        def raw_wait(eng, slab):
            reg, off = slab
            if reg is None:
                eng.wait_ge(raw_ready[off % NRAW], 16 * (off // NRAW + 1))
            else:
                eng.wait_ge(raw_ready[off % NRAW], reg * 4 + 16 * (off // NRAW + 1))

        def load_slabs(sp, src, base, first, last):
            def one(reg, off):
                n = base + off if reg is None else reg + (base + off)
                src_at = off if reg is None else reg + off
                if base + off >= N_MOD + NRAW:
                    sp.wait_ge(lo_ready, n - (N_MOD + NRAW - 1))
                elif base + off >= NRAW:
                    sp.wait_ge(mod_used, n - (NRAW - 1))
                sp.dma_start(raw[:, off % NRAW, :], src(src_at)).then_inc(raw_ready[off % NRAW], 16)
            if last - first <= NRAW:
                for off in range(first, last):
                    one(None, off)
                return
            with loop(sp, last - first, NRAW) as i:
                for s in range(NRAW):
                    one(i, first + s)

        def round_slab(act, reg, m):
            raw_wait(act, (reg, N_MOD + m))
            act.wait_ge(multiplied, m + 1 if reg is None else reg + (m + 1))
            act.activation(w_hi[m % 2][:, :], raw[:, m % NRAW, :], ACT.Copy).then_inc(hi_ready, 1)

        def split_slab(dve, reg, m):
            dve.wait_ge(hi_ready, m + 1 if reg is None else reg + (m + 1))
            dve.tensor_tensor(w_lo[m % 2][:, :], raw[:, m % NRAW, :], w_hi[m % 2][:, :].bitcast(F),
                              ALU.subtract).then_inc(lo_ready, 1)

        def carry(eng):
            eng.sem_inc(passed, 1)

        def mm3(pe, out, lhs, rhs, start, stop):
            pe.matmul(out, lhs[0], rhs[0], start=start, stop=False)
            pe.matmul(out, lhs[0], rhs[1], start=False, stop=False)
            return pe.matmul(out, lhs[1], rhs[0], start=False, stop=stop)

        def feature_slab(pe, out, reg, m, half, x_hi, x_lo, cols):
            pe.wait_ge(lo_ready, m + 1 if reg is None else reg + (m + 1))
            for k in range(8):
                c = slice(k * P, (k + 1) * P)
                kk = 8 * half + k
                last = mm3(pe, out, (w_hi[m % 2][:, c], w_lo[m % 2][:, c]),
                           (x_hi[:, kk, cols], x_lo[:, kk, cols]), kk == 0, kk == KT - 1)
            last.then_inc(multiplied, 1)

        def token_slab(pe, outs, reg, m, g, x_hi, x_lo):
            pe.wait_ge(lo_ready, m + 1 if reg is None else reg + (m + 1))
            for k in range(2):
                c = slice(k * 512, (k + 1) * 512)
                kk = 2 * g + k
                for t, out in enumerate(outs):
                    tok = slice(t * P, (t + 1) * P)
                    last = mm3(pe, out, (x_hi[:, kk, tok], x_lo[:, kk, tok]),
                               (w_hi[m % 2][:, c], w_lo[m % 2][:, c]), kk == 0, kk == KT - 1)
            last.then_inc(multiplied, 1)

        PS = ctx.enter_context(nc.psum_tensor("PS", [P, 8, 512], F))
        cst = keep("cst", [P, C_KEEP])
        ident = cst[:, C_IDENT:C_IDENT + P]
        h_dram = nc.dram_tensor("h_dram", (P, TT, D), F, kind="Internal").ap()
        x_tok = io["x"].rearrange("(t p) d -> p t d", p=P)
        small = lasting_sem("small")

        def small_load(eng, dst, src):
            eng.dma_start(dst, src).then_inc(small, 16)

        def bcast(row):
            return bass.AP(row.tensor, row.offset, [[0, P], [1, row.shape[-1]]])

        chains = {}

        def chain(eng, name):
            if name not in chains:
                chains[name] = [sem(name), 0]

            def step(instruction):
                chains[name][1] += 1
                instruction.then_inc(chains[name][0], 1)
                eng.wait_ge(chains[name][0], chains[name][1])
            return step

        src_mod = lambda n: io["w_mod_s"][n]
        src_a = lambda n: io["w_in_a"][n]
        src_b = lambda n: io["w_in_b"][n]
        src_out = lambda n: io["w_out_s"][n]
        src_in2 = lambda n: io["w_in2_s"][n]
        src_out2 = lambda n: io["w_out2_s"][n]
        src_wq = lambda n: io["wq_s"][n]
        src_u = lambda n: io["u_s"][n]
        v_view = io["v"].rearrange("(i j) (a c) -> (j a) i c", j=N_KEYS, a=2)
        src_v = lambda n: v_view[n]
        base = {}
        at = 0
        for name, n in (("mod", N_MOD), ("a", N_WIN_A), ("b", N_WIN_B), ("out", N_OUT), ("in2", N_WIN2),
                        ("out2", N_OUT2), ("wq", N_WQ), ("u", N_U), ("v", N_V)):
            base[name] = at
            at += n
        split_at = {k: v - N_MOD for k, v in base.items()}

        def transpose_in(pe, src, sem_src, copied, done, banks=(0, 1)):
            for b in range(KT // 2):
                if b >= 2:
                    pe.wait_ge(copied, b - 1)
                for k in range(2):
                    for t in range(TT):
                        if sem_src is not None and b == 0 and k == 0:
                            pe.wait_ge(sem_src[0], sem_src[1][t])
                        last = pe.transpose(PS[:, banks[b % 2], (2 * k + t) * P:(2 * k + t + 1) * P],
                                            src[:, t, (2 * b + k) * P:(2 * b + k + 1) * P], ident)
                last.then_inc(done, 1)

        def transposed_round(act, done, dst_hi, rounded, banks=(0, 1)):
            for b in range(KT // 2):
                act.wait_ge(done, b + 1)
                act.activation(dst_hi[:, 2 * b:2 * b + 2, :], PS[:, banks[b % 2], :], ACT.Copy).then_inc(rounded, 1)

        def transposed_split(dve, dst_hi, dst_lo, rounded, copied, banks=(0, 1)):
            for b in range(KT // 2):
                dve.wait_ge(rounded, b + 1)
                dve.tensor_tensor(dst_lo[:, 2 * b:2 * b + 2, :], PS[:, banks[b % 2], :].rearrange("p (k t) -> p k t", k=2),
                                  dst_hi[:, 2 * b:2 * b + 2, :].bitcast(F), ALU.subtract).then_inc(copied, 1)

        h_buf = nc.alloc_sbuf_tensor_at("h_buf", [P, TT, D], F, offset=H_OFFSET)
        stats = keep("stats", [P, TT, 4, 6])
        mv = keep("mv", [P, TT, 8])

        def norm_stats(dve, step, y, t, asked):
            for c in range(4):
                i = dve.bn_stats(stats[:, t, c, :], y[:, t, c * 512:(c + 1) * 512])
            step(i)
            step(dve.bn_aggr(mv[:, t, 0:2], stats[:, t, :, :]))
            dve.tensor_scalar(mv[:, t, 2:3], mv[:, t, 1:2], 1e-5, None, ALU.add).then_inc(asked, 1)

        def norm_apply(dve, step, y, t, given, given_before, g, b):
            dve.wait_ge(given, given_before + t + 1)
            step(dve.reciprocal(mv[:, t, 4:5], mv[:, t, 3:4]))
            step(dve.tensor_scalar(y[:, t, :], y[:, t, :], mv[:, t, 0:1], mv[:, t, 4:5], ALU.subtract, ALU.mult))
            step(dve.tensor_tensor(y[:, t, :], y[:, t, :], g[:, :], ALU.mult))
            return dve.tensor_tensor(y[:, t, :], y[:, t, :], b[:, :], ALU.add)

        with ExitStack() as first:
            def buf(name, shape, dt=F, where=first):
                return where.enter_context(nc.sbuf_tensor(name, shape, dt))

            csta = buf("csta", [P, C_ALL - C_KEEP])
            perm = csta[:, C_PERM - C_KEEP:C_PERM - C_KEEP + P]
            cos_t = csta[:, C_COS - C_KEEP:C_COS - C_KEEP + T]
            sin_t = csta[:, C_SIN - C_KEEP:C_SIN - C_KEEP + T]
            na_mask = csta[:, C_NAMASK - C_KEEP:C_NAMASK - C_KEEP + 64]
            modT = buf("modT", [P, 96])
            lam = buf("lam", [P, 8])
            o_a = buf("o_a", [P, TT, WA])
            o_b = buf("o_b", [P, TT, WA])
            late = first.enter_context(ExitStack())
            x_hi = buf("x_hi", [P, KT, 2 * T], R, late)
            x_lo = buf("x_lo", [P, KT, 2 * T], R, late)

            with ExitStack() as ph:
                xs = buf("xs", [P, 4, D], F, ph)
                xT = buf("xT", [P, KT, 2 * T], F, ph)
                junk = buf("junk", [P, D], F, ph)
                cin = buf("cin", [P, KT, 2], F, ph)
                cex = buf("cex", [P, KT, 2], F, ph)
                csilu = buf("csilu", [P, KT, 2], F, ph)
                bm = buf("bm", [P, 48 + KT], F, ph)
                lamv = buf("lamv", [P, 4, 64], F, ph)
                lamp = buf("lamp", [P, 2, 64], F, ph)
                ms = buf("ms", [P, 4, 4], F, ph)
                ab = buf("ab", [P, 2, KT], F, ph)
                x_in = [sem(f"x_in{i}") for i in range(4)]
                c_in = sem("c_in")
                exp_c, silu_c, sq, rms_asked, rms_given, normed = (
                    sem(n) for n in ("exp_c", "silu_c", "sq", "rms_asked", "rms_given", "normed"))
                tr, tr_out, mod_out, lam_asked, lam_given, affine, x_round = (
                    sem(n) for n in ("tr", "tr_out", "mod_out", "lam_asked", "lam_given", "affine", "x_round"))
                with stage() as blk:
                    @blk.sync
                    def _(sp):
                        sp.dma_start(cin[:, :, :], io["c_cols"]).then_inc(c_in, 16)
                        load_slabs(sp, src_mod, 0, 0, NRAW)
                        load_slabs(sp, src_mod, 0, NRAW, N_MOD)
                        load_slabs(sp, src_a, base["a"], 0, NRAW)

                    @blk.gpsimd
                    def _(pool):
                        clear_last_stage(pool)
                        small_load(pool, cst[:, :], io["consts"][:, 0:C_KEEP])
                        small_load(pool, csta[:, :], io["consts"][:, C_KEEP:C_ALL])
                        small_load(pool, bm[:, :], io["mod_cols"])
                        small_load(pool, lamv[:, :, :].rearrange("p a b -> p (a b)"), bcast(io["lam_in"]))

                    @blk.scalar
                    def _(act):
                        for t in range(4):
                            act.dma_start(xs[:, t, :], io["x" if t < 2 else "ctx"][(t % 2) * P:(t % 2 + 1) * P, :])\
                               .then_inc(x_in[t], 16)
                        act.wait_ge(c_in, 16)
                        act.activation(cex[:, :, :], cin[:, :, :], ACT.Exp, scale=-1.0).then_inc(exp_c, 1)
                        act.wait_ge(lam_asked, 1)
                        act.activation(lam[:, 2:4], lam[:, 0:2], ACT.Exp).then_inc(lam_given, 1)
                        for t in range(4):
                            act.wait_ge(x_in[t], 16)
                            if t:
                                act.wait_ge(sq, t)
                            act.activation(junk[:, :], xs[:, t, :], ACT.Square, accum_out=ms[:, t, 0:1]).then_inc(sq, 1)
                        for t in range(4):
                            act.wait_ge(rms_asked, t + 1)
                            act.activation(ms[:, t, 2:3], ms[:, t, 1:2], ACT.Sqrt).then_inc(rms_given, 1)
                        for k in range(KT):
                            act.wait_ge(tr, k + 1)
                            act.activation(xT[:, k, :], PS[:, k % 2, :], ACT.Copy).then_inc(tr_out, 1)
                        for q in range(4):
                            act.wait_ge(affine, q + 1)
                            act.activation(x_hi[:, 4 * q:4 * q + 4, :], xT[:, 4 * q:4 * q + 4, :], ACT.Copy)\
                               .then_inc(x_round, 1)
                        round_slab(act, None, 0)

                    @blk.vector
                    def _(dve):
                        step = chain(dve, "dve0")
                        dve.wait_ge(exp_c, 1)
                        step(dve.tensor_scalar(cex[:, :, :], cex[:, :, :], 1.0, None, ALU.add))
                        step(dve.reciprocal(cex[:, :, :], cex[:, :, :]))
                        dve.tensor_tensor(csilu[:, :, :], cin[:, :, :], cex[:, :, :], ALU.mult).then_inc(silu_c, 1)
                        dve.wait_ge(small, 64)
                        step(dve.tensor_tensor(lamp[:, :, :], lamv[:, 0:4:2, :], lamv[:, 1:4:2, :], ALU.mult))
                        dve.tensor_reduce(lam[:, 0:2], lamp[:, :, :], X, ALU.add).then_inc(lam_asked, 1)
                        dve.wait_ge(lam_given, 1)
                        step(dve.tensor_tensor(lam[:, 4:5], lam[:, 3:4], lam[:, 2:3], ALU.subtract))
                        dve.tensor_scalar(lam[:, 7:8], lam[:, 4:5], -LAMBDA_INIT, None, ALU.add)
                        for t in range(4):
                            dve.wait_ge(sq, t + 1)
                            dve.tensor_scalar(ms[:, t, 1:2], ms[:, t, 0:1], 1.0 / D, 1e-6, ALU.mult, ALU.add)\
                               .then_inc(rms_asked, 1)
                        for t in range(4):
                            dve.wait_ge(rms_given, t + 1)
                            step(dve.reciprocal(ms[:, t, 3:4], ms[:, t, 2:3]))
                            dve.tensor_scalar(xs[:, t, :], xs[:, t, :], ms[:, t, 3:4], None, ALU.mult).then_inc(normed, 1)
                        dve.wait_ge(mod_used, N_MOD)
                        mt = modT[:, :].rearrange("p (a w) -> p a w", w=2)
                        for w in range(2):
                            i = dve.tensor_tensor(mt[:, :, w], PS[:, 7, 0:96].rearrange("p (a w) -> p a w", w=2)[:, :, w],
                                                  bm[:, 0:48], ALU.add)
                        step(i)
                        dve.wait_ge(tr_out, KT)
                        for w in range(2):
                            i = dve.scalar_tensor_tensor(ab[:, w, :], mt[:, 16:32, w], 1.0, bm[:, 48:48 + KT],
                                                         ALU.add, ALU.mult)
                        step(i)
                        for k in range(KT):
                            for w in range(2):
                                part = xT[:, k, w * T:(w + 1) * T]
                                i = dve.tensor_scalar(part, part, ab[:, w, k:k + 1], mt[:, k, w:w + 1], ALU.mult, ALU.add)
                            if k % 4 == 3:
                                i.then_inc(affine, 1)
                        for q in range(4):
                            dve.wait_ge(x_round, q + 1)
                            s = slice(4 * q, 4 * q + 4)
                            dve.tensor_tensor(x_lo[:, s, :], xT[:, s, :], x_hi[:, s, :].bitcast(F), ALU.subtract)
                        split_slab(dve, None, 0)

                    @blk.tensor
                    def _(pe):
                        pe.sem_inc(multiplied, 2)
                        pe.wait_ge(silu_c, 1)

                        def mod_tiles(first_tile, last_tile):
                            with loop(pe, last_tile - first_tile, 2) as j:
                                for u in range(2):
                                    for half in range(2):
                                        s = 2 * u + half
                                        pe.wait_ge(raw_ready[s], j * 8 + (8 * first_tile + 16))
                                        for k in range(8):
                                            kk = 8 * half + k
                                            last = pe.matmul(PS[:, 7, ds(j * 2 + 2 * (first_tile + u), 2)],
                                                             raw[:, s, k * P:(k + 1) * P], csilu[:, kk, :],
                                                             start=(kk == 0), stop=(kk == KT - 1))
                                        last.then_inc(mod_used, 1)

                        mod_tiles(0, 8)
                        pe.wait_ge(small, 64)
                        for k in range(KT):
                            if k >= 2:
                                pe.wait_ge(tr_out, k - 1)
                            for t in range(4):
                                if k == 0:
                                    pe.wait_ge(normed, t + 1)
                                last = pe.transpose(PS[:, k % 2, t * P:(t + 1) * P], xs[:, t, k * P:(k + 1) * P], ident)
                            last.then_inc(tr, 1)
                        mod_tiles(8, 48)

            def project(half_name, q_sb, k_sb, v_sb, g_sb, rope, nxt, ph, more_loads):
                n = half_name
                m0 = split_at[n]
                src = src_a if n == "a" else src_b
                acc_free, copied, permuted, perm_free = (sem(f"{x}_{n}") for x in ("acc_free", "copied", "permuted", "perm_free"))
                staged = buf(f"staged_{n}", [P, 2, T], F, ph)
                roped = buf(f"roped_{n}", [P, 2, 2, T], F, ph)
                with stage() as blk:
                    @blk.sync
                    def _(sp):
                        load_slabs(sp, src, base[n], NRAW, N_WIN_A)
                        load_slabs(sp, nxt[0], nxt[1], 0, NRAW)

                    @blk.gpsimd
                    def _(pool):
                        clear_last_stage(pool)
                        more_loads(pool)

                    @blk.scalar
                    def _(act):
                        act.sem_inc(acc_free, 2)
                        for part, dst, width in ((0, q_sb, T), (1, k_sb, 2 * T)):
                            m1 = m0 + 16 * part
                            with loop(act, HEADS, 2) as j:
                                for u in range(2):
                                    round_slab(act, j * 2, m1 + 2 * u + 1)
                                    round_slab(act, j * 2, m1 + 2 * u + 2)
                                    act.wait_ge(multiplied, j * 2 + (2 + m1 + 2 * u + 2))
                                    if not rope:
                                        act.activation(dst[:, j + u, :], PS[:, u, 0:width], ACT.Copy).then_inc(acc_free, 1)
                                        continue
                                    act.wait_ge(perm_free, j + (8 * part + u + 1))
                                    if part:
                                        act.activation(dst[:, j + u, T:2 * T], PS[:, u, T:2 * T], ACT.Copy)
                                    act.activation(staged[:, u, :], PS[:, u, 0:T], ACT.Copy).then_inc(acc_free, 1)
                        for part, dst, nt in ((2, v_sb, 4), (3, g_sb, 2)):
                            for c in range(2):
                                m1 = m0 + 16 * part + 8 * c
                                for g in range(8):
                                    round_slab(act, None, m1 + g + 1)
                                act.wait_ge(multiplied, 2 + m1 + 8)
                                for t in range(nt):
                                    i = act.activation(dst[:, t, c * 512:(c + 1) * 512], PS[:, 4 * ((c + 1) % 2) + t, :], ACT.Copy)
                                i.then_inc(copied, 1)

                    @blk.vector
                    def _(dve):
                        if rope:
                            dve.sem_inc(perm_free, 2)
                        step = chain(dve, f"dve_{n}")
                        rotated = sem(f"rotated_{n}")
                        for part, dst in ((0, q_sb), (1, k_sb)):
                            m1 = m0 + 16 * part
                            with loop(dve, HEADS, 2) as j:
                                for s in range(4):
                                    split_slab(dve, j * 2, m1 + s + 1)
                                for u in range(2 if rope else 0):
                                    dve.wait_ge(permuted, j + (8 * part + u + 1))
                                    dve.tensor_tensor(roped[:, u, 0, :], staged[:, u, :], cos_t, ALU.mult)
                                    dve.tensor_tensor(roped[:, u, 1, :], PS[:, 2 + u, 0:T], sin_t, ALU.mult).then_inc(rotated, 1)
                                    dve.wait_ge(rotated, j + (8 * part + u + 1))
                                    dve.tensor_tensor(dst[:, j + u, 0:T], roped[:, u, 0, :], roped[:, u, 1, :], ALU.add)\
                                       .then_inc(perm_free, 1)
                        for g in range(32):
                            split_slab(dve, None, m0 + 32 + g + 1)

                    @blk.tensor
                    def _(pe):
                        for part, cols in ((0, slice(0, T)), (1, slice(0, 2 * T))):
                            m1 = m0 + 16 * part
                            with loop(pe, HEADS, 2) as j:
                                for u in range(2):
                                    pe.wait_ge(acc_free, j + (8 * part + u + 1))
                                    for half in range(2):
                                        feature_slab(pe, PS[:, u, cols], j * 2, m1 + 2 * u + half, half, x_hi, x_lo, cols)
                                for u in range(2 if rope else 0):
                                    pe.wait_ge(acc_free, j + (8 * part + u + 3))
                                    pe.matmul(PS[:, 2 + u, 0:T], perm, staged[:, u, :], start=True, stop=True)\
                                      .then_inc(permuted, 1)
                        for part, nt in ((2, 4), (3, 2)):
                            for c in range(2):
                                m1 = m0 + 16 * part + 8 * c
                                if part == 2 and c == 1:
                                    pe.wait_ge(acc_free, 18)
                                    if rope:
                                        pe.wait_ge(perm_free, 18)
                                if part == 3:
                                    pe.wait_ge(copied, c + 1)
                                b0 = 4 * ((c + 1) % 2)
                                for g in range(8):
                                    token_slab(pe, [PS[:, b0 + t, :] for t in range(nt)], None, m1 + g, g, x_hi, x_lo)

            def attend_a(q_sb, k_sb, v_sb, ph):
                qs = buf("qs_a", [P, 2, T], F, ph)
                ks = buf("ks_a", [P, 2, 2 * T], F, ph)
                pr = [buf(f"pr_a{i}", [P, 2, 512], F, ph) for i in range(2)]
                at_ = buf("at_a", [P, 2, 512], F, ph)
                atT = buf("atT_a", [P, 2, 512], F, ph)
                sm = buf("sm_a", [P, 2, 12], F, ph)
                names = ("head_in", "s_used", "scores", "mx", "nm", "exps", "recips", "recl", "p1s", "attn", "attnT", "attnT_sb",
                         "pv", "o_out")
                head_in, s_used, scores, mx, nm, exps, recips, recl, p1s, attn, attnT, attnT_sb, pv, o_out = (
                    sem("a_" + x) for x in names)
                with stage() as blk:
                    @blk.gpsimd
                    def _(pool):
                        clear_last_stage(pool)
                        pool.sem_inc(s_used, 4)
                        with loop(pool, HEADS, 2) as h:
                            for w in range(2):
                                pool.wait_ge(s_used, h * 2 + (2 * w + 2))
                                pool.tensor_copy(qs[:, w, :], q_sb[:, h + w, :])
                                pool.tensor_copy(ks[:, w, :], k_sb[:, h + w, :]).then_inc(head_in, 1)

                    @blk.tensor
                    def _(pe):
                        with loop(pe, HEADS, 2) as h:
                            def score(e):
                                w, t = e // 2, e % 2
                                if t == 0:
                                    pe.wait_ge(head_in, h + (w + 1))
                                if e >= 2:
                                    pe.wait_ge(exps, h * 4 + (2 * (e - 2) + 2))
                                for i in range(2):
                                    r = slice(64 * i, 64 * i + 64)
                                    last = pe.matmul(PS[:, 2 * t + i, :], qs[r, w, t * P:(t + 1) * P], ks[r, w, :],
                                                     start=True, stop=True)
                                last.then_inc(scores, 1)

                            def values(e):
                                w, t = e // 2, e % 2
                                pe.wait_ge(attn, h * 2 + (e + 1))
                                for c in range(4):
                                    last = pe.transpose(PS[:, 4 + t, c * P:(c + 1) * P], at_[:, t, c * P:(c + 1) * P], ident)
                                last.then_inc(attnT, 1)
                                pe.wait_ge(attnT_sb, h * 2 + (e + 1))
                                if e >= 2:
                                    pe.wait_ge(o_out, h * 2 + (e - 1))
                                for c in range(4):
                                    last = pe.matmul(PS[:, 6 + t, 0:P], atT[:, t, c * P:(c + 1) * P],
                                                     v_sb[:, c, ds(h * P + w * P, P)], start=(c == 0), stop=(c == 3))
                                last.then_inc(pv, 1)

                            score(0)
                            score(1)
                            values(0)
                            score(2)
                            values(1)
                            score(3)
                            values(2)
                            values(3)
                            pe.wait_ge(o_out, h * 2 + 4)
                            pe.sem_inc(s_used, 4)

                    @blk.vector
                    def _(dve):
                        with loop(dve, HEADS, 2) as h:
                            def maxima(e):
                                t = e % 2
                                dve.wait_ge(scores, h * 2 + (e + 1))
                                dve.tensor_reduce(sm[:, t, 0:2], PS[:, 2 * t:2 * t + 2, :], X, ALU.max).then_inc(mx, 1)
                                dve.wait_ge(mx, h * 2 + (e + 1))
                                dve.tensor_scalar(sm[:, t, 2:4], sm[:, t, 0:2], -0.125, None, ALU.mult).then_inc(nm, 1)

                            def weigh(e):
                                t = e % 2
                                dve.wait_ge(exps, h * 4 + (2 * e + 2))
                                dve.reciprocal(sm[:, t, 6:8], sm[:, t, 4:6]).then_inc(recips, 1)
                                dve.wait_ge(recips, h * 2 + (e + 1))
                                dve.tensor_tensor(sm[:, t, 8:9], sm[:, t, 7:8], lam[:, 7:8], ALU.mult).then_inc(recl, 1)
                                dve.wait_ge(recl, h * 2 + (e + 1))
                                dve.tensor_scalar(pr[t][:, 1, :], pr[t][:, 1, :], sm[:, t, 8:9], None, ALU.mult).then_inc(p1s, 1)
                                dve.wait_ge(p1s, h * 2 + (e + 1))
                                dve.scalar_tensor_tensor(at_[:, t, :], pr[t][:, 0, :], sm[:, t, 6:7], pr[t][:, 1, :],
                                                         ALU.mult, ALU.add).then_inc(attn, 1)
                            maxima(0)
                            maxima(1)
                            weigh(0)
                            maxima(2)
                            weigh(1)
                            maxima(3)
                            weigh(2)
                            weigh(3)

                    @blk.scalar
                    def _(act):
                        act.preload_act_table(ACT.Exp)
                        with loop(act, HEADS, 2) as h:
                            def exponentials(e):
                                t = e % 2
                                act.wait_ge(nm, h * 2 + (e + 1))
                                for i in range(2):
                                    act.activation(pr[t][:, i, :], PS[:, 2 * t + i, :], ACT.Exp, bias=sm[:, t, 2 + i:3 + i],
                                                   scale=0.125, accum_out=sm[:, t, 4 + i:5 + i]).then_inc(exps, 1)

                            def copy_t(e):
                                t = e % 2
                                act.wait_ge(attnT, h * 2 + (e + 1))
                                act.activation(atT[:, t, :], PS[:, 4 + t, :], ACT.Copy).then_inc(attnT_sb, 1)

                            def copy_o(e):
                                w, t = e // 2, e % 2
                                act.wait_ge(pv, h * 2 + (e + 1))
                                act.activation(o_a[:, t, ds(h * P + w * P, P)], PS[:, 6 + t, 0:P], ACT.Copy).then_inc(o_out, 1)
                            exponentials(0)
                            exponentials(1)
                            copy_t(0)
                            copy_o(0)
                            exponentials(2)
                            copy_t(1)
                            copy_o(1)
                            exponentials(3)
                            copy_t(2)
                            copy_o(2)
                            copy_t(3)
                            copy_o(3)

            def attend_b(q_sb, k_sb, v_sb, bias, ph):
                qs = buf("qs_b", [P, 2, T], F, ph)
                sc = buf("sc_b", [P, 2, 512], F, ph)
                at_ = buf("at_b", [P, 2, 512], F, ph)
                atT = buf("atT_b", [P, 2, 512], F, ph)
                sm = buf("sm_b", [P, 2, 4], F, ph)
                names = ("head_in", "s_used", "scores", "biased", "mx", "exps", "recips", "attnT", "attnT_sb", "pv", "o_out",
                         "masked")
                head_in, s_used, scores, biased, mx, exps, recips, attnT, attnT_sb, pv, o_out, masked = (
                    sem("b_" + x) for x in names)
                scale = float(P) ** -0.5
                with stage() as blk:
                    @blk.gpsimd
                    def _(pool):
                        clear_last_stage(pool)
                        pool.sem_inc(s_used, 4)
                        m = na_mask[:, None, :].broadcast_to([P, 4, 64])
                        for t in range(TT):
                            for h in range(HEADS):
                                b = bias[:, t, h, :].rearrange("p (r c) -> p r c", c=64)
                                i = pool.tensor_tensor(b, b, m, ALU.add)
                        i.then_inc(masked, 1)
                        with loop(pool, HEADS, 2) as h:
                            for w in range(2):
                                pool.wait_ge(s_used, h * 2 + (2 * w + 2))
                                pool.tensor_copy(qs[:, w, :], q_sb[:, h + w, :]).then_inc(head_in, 1)

                    @blk.tensor
                    def _(pe):
                        with loop(pe, HEADS, 2) as h:
                            def score(e):
                                w, t = e // 2, e % 2
                                if t == 0:
                                    pe.wait_ge(head_in, h + (w + 1))
                                if e >= 2:
                                    pe.wait_ge(biased, h * 2 + (e - 1))
                                pe.matmul(PS[:, t, :], qs[:, w, t * P:(t + 1) * P], k_sb[:, h + w, :],
                                          start=True, stop=True).then_inc(scores, 1)

                            def values(e):
                                w, t = e // 2, e % 2
                                pe.wait_ge(exps, h * 2 + (e + 1))
                                for c in range(4):
                                    last = pe.transpose(PS[:, 4 + t, c * P:(c + 1) * P], at_[:, t, c * P:(c + 1) * P], ident)
                                last.then_inc(attnT, 1)
                                pe.wait_ge(attnT_sb, h * 2 + (e + 1))
                                if e >= 2:
                                    pe.wait_ge(o_out, h * 2 + (e - 1))
                                for c in range(4):
                                    last = pe.matmul(PS[:, 6 + t, 0:P], atT[:, t, c * P:(c + 1) * P],
                                                     v_sb[:, c, ds(h * P + w * P, P)], start=(c == 0), stop=(c == 3))
                                last.then_inc(pv, 1)
                            score(0)
                            score(1)
                            values(0)
                            score(2)
                            values(1)
                            score(3)
                            values(2)
                            values(3)
                            pe.wait_ge(o_out, h * 2 + 4)
                            pe.sem_inc(s_used, 4)

                    @blk.vector
                    def _(dve):
                        dve.wait_ge(masked, 1)
                        with loop(dve, HEADS, 2) as h:
                            def add_bias(e):
                                w, t = e // 2, e % 2
                                dve.wait_ge(scores, h * 2 + (e + 1))
                                dve.scalar_tensor_tensor(sc[:, t, 0:T], PS[:, t, 0:T], scale, bias[:, t, h + w, :],
                                                         ALU.mult, ALU.add)
                                dve.tensor_scalar(sc[:, t, T:2 * T], PS[:, t, T:2 * T], scale, None, ALU.mult).then_inc(biased, 1)
                                dve.wait_ge(biased, h * 2 + (e + 1))
                                dve.tensor_reduce(sm[:, t, 0:1], sc[:, t, :], X, ALU.max, negate=True).then_inc(mx, 1)

                            def recip(e):
                                t = e % 2
                                dve.wait_ge(exps, h * 2 + (e + 1))
                                dve.reciprocal(sm[:, t, 2:3], sm[:, t, 1:2]).then_inc(recips, 1)
                            add_bias(0)
                            add_bias(1)
                            recip(0)
                            dve.wait_ge(exps, h * 2 + 1)
                            add_bias(2)
                            recip(1)
                            add_bias(3)
                            recip(2)
                            recip(3)

                    @blk.scalar
                    def _(act):
                        act.preload_act_table(ACT.Exp)
                        with loop(act, HEADS, 2) as h:
                            def exponential(e):
                                t = e % 2
                                act.wait_ge(mx, h * 2 + (e + 1))
                                act.activation(at_[:, t, :], sc[:, t, :], ACT.Exp, bias=sm[:, t, 0:1],
                                               accum_out=sm[:, t, 1:2]).then_inc(exps, 1)

                            def copy_t(e):
                                t = e % 2
                                act.wait_ge(attnT, h * 2 + (e + 1))
                                act.activation(atT[:, t, :], PS[:, 4 + t, :], ACT.Copy).then_inc(attnT_sb, 1)

                            def copy_o(e):
                                w, t = e // 2, e % 2
                                act.wait_ge(pv, h * 2 + (e + 1))
                                act.wait_ge(recips, h * 2 + (e + 1))
                                act.activation(o_b[:, t, ds(h * P + w * P, P)], PS[:, 6 + t, 0:P], ACT.Copy,
                                               scale=sm[:, t, 2:3]).then_inc(o_out, 1)
                            exponential(0)
                            exponential(1)
                            copy_t(0)
                            copy_o(0)
                            exponential(2)
                            copy_t(1)
                            copy_o(1)
                            exponential(3)
                            copy_t(2)
                            copy_o(2)
                            copy_t(3)
                            copy_o(3)

            def gate(g_sb, o_sb, norm, ph, n):
                ex = buf(f"ex_{n}", [P, TT, WA], F, ph)
                one, two, ssq, asked, given = (sem(f"{x}_{n}") for x in ("g_exp", "g_silu", "g_ssq", "g_asked", "g_given"))
                if norm:
                    ss = buf("ss", [P, 3, TT * HEADS], F, ph)
                    sub_g = buf("sub_g", [P, P], F, ph)
                    loaded = sem("sub_g_in")
                with stage() as blk:
                    @blk.gpsimd
                    def _(pool):
                        clear_last_stage(pool)
                        if norm:
                            pool.dma_start(sub_g[:, :], bcast(io["subln_g"])).then_inc(loaded, 16)

                    @blk.scalar
                    def _(act):
                        act.activation(ex[:, :, :], g_sb[:, :, :], ACT.Exp, scale=-1.0).then_inc(one, 1)
                        if norm:
                            act.wait_ge(asked, 1)
                            act.activation(ss[:, 2, :], ss[:, 1, :], ACT.Sqrt).then_inc(given, 1)

                    @blk.vector
                    def _(dve):
                        step = chain(dve, f"dve_gate_{n}")
                        if norm:
                            sq = buf("sq_o", [P, TT, WA], F, ph)
                            step(dve.tensor_tensor(sq[:, :, :], o_sb[:, :, :], o_sb[:, :, :], ALU.mult))
                            step(dve.tensor_reduce(ss[:, 0, :], sq[:, :, :].rearrange("p t (h c) -> p (t h) c", c=P), X, ALU.add))
                            dve.tensor_scalar(ss[:, 1, :], ss[:, 0, :], 1.0 / P, 1e-5, ALU.mult, ALU.add).then_inc(asked, 1)
                        dve.wait_ge(one, 1)
                        step(dve.tensor_scalar(ex[:, :, :], ex[:, :, :], 1.0, None, ALU.add))
                        step(dve.reciprocal(ex[:, :, :], ex[:, :, :]))
                        step(dve.tensor_tensor(ex[:, :, :], ex[:, :, :], g_sb[:, :, :], ALU.mult))
                        if norm:
                            dve.wait_ge(given, 1)
                            dve.wait_ge(loaded, 16)
                            step(dve.reciprocal(ss[:, 0, :], ss[:, 2, :]))
                            o3 = o_sb[:, :, :].rearrange("p t (h c) -> p (t h) c", c=P)
                            step(dve.tensor_tensor(o3, o3, ss[:, 0, :, None].broadcast_to([P, TT * HEADS, P]), ALU.mult))
                            step(dve.scalar_tensor_tensor(o3, o3, 1.0 - LAMBDA_INIT,
                                                          sub_g[:, None, :].broadcast_to([P, TT * HEADS, P]), ALU.mult, ALU.mult))
                        dve.tensor_tensor(o_sb[:, :, :], o_sb[:, :, :], ex[:, :, :], ALU.mult)

            for n in ("a", "b"):
                with ExitStack() as ph:
                    q_sb = buf(f"q_{n}", [P, HEADS, T], F, ph)
                    k_sb = buf(f"k_{n}", [P, HEADS, 2 * T], F, ph)
                    v_sb = buf(f"v_{n}", [P, 4, WA], F, ph)
                    g_sb = buf(f"g_{n}", [P, TT, WA], F, ph)
                    bias = None
                    if n == "b":
                        bias = buf("bias", [P, TT, HEADS, T], F, ph)
                        bias_in = sem("bias_in")

                    def more_loads(pool):
                        if n == "b":
                            for t in range(TT):
                                for r2 in range(2):
                                    r = 2 * t + r2
                                    pool.dma_start(bias[64 * r2:64 * r2 + 64, t, :, :],
                                                   io["rpb_e"][:, :, (7 - r) * 64:(11 - r) * 64].rearrange("h j c -> j h c"))\
                                        .then_inc(bias_in, 16)
                            pool.wait_ge(bias_in, 64)
                    nxt = (src_b, base["b"]) if n == "a" else (src_out, base["out"])
                    with ExitStack() as ph2:
                        project(n, q_sb, k_sb, v_sb, g_sb, n == "a", nxt, ph2, more_loads)
                    with ExitStack() as ph2:
                        if n == "a":
                            attend_a(q_sb, k_sb, v_sb, ph2)
                        else:
                            attend_b(q_sb, k_sb, v_sb, bias, ph2)
                    with ExitStack() as ph2:
                        gate(g_sb, o_a if n == "a" else o_b, n == "a", ph2, n)
            late.close()
            with ExitStack() as ph:
                oc_hi = buf("oc_hi", [P, KT, T], R, ph)
                oc_lo = buf("oc_lo", [P, KT, T], R, ph)
                gate_b = buf("gate_b", [P, D], F, ph)
                par = [buf(f"par{i}", [P, D], F, ph) for i in range(3)]
                diag = buf("diag", [P, 2, P], F, ph)
                tmp = buf("tmp1", [P, TT, 512], F, ph)
                junk = buf("junk1", [P, D], F, ph)
                tr, rnd, cp, diag_made, gate_mm, gate_out, xin, gated, resid, squared, asked, given, prod = (
                    sem(x + "_1") for x in ("tr", "rnd", "cp", "diag_made", "gate_mm", "gate_out", "xin", "gated", "resid",
                                            "squared", "asked", "given", "prod"))
                m0 = split_at["out"]
                with stage() as blk:
                    @blk.sync
                    def _(sp):
                        load_slabs(sp, src_out, base["out"], NRAW, N_OUT)
                        load_slabs(sp, src_in2, base["in2"], 0, NRAW)

                    @blk.gpsimd
                    def _(pool):
                        clear_last_stage(pool)
                        pool.dma_start(h_buf[:, :, :], x_tok).then_inc(xin, 16)
                        for i, name in enumerate(("final_g", "ln_in_g", "ln_in_b")):
                            pool.dma_start(par[i][:, :], bcast(io[name])).then_inc(xin, 16)

                    @blk.tensor
                    def _(pe):
                        both = [o_a, o_b]
                        for b in range(KT // 2):
                            if b >= 2:
                                pe.wait_ge(cp, b - 1)
                            for k in range(2):
                                for t in range(TT):
                                    kk = 2 * b + k
                                    src = both[kk // 8][:, t, (kk % 8) * P:(kk % 8 + 1) * P]
                                    last = pe.transpose(PS[:, b % 2, (2 * k + t) * P:(2 * k + t + 1) * P], src, ident)
                            last.then_inc(tr, 1)
                        for b in range(KT):
                            pe.wait_ge(diag_made, b + 1)
                            if b % 4 == 0 and b >= 8:
                                pe.wait_ge(gate_out, b // 4 - 1)
                            pe.matmul(PS[:, 2 + (b // 4) % 2, (b % 4) * P:(b % 4 + 1) * P],
                                      cst[:, C_ONES:C_ONES + P], diag[:, b % 2, :], start=True, stop=True).then_inc(gate_mm, 1)
                        pe.wait_ge(cp, 8)
                        with loop(pe, 4, 2) as c:
                            for u in range(2):
                                pe.wait_ge(gated, c + (u + 1))
                                for g in range(8):
                                    token_slab(pe, [PS[:, 4 + 2 * u + t, :] for t in range(TT)], c * 8, m0 + 8 * u + g, g,
                                               oc_hi, oc_lo)

                    @blk.scalar
                    def _(act):
                        for b in range(KT // 2):
                            act.wait_ge(tr, b + 1)
                            act.activation(oc_hi[:, 2 * b:2 * b + 2, :], PS[:, b % 2, :].rearrange("p (k t) -> p k t", k=2),
                                           ACT.Copy).then_inc(rnd, 1)
                        for q in range(4):
                            act.wait_ge(gate_mm, 4 * q + 4)
                            act.activation(gate_b[:, q * 512:(q + 1) * 512], PS[:, 2 + q % 2, :], ACT.Copy).then_inc(gate_out, 1)
                        with loop(act, N_OUT, NRAW) as i:
                            for s in range(NRAW):
                                round_slab(act, i, m0 + s + 1)
                        for t in range(TT):
                            act.wait_ge(resid, 4)
                            if t:
                                act.wait_ge(squared, t)
                            act.activation(junk[:, :], h_buf[:, t, :], ACT.Square, accum_out=mv[:, t, 5:6]).then_inc(squared, 1)
                        for n in range(2 * TT):
                            t = n % TT
                            act.wait_ge(asked, n + 1)
                            act.activation(mv[:, t, 3:4], mv[:, t, 2:3], ACT.Sqrt).then_inc(given, 1)

                    @blk.vector
                    def _(dve):
                        step = chain(dve, "dve_out1")
                        for b in range(KT // 2):
                            dve.wait_ge(rnd, b + 1)
                            s = slice(2 * b, 2 * b + 2)
                            dve.tensor_tensor(oc_lo[:, s, :], PS[:, b % 2, :].rearrange("p (k t) -> p k t", k=2),
                                              oc_hi[:, s, :].bitcast(F), ALU.subtract).then_inc(cp, 1)
                        mt = modT[:, :].rearrange("p (a w) -> p a w", w=2)
                        for b in range(KT):
                            if b >= 2:
                                dve.wait_ge(gate_mm, b - 1)
                            dve.tensor_scalar(diag[:, b % 2, :], ident, mt[:, 32 + b, 0:1], None, ALU.mult).then_inc(diag_made, 1)
                        dve.sem_inc(gated, 2)
                        dve.wait_ge(gate_out, 4)
                        dve.wait_ge(xin, 64)
                        with loop(dve, 4, 2) as c:
                            for u in range(2):
                                for g in range(8):
                                    split_slab(dve, c * 8, m0 + 8 * u + g + 1)
                                dve.wait_ge(multiplied, c * 8 + (2 + m0 + 8 * u + 8))
                                for t in range(TT):
                                    i = dve.tensor_tensor(tmp[:, t, :], PS[:, 4 + 2 * u + t, :],
                                                          gate_b[:, ds(c * 512 + u * 512, 512)], ALU.mult)
                                i.then_inc(gated, 1)
                                dve.wait_ge(gated, c + (u + 3))
                                for t in range(TT):
                                    hh = h_buf[:, t, ds(c * 512 + u * 512, 512)]
                                    i = dve.tensor_tensor(hh, hh, tmp[:, t, :], ALU.add)
                                i.then_inc(resid, 1)
                                dve.wait_ge(resid, c + (u + 1))
                        for t in range(TT):
                            dve.wait_ge(squared, t + 1)
                            dve.tensor_scalar(mv[:, t, 2:3], mv[:, t, 5:6], 1.0 / D, 1e-6, ALU.mult, ALU.add).then_inc(asked, 1)
                        for t in range(TT):
                            dve.wait_ge(given, t + 1)
                            step(dve.reciprocal(mv[:, t, 4:5], mv[:, t, 3:4]))
                            step(dve.scalar_tensor_tensor(h_buf[:, t, :], h_buf[:, t, :], mv[:, t, 4:5], par[0][:, :],
                                                          ALU.mult, ALU.mult))
                            norm_stats(dve, step, h_buf, t, asked)
                        for t in range(TT):
                            norm_apply(dve, step, h_buf, t, given, TT, par[1], par[2])

        second = ExitStack()
        ctx.enter_context(second)

        def buf2(name, shape, dt=F, where=second):
            return where.enter_context(nc.sbuf_tensor(name, shape, dt))

        mix_hi = buf2("mix_hi", [P, KT, T], R)
        mix_lo = buf2("mix_lo", [P, KT, T], R)
        cell = second.enter_context(ExitStack())
        q2 = buf2("q2", [P, HEADS, T], F, cell)
        k2 = buf2("k2", [P, HEADS, T], F, cell)
        v2 = buf2("v2", [P, TT, HEADS, P + 1], F, cell)
        o2 = buf2("o2", [P, TT, WA], F, cell)
        gates = buf2("gates", [P, TT, 16], F, cell)
        with ExitStack() as ph:
            h_hi = buf2("h_hi", [P, KT, T], R, ph)
            h_lo = buf2("h_lo", [P, KT, T], R, ph)
            wg = buf2("wg", [P, KT, 16], F, ph)
            wg_hi = buf2("wg_hi", [P, KT, 16], R, ph)
            wg_lo = buf2("wg_lo", [P, KT, 16], R, ph)
            bg = buf2("bg", [P, 16], F, ph)
            cv = buf2("cv", [P, 4, HEADS], F, ph)
            c_sb = buf2("c_sb", [P, 2, T], F, ph)
            z = buf2("z", [P, 2, T + 2], F, ph)
            yc = buf2("yc", [P, 2, 2, T], F, ph)
            tr, rnd, cp, par_in, wg_round, wg_split, gates_done, zeroed, c_copied, conv, conv_free, acc_free, vo_free = (
                sem(x + "_2") for x in ("tr", "rnd", "cp", "par_in", "wg_round", "wg_split", "gates_done", "zeroed", "c_copied",
                                        "conv", "conv_free", "acc_free", "vo_free"))
            m0 = split_at["in2"]
            with stage() as blk:
                @blk.sync
                def _(sp):
                    load_slabs(sp, src_in2, base["in2"], NRAW, N_WIN2)
                    load_slabs(sp, src_out2, base["out2"], 0, NRAW)

                @blk.gpsimd
                def _(pool):
                    clear_last_stage(pool)
                    pool.dma_start(cv[:, :, :].rearrange("p a b -> p (a b)"), io["conv_cols"]).then_inc(par_in, 16)
                    pool.dma_start(wg[:, :, :].rearrange("p a b -> p (a b)"), io["w_gate_cols"]).then_inc(par_in, 16)
                    pool.dma_start(bg[:, :], bcast(io["b_gate"])).then_inc(par_in, 16)
                    pool.memset(z[:, :, 0:2], 0.0)
                    pool.memset(v2[:, :, :, P:P + 1], 1.0).then_inc(zeroed, 1)

                @blk.tensor
                def _(pe):
                    transpose_in(pe, h_buf, None, cp, tr, banks=(6, 7))
                    pe.wait_ge(cp, 8)
                    with loop(pe, HEADS, 2) as j:
                        for u in range(2):
                            pe.wait_ge(conv_free, j * 3 + (3 * u + 3))
                            for part in range(3):
                                for half in range(2):
                                    feature_slab(pe, PS[:, 3 * u + part, 0:T], j * 6, m0 + 6 * u + 2 * part + half, half,
                                                 h_hi, h_lo, slice(0, T))
                    with loop(pe, 2 * HEADS, 2) as j:
                        for u in range(2):
                            pe.wait_ge(acc_free, j + (u + 1))
                            for half in range(2):
                                feature_slab(pe, PS[:, 6 + u, 0:T], j * 2, m0 + 48 + 2 * u + half, half, h_hi, h_lo, slice(0, T))
                    pe.wait_ge(acc_free, 2 * HEADS + 1)
                    pe.wait_ge(wg_split, 1)
                    for t in range(TT):
                        tok = slice(t * P, (t + 1) * P)
                        for k in range(KT):
                            last = mm3(pe, PS[:, 6, t * 16:t * 16 + 16], (h_hi[:, k, tok], h_lo[:, k, tok]),
                                       (wg_hi[:, k, :], wg_lo[:, k, :]), k == 0, k == KT - 1)
                    last.then_inc(gates_done, 1)
                    pe.wait_ge(conv_free, 6 + 3 * HEADS)
                    for c in range(4):
                        if c >= 2:
                            pe.wait_ge(vo_free, c - 1)
                        for g in range(8):
                            token_slab(pe, [PS[:, 2 * (c % 2) + t, :] for t in range(TT)], None, m0 + 80 + 8 * c + g, g, h_hi, h_lo)

                @blk.scalar
                def _(act):
                    transposed_round(act, tr, h_hi, rnd, banks=(6, 7))
                    act.sem_inc(acc_free, 2)
                    act.wait_ge(par_in, 48)
                    act.activation(wg_hi[:, :, :], wg[:, :, :], ACT.Copy).then_inc(wg_round, 1)
                    with loop(act, HEADS, 2) as j:
                        for u in range(2):
                            for s in range(6):
                                round_slab(act, j * 6, m0 + 6 * u + s + 1)
                            act.wait_ge(multiplied, j * 6 + (2 + m0 + 6 * u + 4))
                            act.wait_ge(conv_free, j * 3 + (3 * u + 3))
                            act.activation(c_sb[:, u, :], PS[:, 3 * u + 1, 0:T], ACT.Copy).then_inc(c_copied, 1)
                    for part, dst in ((0, q2), (1, k2)):
                        with loop(act, HEADS, 2) as j:
                            for u in range(2):
                                for s in range(2):
                                    round_slab(act, j * 2, m0 + 48 + 16 * part + 2 * u + s + 1)
                                act.wait_ge(multiplied, j * 2 + (2 + m0 + 48 + 16 * part + 2 * u + 2))
                                act.activation(dst[:, j + u, :], PS[:, 6 + u, 0:T], ACT.Copy).then_inc(acc_free, 1)
                    for c in range(4):
                        m1 = m0 + 80 + 8 * c
                        for g in range(8):
                            round_slab(act, None, m1 + g + 1)
                        act.wait_ge(multiplied, 2 + m1 + 8)
                        if c < 2:
                            act.wait_ge(zeroed, 1)
                        for t in range(TT):
                            if c < 2:
                                i = act.activation(v2[:, t, 4 * c:4 * c + 4, 0:P],
                                                   PS[:, 2 * (c % 2) + t, :].rearrange("p (h e) -> p h e", h=4), ACT.Copy)
                            else:
                                i = act.activation(o2[:, t, (c - 2) * 512:(c - 1) * 512], PS[:, 2 * (c % 2) + t, :], ACT.Copy)
                        i.then_inc(vo_free, 1)

                @blk.vector
                def _(dve):
                    step = chain(dve, "dve_in2")
                    transposed_split(dve, h_hi, h_lo, rnd, cp, banks=(6, 7))
                    dve.wait_ge(wg_round, 1)
                    dve.tensor_tensor(wg_lo[:, :, :], wg[:, :, :], wg_hi[:, :, :].bitcast(F), ALU.subtract).then_inc(wg_split, 1)
                    dve.sem_inc(conv_free, 6)
                    dve.wait_ge(zeroed, 1)
                    with loop(dve, HEADS, 2) as j:
                        for u in range(2):
                            for s in range(6):
                                split_slab(dve, j * 6, m0 + 6 * u + s + 1)
                            dve.wait_ge(c_copied, j + (u + 1))
                            dve.wait_ge(multiplied, j * 6 + (2 + m0 + 6 * u + 6))
                            y = yc[:, u, 0, :]

                            def tap(n):
                                return cv[:, n, ds(j + u, 1)]
                            n = 6 * u
                            dve.tensor_tensor(z[:, u, 2:T + 2], c_sb[:, u, :], PS[:, 3 * u + 2, 0:T], ALU.mult).then_inc(conv, 1)
                            dve.wait_ge(conv, j * 6 + (n + 1))
                            dve.tensor_scalar(y, z[:, u, 2:T + 2], tap(2), tap(3), ALU.mult, ALU.add).then_inc(conv, 1)
                            dve.wait_ge(conv, j * 6 + (n + 2))
                            dve.scalar_tensor_tensor(y, z[:, u, 1:T + 1], tap(1), y, ALU.mult, ALU.add).then_inc(conv, 1)
                            dve.wait_ge(conv, j * 6 + (n + 3))
                            dve.scalar_tensor_tensor(y, z[:, u, 0:T], tap(0), y, ALU.mult, ALU.add).then_inc(conv, 1)
                            dve.wait_ge(conv, j * 6 + (n + 4))
                            dve.tensor_tensor(yc[:, u, 1, :], y, PS[:, 3 * u, 0:T], ALU.mult).then_inc(conv, 1)
                            dve.wait_ge(conv, j * 6 + (n + 5))
                            dve.tensor_copy(mix_hi[:, j + u, :], yc[:, u, 1, :]).then_inc(conv, 1)
                            dve.wait_ge(conv, j * 6 + (n + 6))
                            dve.tensor_tensor(mix_lo[:, j + u, :], yc[:, u, 1, :], mix_hi[:, j + u, :].bitcast(F), ALU.subtract)\
                               .then_inc(conv_free, 3)
                    with loop(dve, 32, NRAW) as i:
                        for s in range(NRAW):
                            split_slab(dve, i, m0 + 48 + s + 1)
                    dve.wait_ge(gates_done, 1)
                    for t in range(TT):
                        dve.tensor_tensor(gates[:, t, :], PS[:, 6, t * 16:t * 16 + 16], bg[:, :], ALU.add)
                    with loop(dve, 32, NRAW) as i:
                        for s in range(NRAW):
                            split_slab(dve, i, m0 + 80 + s + 1)

        with ExitStack() as ph:
            lg = buf2("lg", [P, TT, 5, HEADS], F, ph)
            row = buf2("row", [HEADS, 8, T], F, ph)
            neg = buf2("neg", [HEADS, HEADS, T], F, ph)
            colb = buf2("colb", [P, TT, 2, HEADS], F, ph)
            qk = buf2("qk", [P, 2, 2, T], F, ph)
            ee = buf2("ee", [P, 2, 3, P], F, ph)
            ss = buf2("ss2", [P, 2, 3, P], F, ph)
            num = buf2("num", [P, 2, TT, P + 1], F, ph)
            den = buf2("den", [P, 2, 3, TT], F, ph)
            hm = buf2("hm", [P, TT, HEADS, P], F, ph)
            eye8 = buf2("eye8", [HEADS, HEADS], F, ph)
            mh_g = buf2("mh_g", [P, WA], F, ph)
            st = buf2("st", [P, TT, HEADS, 6], F, ph)
            hv = buf2("hv", [P, TT * HEADS, 6], F, ph)
            ex = buf2("ex2", [P, TT, WA], F, ph)
            (g_abs, g_exp, g_ln, g_dve, g_tr, g_rows, g_b, g_em, g_trb, g_col, par_in, head_in, s_used, scores, tri, exps, wts, nums,
             num_sb, dens, hms, o_exp, asked, given, ymr, tr, rnd, cp, neg_made) = (
                sem(x + "_3") for x in ("g_abs", "g_exp", "g_ln", "g_dve", "g_tr", "g_rows", "g_b", "g_em", "g_trb", "g_col",
                                        "par_in", "head_in", "s_used", "scores", "tri", "exps", "wts", "nums", "num_sb", "dens",
                                        "hms", "o_exp", "asked", "given", "ymr", "tr", "rnd", "cp", "neg_made"))
            scale = float(P) ** -0.5
            with stage() as blk:
                @blk.gpsimd
                def _(pool):
                    clear_last_stage(pool)
                    pool.dma_start(eye8[:, :], io["consts"][0:HEADS, C_EYE8:C_EYE8 + HEADS]).then_inc(par_in, 16)
                    pool.dma_start(mh_g[:, :], bcast(io["mh_g"])).then_inc(par_in, 16)
                    pool.sem_inc(s_used, 2)
                    with loop(pool, HEADS, 2) as h:
                        for w in range(2):
                            pool.wait_ge(s_used, h + (w + 1))
                            pool.tensor_copy(qk[:, w, 0, :], q2[:, h + w, :])
                            pool.tensor_copy(qk[:, w, 1, :], k2[:, h + w, :]).then_inc(head_in, 1)

                @blk.scalar
                def _(act):
                    act.preload_act_table_set("natural_log_exp_and_others")
                    act.activation(ex[:, :, :], o2[:, :, :], ACT.Exp, scale=-1.0).then_inc(o_exp, 1)
                    act.wait_ge(g_abs, 1)
                    act.activation(lg[:, :, 2, :], lg[:, :, 1, :], ACT.Exp).then_inc(g_exp, 1)
                    act.wait_ge(g_exp, 1)
                    act.activation(lg[:, :, 3, :], lg[:, :, 2, :], ACT.Ln, bias=cst[:, C_ONES:C_ONES + 1]).then_inc(g_ln, 1)
                    act.wait_ge(g_tr, 1)
                    act.activation(row[:, 0:2, :], PS[0:HEADS, 7, :].rearrange("p (a t) -> p a t", a=2), ACT.Copy).then_inc(g_rows, 1)
                    act.wait_ge(g_b, 1)
                    act.activation(row[:, 6, :], row[:, 6, :], ACT.Exp, scale=-1.0).then_inc(g_em, 1)
                    act.wait_ge(g_trb, 1)
                    act.activation(colb[:, :, :, :].rearrange("p t a h -> p (t a h)"), PS[:, 7, 0:32], ACT.Copy).then_inc(g_col, 1)
                    act.wait_ge(g_col, 1)
                    with loop(act, HEADS, 2) as h:
                        for w in range(2):
                            act.wait_ge(tri, h + (w + 1))
                            a0, a1 = colb[:, 0, 0, ds(h + w, 1)], colb[:, 1, 0, ds(h + w, 1)]
                            act.activation(ee[:, w, 0, :], ee[:, w, 0, :], ACT.Exp, bias=a0)
                            act.activation(ee[:, w, 1, :], PS[:, 2 + w, P:T], ACT.Exp, bias=a0)
                            act.activation(ee[:, w, 2, :], ee[:, w, 2, :], ACT.Exp, bias=a1).then_inc(exps, 1)
                            act.wait_ge(nums, h + (w + 1))
                            act.activation(num[:, w, :, :], PS[:, 4 + w, 0:2 * (P + 1)].rearrange("p (t e) -> p t e", t=2),
                                           ACT.Copy).then_inc(num_sb, 1)
                    act.wait_ge(asked, 1)
                    act.activation(hv[:, :, 3], hv[:, :, 2], ACT.Sqrt).then_inc(given, 1)
                    for b in range(4):
                        act.wait_ge(tr, b + 1)
                        act.activation(mix_hi[:, 8 + 2 * b:10 + 2 * b, :], PS[:, b % 2, :].rearrange("p (k t) -> p k t", k=2),
                                       ACT.Copy).then_inc(rnd, 1)

                @blk.tensor
                def _(pe):
                    pe.wait_ge(g_dve, 1)
                    for a in range(2):
                        for t in range(TT):
                            last = pe.transpose(PS[0:HEADS, 7, a * T + t * P:a * T + (t + 1) * P], lg[:, t, 4 * a, :], ident)
                    last.then_inc(g_tr, 1)
                    pe.wait_ge(g_em, 1)
                    pe.wait_ge(par_in, 32)
                    for t in range(TT):
                        for a, r in ((0, 3), (1, 6)):
                            last = pe.transpose(PS[:, 7, (2 * t + a) * HEADS:(2 * t + a + 1) * HEADS],
                                                row[:, r, t * P:(t + 1) * P], eye8[:, :])
                    last.then_inc(g_trb, 1)
                    pe.wait_ge(g_col, 1)
                    pe.wait_ge(neg_made, 1)

                    def values(h, w):
                        pe.wait_ge(wts, h + (w + 1))
                        if True:
                            pe.wait_ge(s_used, h + (w + 1))
                        v0, v1 = v2[:, 0, h + w, :], v2[:, 1, h + w, :]
                        pe.matmul(PS[:, 4 + w, 0:P + 1], ss[:, w, 0, :], v0, start=True, stop=True)
                        pe.matmul(PS[:, 4 + w, P + 1:2 * P + 2], ss[:, w, 1, :], v0, start=True, stop=False)
                        pe.matmul(PS[:, 4 + w, P + 1:2 * P + 2], ss[:, w, 2, :], v1, start=False, stop=True).then_inc(nums, 1)
                    with loop(pe, HEADS, 2) as h:
                        for w in range(2):
                            pe.wait_ge(head_in, h + (w + 1))
                            q, k = qk[:, w, 0, :], qk[:, w, 1, :]
                            pe.matmul(PS[:, w, 0:T], k[:, 0:P], q, start=True, stop=True)
                            pe.matmul(PS[:, w, T:T + P], k[:, P:T], q[:, P:T], start=True, stop=True)
                            pe.matmul(PS[:, 2 + w, 0:T], cst[0:HEADS, C_ONES:C_ONES + P], neg[:, h + w, :],
                                      start=True, stop=True).then_inc(scores, 1)
                        for w in range(2):
                            values(h, w)
                    for b in range(4):
                        pe.wait_ge(ymr, 1)
                        if b >= 2:
                            pe.wait_ge(cp, b - 1)
                        for k in range(2):
                            for t in range(TT):
                                last = pe.transpose(PS[:, b % 2, (2 * k + t) * P:(2 * k + t + 1) * P],
                                                    hm[:, t, 2 * b + k, :], ident)
                        last.then_inc(tr, 1)

                @blk.vector
                def _(dve):
                    step = chain(dve, "dve_cell")
                    gi, gf = gates[:, :, 0:HEADS], gates[:, :, HEADS:16]
                    step(dve.tensor_scalar(lg[:, :, 1, :], gf, -1.0, None, ALU.mult))
                    step(dve.tensor_tensor(lg[:, :, 1, :], lg[:, :, 1, :], gf, ALU.min))
                    dve.tensor_copy(lg[:, :, 0, :], gi).then_inc(g_abs, 1)
                    dve.wait_ge(g_ln, 1)
                    step(dve.tensor_scalar(lg[:, :, 4, :], gf, 0.0, None, ALU.min))
                    dve.tensor_tensor(lg[:, :, 4, :], lg[:, :, 4, :], lg[:, :, 3, :], ALU.subtract).then_inc(g_dve, 1)
                    step(dve.memset(row[:, 7, :], 1.0))
                    dve.wait_ge(g_rows, 1)
                    one = row[:, 7, :]
                    step(dve.tensor_tensor_scan(row[:, 2, :], one, row[:, 1, :], 0.0, ALU.mult, ALU.add))
                    step(dve.tensor_tensor(row[:, 3, :], row[:, 0, :], row[:, 2, :], ALU.subtract))
                    step(dve.tensor_tensor_scan(row[:, 4, :], one, row[:, 3, :], 0.0, ALU.mult, ALU.max))
                    step(dve.tensor_scalar(row[:, 5, :], row[:, 4, :], -1.0, None, ALU.mult))
                    dve.tensor_tensor(row[:, 6, :], row[:, 4, :], row[:, 2, :], ALU.add).then_inc(g_b, 1)
                    dve.wait_ge(par_in, 32)
                    for h in range(HEADS):
                        i = dve.tensor_scalar(neg[:, h, :], row[:, 5, :], eye8[:, h:h + 1], None, ALU.mult)
                    i.then_inc(neg_made, 1)
                    dve.wait_ge(g_col, 1)
                    tri_m = cst[:, C_TRI:C_TRI + P]
                    with loop(dve, HEADS, 2) as h:
                        for w in range(2):
                            dve.wait_ge(scores, h + (w + 1))
                            dve.tensor_tensor(ee[:, w, 0, :], PS[:, 2 + w, 0:P], tri_m, ALU.add)
                            dve.tensor_tensor(ee[:, w, 2, :], PS[:, 2 + w, P:T], tri_m, ALU.add).then_inc(tri, 1)
                        for w in range(2):
                            dve.wait_ge(exps, h + (w + 1))
                            dve.scalar_tensor_tensor(ss[:, w, :, :].rearrange("p b t -> p (b t)"), PS[:, w, 0:3 * P], scale,
                                                     ee[:, w, :, :].rearrange("p b t -> p (b t)"), ALU.mult, ALU.mult).then_inc(wts, 1)
                        for w in range(2):
                            dve.wait_ge(num_sb, h + (w + 1))
                            d = num[:, w, :, P]
                            dve.scalar_tensor_tensor(den[:, w, 0, :], d, -1.0, d, ALU.mult, ALU.max).then_inc(dens, 1)
                            dve.wait_ge(dens, h * 3 + (3 * w + 1))
                            dve.tensor_tensor(den[:, w, 1, :], den[:, w, 0, :], colb[:, :, 1, ds(h + w, 1)].rearrange("p t o -> p (t o)"),
                                              ALU.max).then_inc(dens, 1)
                            dve.wait_ge(dens, h * 3 + (3 * w + 2))
                            dve.reciprocal(den[:, w, 2, :], den[:, w, 1, :]).then_inc(dens, 1)
                            dve.wait_ge(dens, h * 3 + (3 * w + 3))
                            for t in range(TT):
                                i = dve.tensor_scalar(hm[:, t, h + w, :], num[:, w, t, 0:P], den[:, w, 2, t:t + 1], None, ALU.mult)
                            i.then_inc(hms, 1)
                            dve.wait_ge(hms, h + (w + 1))
                            dve.sem_inc(s_used, 1)
                    for t in range(TT):
                        for h in range(HEADS):
                            i = dve.bn_stats(st[:, t, h, :], hm[:, t, h, :])
                    step(i)
                    for n in range(TT * HEADS):
                        i = dve.bn_aggr(hv[:, n, 0:2], st[:, n // HEADS, n % HEADS, :])
                    step(i)
                    dve.tensor_scalar(hv[:, :, 2], hv[:, :, 1], 1e-5, None, ALU.add).then_inc(asked, 1)
                    dve.wait_ge(o_exp, 1)
                    step(dve.tensor_scalar(ex[:, :, :], ex[:, :, :], 1.0, None, ALU.add))
                    step(dve.reciprocal(ex[:, :, :], ex[:, :, :]))
                    step(dve.tensor_tensor(ex[:, :, :], ex[:, :, :], mh_g[:, None, :].broadcast_to([P, TT, WA]), ALU.mult))
                    dve.wait_ge(given, 1)
                    step(dve.reciprocal(hv[:, :, 4], hv[:, :, 3]))
                    for n in range(TT * HEADS):
                        hh = hm[:, n // HEADS, n % HEADS, :]
                        i = dve.tensor_scalar(hh, hh, hv[:, n, 0:1], hv[:, n, 4:5], ALU.subtract, ALU.mult)
                    step(i)
                    flat = hm[:, :, :, :].rearrange("p t h e -> p t (h e)")
                    dve.tensor_tensor(flat, flat, ex[:, :, :], ALU.mult).then_inc(ymr, 1)
                    for b in range(4):
                        dve.wait_ge(rnd, b + 1)
                        s = slice(8 + 2 * b, 10 + 2 * b)
                        dve.tensor_tensor(mix_lo[:, s, :], PS[:, b % 2, :].rearrange("p (k t) -> p k t", k=2),
                                          mix_hi[:, s, :].bitcast(F), ALU.subtract).then_inc(cp, 1)
        cell.close()

        with ExitStack() as ph:
            par = [buf2(f"parb{i}", [P, D], F, ph) for i in range(2)]
            par_in, acc_free, resid, asked, given, stored, ready = (
                sem(x + "_4") for x in ("par_in", "acc_free", "resid", "asked", "given", "stored", "ready"))
            m0 = split_at["out2"]
            with stage() as blk:
                @blk.sync
                def _(sp):
                    load_slabs(sp, src_out2, base["out2"], NRAW, N_OUT2)
                    load_slabs(sp, src_wq, base["wq"], 0, NRAW)
                    sp.wait_ge(ready, 2)
                    sp.dma_start(h_dram, h_buf[:, :, :]).then_inc(stored, 16)
                    sp.wait_ge(stored, 16)

                @blk.gpsimd
                def _(pool):
                    clear_last_stage(pool)
                    for i, name in enumerate(("ln1_g", "ln1_b")):
                        pool.dma_start(par[i][:, :], bcast(io[name])).then_inc(par_in, 16)

                @blk.tensor
                def _(pe):
                    with loop(pe, 4, 2) as c:
                        for u in range(2):
                            pe.wait_ge(acc_free, c + (u + 1))
                            for g in range(8):
                                token_slab(pe, [PS[:, 2 * u + t, :] for t in range(TT)], c * 8, m0 + 8 * u + g, g, mix_hi, mix_lo)

                @blk.scalar
                def _(act):
                    with loop(act, N_OUT2, NRAW) as i:
                        for s in range(NRAW):
                            round_slab(act, i, m0 + s + 1)
                    for t in range(TT):
                        act.wait_ge(asked, t + 1)
                        act.activation(mv[:, t, 3:4], mv[:, t, 2:3], ACT.Sqrt).then_inc(given, 1)

                @blk.vector
                def _(dve):
                    step = chain(dve, "dve_out2")
                    dve.sem_inc(acc_free, 2)
                    with loop(dve, 4, 2) as c:
                        for u in range(2):
                            for g in range(8):
                                split_slab(dve, c * 8, m0 + 8 * u + g + 1)
                            dve.wait_ge(multiplied, c * 8 + (2 + m0 + 8 * u + 8))
                            for t in range(TT):
                                hh = h_buf[:, t, ds(c * 512 + u * 512, 512)]
                                i = dve.scalar_tensor_tensor(hh, hh, ALPHA, PS[:, 2 * u + t, :], ALU.mult, ALU.add)
                            i.then_inc(acc_free, 1)
                    dve.wait_ge(acc_free, 6)
                    dve.wait_ge(par_in, 32)
                    for t in range(TT):
                        norm_stats(dve, step, h_buf, t, asked)
                    for t in range(TT):
                        norm_apply(dve, step, h_buf, t, given, 0, par[0], par[1]).then_inc(ready, 1)
        second.close()

        top = ExitStack()
        ctx.enter_context(top)

        def buf3(name, shape, dt=F, where=top):
            return where.enter_context(nc.sbuf_tensor(name, shape, dt))
        pick = buf3("pick", [P, 3, T])
        hT = top.enter_context(ExitStack())
        h_hi_at = nc.sbuf_base
        h_hi = buf3("h2_hi", [P, KT, T], R, hT)
        h_lo = buf3("h2_lo", [P, KT, T], R, hT)

        with ExitStack() as ph:
            qp = buf3("qp", [P, 2 * HEADS, T], F, ph)
            keys = buf3("keys", [P, 2 * HEADS, N_KEYS], F, ph)
            sv = buf3("sv", [P, TT, 2 * HEADS, TOPK], F, ph)
            si = buf3("si", [P, TT, 2 * HEADS, TOPK], F, ph)
            ts = buf3("ts", [P, TT, HEADS, TOPK], F, ph)
            gt = buf3("gt", [P, TT, HEADS, TOPK], F, ph)
            gs = buf3("gs", [P, TT, HEADS, 2], F, ph)
            eid = buf3("eid", [P, TT, 2, HEADS, TOPK], F, ph)
            t8 = buf3("t8", [P, TT, TOPK], F, ph)
            i8 = buf3("i8", [P, TT, TOPK], U32, ph)
            rest = buf3("rest", [P, TT, 256], F, ph)
            cand = buf3("cand", [P, TT, 256], F, ph)
            abu = buf3("abu", [P, TT, 2, TOPK], U32, ph)
            abf = buf3("abf", [P, TT, 2, TOPK], F, ph)
            eq = buf3("eq", [P, TT, 2, 256], F, ph)
            tr, rnd, cp, keys_in, acc_free, s_done, s_free, tk, sh, g_exp, g_ready, p_tr, p_out = (
                sem(x + "_5") for x in ("tr", "rnd", "cp", "keys_in", "acc_free", "s_done", "s_free", "tk", "sh", "g_exp",
                                        "g_ready", "p_tr", "p_out"))
            m0 = split_at["wq"]
            with stage() as blk:
                @blk.sync
                def _(sp):
                    sp.dma_start(keys[:, :, :], io["keys"]).then_inc(keys_in, 16)
                    load_slabs(sp, src_wq, base["wq"], NRAW, N_WQ)
                    load_slabs(sp, src_u, base["u"], 0, NRAW)

                @blk.gpsimd
                def _(pool):
                    clear_last_stage(pool)

                @blk.tensor
                def _(pe):
                    transpose_in(pe, h_buf, None, cp, tr, banks=(0, 1))
                    pe.wait_ge(cp, 8)
                    with loop(pe, 2 * HEADS, 2) as j:
                        for u in range(2):
                            pe.wait_ge(acc_free, j + (u + 1))
                            for half in range(2):
                                feature_slab(pe, PS[:, 2 + u, 0:T], j * 2, m0 + 2 * u + half, half, h_hi, h_lo, slice(0, T))
                    pe.wait_ge(acc_free, 2 + 2 * HEADS)
                    pe.wait_ge(keys_in, 16)
                    for hp in range(2 * HEADS):
                        pe.wait_ge(s_free, hp + 1)
                        for t in range(TT):
                            last = pe.matmul(PS[:, 4 + hp % 2, t * N_KEYS:(t + 1) * N_KEYS], qp[:, hp, t * P:(t + 1) * P],
                                             keys[:, hp, :], start=True, stop=True)
                        last.then_inc(s_done, 1)
                    pe.wait_ge(g_ready, 1)
                    for a in range(3):
                        for t in range(TT):
                            src = gt[:, t, :, :] if a == 2 else eid[:, t, a, :, :]
                            last = pe.transpose(PS[:, a, t * P:(t + 1) * P], src.rearrange("p h k -> p (h k)"), ident)
                    last.then_inc(p_tr, 1)

                @blk.scalar
                def _(act):
                    transposed_round(act, tr, h_hi, rnd, banks=(0, 1))
                    act.sem_inc(acc_free, 2)
                    with loop(act, 2 * HEADS, 2) as j:
                        for u in range(2):
                            for s in range(2):
                                round_slab(act, j * 2, m0 + 2 * u + s + 1)
                            act.wait_ge(multiplied, j * 2 + (2 + m0 + 2 * u + 2))
                            act.activation(qp[:, j + u, :], PS[:, 2 + u, 0:T], ACT.Copy).then_inc(acc_free, 1)
                    act.wait_ge(sh, 1)
                    act.activation(gt[:, :, :, :], gt[:, :, :, :], ACT.Exp).then_inc(g_exp, 1)
                    act.wait_ge(p_tr, 1)
                    act.activation(pick[:, :, :], PS[:, 0:3, 0:T], ACT.Copy).then_inc(p_out, 1)

                @blk.vector
                def _(dve):
                    step = chain(dve, "dve_top")
                    transposed_split(dve, h_hi, h_lo, rnd, cp, banks=(0, 1))
                    with loop(dve, N_WQ, NRAW) as i:
                        for s in range(NRAW):
                            split_slab(dve, i, m0 + s + 1)
                    dve.sem_inc(s_free, 2)
                    low = -3.0e38

                    def top16(src, n, values_of, count, first):
                        def after(i, k):
                            i.then_inc(tk, 1)
                            dve.wait_ge(tk, count(k))
                            carry(dve)
                        for t in range(TT):
                            i = dve.max(t8[:, t, 0:8], src[t])
                        after(i, first + 1)
                        for t in range(TT):
                            dve.max_index(i8[:, t, 0:8], t8[:, t, 0:8], src[t])
                            i = dve.match_replace(rest[:, t, 0:n], t8[:, t, 0:8], src[t], low)
                        after(i, first + 2)
                        for t in range(TT):
                            i = dve.max(t8[:, t, 8:16], rest[:, t, 0:n])
                        after(i, first + 3)
                        for t in range(TT):
                            i = dve.max_index(i8[:, t, 8:16], t8[:, t, 8:16], rest[:, t, 0:n])
                        after(i, first + 4)

                    with loop(dve, 2 * HEADS, 2) as j:
                        for u in range(2):
                            dve.wait_ge(s_done, j + (u + 1))
                            carry(dve)
                            top16([PS[:, 4 + u, t * N_KEYS:(t + 1) * N_KEYS] for t in range(TT)], N_KEYS, None,
                                  lambda k: j * 5 + k, 5 * u)
                            dve.sem_inc(s_free, 1)
                            dve.tensor_copy(sv[:, :, j + u, :], t8[:, :, :])
                            dve.tensor_copy(si[:, :, j + u, :], i8[:, :, :]).then_inc(tk, 1)
                            dve.wait_ge(tk, j * 5 + (5 * u + 5))
                    b0 = 5 * 2 * HEADS
                    per = 9
                    iota16 = cst[:, C_IOTA:C_IOTA + TOPK]
                    with loop(dve, HEADS) as h:
                        def after(i, k):
                            i.then_inc(tk, 1)
                            dve.wait_ge(tk, h * per + (b0 + k))
                            carry(dve)
                        for t in range(TT):
                            s0 = sv[:, t, h * 2, :][:, :, None].broadcast_to([P, TOPK, TOPK])
                            s1 = sv[:, t, h * 2 + 1, :][:, None, :].broadcast_to([P, TOPK, TOPK])
                            i = dve.tensor_tensor(cand[:, t, :].rearrange("p (a b) -> p a b", a=TOPK), s0, s1, ALU.add)
                        after(i, 1)
                        top16([cand[:, t, :] for t in range(TT)], 256, None, lambda k: h * per + (b0 + k), 1)
                        dve.tensor_copy(ts[:, :, h, :], t8[:, :, :])
                        dve.tensor_scalar(abu[:, :, 0, :], i8[:, :, :], 4, None, ALU.logical_shift_right)
                        after(dve.tensor_scalar(abu[:, :, 1, :], i8[:, :, :], 15, None, ALU.bitwise_and), 6)
                        after(dve.tensor_copy(abf[:, :, :, :], abu[:, :, :, :]), 7)
                        for t in range(TT):
                            for half in range(2):
                                e3 = eq[:, t, half, :].rearrange("p (k a) -> p k a", k=TOPK)
                                i = dve.tensor_tensor(e3, abf[:, t, half, :][:, :, None].broadcast_to([P, TOPK, TOPK]),
                                                      iota16[:, None, :].broadcast_to([P, TOPK, TOPK]), ALU.is_equal)
                        after(i, 8)
                        for t in range(TT):
                            for half in range(2):
                                e3 = eq[:, t, half, :].rearrange("p (k a) -> p k a", k=TOPK)
                                i = dve.tensor_tensor(e3, e3, si[:, t, h * 2 + half, :][:, None, :].broadcast_to([P, TOPK, TOPK]),
                                                      ALU.mult)
                        after(i, 9)
                        for t in range(TT):
                            for half in range(2):
                                e3 = eq[:, t, half, :].rearrange("p (k a) -> p k a", k=TOPK)
                                dve.tensor_reduce(eid[:, t, half, h, :], e3, X, ALU.add)
                    for t in range(TT):
                        i = dve.tensor_tensor(gt[:, t, :, :], ts[:, t, :, :], ts[:, t, :, 0:1].broadcast_to([P, HEADS, TOPK]),
                                              ALU.subtract)
                    i.then_inc(sh, 1)
                    dve.wait_ge(g_exp, 1)
                    step(dve.tensor_reduce(gs[:, :, :, 0], gt[:, :, :, :], X, ALU.add))
                    step(dve.reciprocal(gs[:, :, :, 1], gs[:, :, :, 0]))
                    for t in range(TT):
                        i = dve.tensor_tensor(gt[:, t, :, :], gt[:, t, :, :], gs[:, t, :, 1:2].broadcast_to([P, HEADS, TOPK]),
                                              ALU.mult)
                    i.then_inc(g_ready, 1)
        wt = buf3("wt", [P, N_KEYS, T])
        acc_free = sem("acc_free_u")
        m0 = split_at["u"]
        with stage() as blk:
            @blk.sync
            def _(sp):
                load_slabs(sp, src_u, base["u"], NRAW, N_U)
                load_slabs(sp, src_v, base["v"], 0, NRAW)

            @blk.gpsimd
            def _(pool):
                clear_last_stage(pool)

            @blk.tensor
            def _(pe):
                with loop(pe, N_KEYS, 2) as j:
                    for u in range(2):
                        pe.wait_ge(acc_free, j + (u + 1))
                        for half in range(2):
                            feature_slab(pe, PS[:, u, 0:T], j * 2, m0 + 2 * u + half, half, h_hi, h_lo, slice(0, T))

            @blk.scalar
            def _(act):
                act.preload_act_table(ACT.Gelu)
                act.sem_inc(acc_free, 2)
                with loop(act, N_KEYS, 2) as j:
                    for u in range(2):
                        for s in range(2):
                            round_slab(act, j * 2, m0 + 2 * u + s + 1)
                        act.wait_ge(multiplied, j * 2 + (2 + m0 + 2 * u + 2))
                        act.activation(wt[:, j + u, :], PS[:, u, 0:T], ACT.Gelu).then_inc(acc_free, 1)

            @blk.vector
            def _(dve):
                with loop(dve, N_U, NRAW) as i:
                    for s in range(NRAW):
                        split_slab(dve, i, m0 + s + 1)

        GT = 4
        with ExitStack() as ph:
            row_hot = buf3("row_hot", [P, 2, GT, N_KEYS], F, ph)
            col_hot = buf3("col_hot", [P, 2, GT, N_KEYS], F, ph)
            col_of = buf3("col_of", [P, 2, GT], F, ph)
            rows_made, cols_made, dense, weighed, col_in = (
                sem(x) for x in ("rows_made", "cols_made", "dense", "weighed", "col_in"))
            iota = cst[:, C_IOTA:C_IOTA + N_KEYS]
            with stage() as blk:
                @blk.gpsimd
                def _(pool):
                    clear_last_stage(pool)
                    pool.sem_inc(weighed, 2)
                    with loop(pool, T // GT, 2) as g:
                        for u in range(2):
                            pool.wait_ge(weighed, g + (u + 1))
                            pool.tensor_copy(col_of[:, u, :], pick[:, 1, ds(g * GT + u * GT, GT)]).then_inc(col_in, 1)
                            pool.wait_ge(col_in, g + (u + 1))
                            carry(pool)
                            for t in range(GT):
                                i = pool.tensor_scalar(col_hot[:, u, t, :], iota, col_of[:, u, t:t + 1], None, ALU.is_equal)
                            i.then_inc(cols_made, 1)

                @blk.vector
                def _(dve):
                    with loop(dve, T // GT, 2) as g:
                        for u in range(2):
                            for t in range(GT):
                                tok = ds(g * GT + (u * GT + t), 1)
                                i = dve.tensor_scalar(row_hot[:, u, t, :], iota, pick[:, 0, tok], pick[:, 2, tok],
                                                      ALU.is_equal, ALU.mult)
                            i.then_inc(rows_made, 1)
                        for u in range(2):
                            dve.wait_ge(dense, g + (u + 1))
                            w = wt[:, :, ds(g * GT + u * GT, GT)]
                            dve.tensor_tensor(w, w, PS[:, 2 + u, :].rearrange("p (t j) -> p j t", t=GT), ALU.mult).then_inc(weighed, 1)

                @blk.tensor
                def _(pe):
                    with loop(pe, T // GT, 2) as g:
                        for u in range(2):
                            pe.wait_ge(rows_made, g + (u + 1))
                            pe.wait_ge(cols_made, g + (u + 1))
                            for t in range(GT):
                                last = pe.matmul(PS[:, 2 + u, t * N_KEYS:(t + 1) * N_KEYS], row_hot[:, u, t, :],
                                                 col_hot[:, u, t, :], start=True, stop=True)
                            last.then_inc(dense, 1)

        with ExitStack() as ph:
            wj_hi = [buf3(f"wj_hi{i}", [P, T], R, ph) for i in range(2)]
            wj_lo = [buf3(f"wj_lo{i}", [P, T], R, ph) for i in range(2)]
            hb = nc.alloc_sbuf_tensor_at("hb", [P, TT, D], F, offset=h_hi_at)
            par = [nc.alloc_sbuf_tensor_at(f"parc{i}", [P, D], F, offset=h_hi_at + (TT + i) * D * 4) for i in range(2)]
            wj_round, wj_split, late_in, ff_done, asked, given, ready, out_done = (
                sem(x + "_6") for x in ("wj_round", "wj_split", "late_in", "ff_done", "asked", "given", "ready", "out_done"))
            m0 = split_at["v"]
            with stage() as blk:
                @blk.sync
                def _(sp):
                    load_slabs(sp, src_v, base["v"], NRAW, N_V)
                    for t in range(TT):
                        sp.wait_ge(ready, t + 1)
                        sp.dma_start(io["out"][t * P:(t + 1) * P, :], hb[:, t, :]).then_inc(out_done, 16)
                    sp.wait_ge(out_done, 32)

                @blk.gpsimd
                def _(pool):
                    clear_last_stage(pool)
                    pool.dma_start(hb[:, :, :], h_dram).then_inc(late_in, 16)
                    for i, name in enumerate(("ln2_g", "ln2_b")):
                        pool.dma_start(par[i][:, :], bcast(io[name])).then_inc(late_in, 16)

                def split_weights(act, dve, j, u):
                    n = u if j is None else j + u
                    if act is not None:
                        act.wait_ge(multiplied, 2 + m0 - 4 + 2 * u + 2 if j is None else j * 2 + (2 + m0 - 4 + 2 * u + 2))
                        act.activation(wj_hi[u % 2][:, :], wt[:, n, :], ACT.Copy).then_inc(wj_round, 1)
                    if dve is not None:
                        dve.wait_ge(wj_round, n + 1)
                        dve.tensor_tensor(wj_lo[u % 2][:, :], wt[:, n, :], wj_hi[u % 2][:, :].bitcast(F), ALU.subtract)\
                           .then_inc(wj_split, 1)

                @blk.scalar
                def _(act):
                    def pair(j, last):
                        for u in range(2):
                            split_weights(act, None, j, u)
                            for s in range(2):
                                if not (last and u == 1 and s == 1):
                                    round_slab(act, None if j is None else j * 2, m0 + 2 * u + s + 1)
                    with loop(act, N_KEYS - 2, 2) as j:
                        pair(j, False)
                    for u in range(2):
                        split_weights(act, None, None, N_KEYS - 2 + u)
                        for s in range(2 - u):
                            round_slab(act, None, m0 + 2 * (N_KEYS - 2 + u) + s + 1)
                    for t in range(TT):
                        act.wait_ge(asked, t + 1)
                        act.activation(mv[:, t, 3:4], mv[:, t, 2:3], ACT.Sqrt).then_inc(given, 1)

                @blk.vector
                def _(dve):
                    step = chain(dve, "dve_last")
                    with loop(dve, N_KEYS - 2, 2) as j:
                        for u in range(2):
                            split_weights(None, dve, j, u)
                            for s in range(2):
                                split_slab(dve, j * 2, m0 + 2 * u + s + 1)
                    for u in range(2):
                        split_weights(None, dve, None, N_KEYS - 2 + u)
                        for s in range(2 - u):
                            split_slab(dve, None, m0 + 2 * (N_KEYS - 2 + u) + s + 1)
                    dve.wait_ge(late_in, 48)
                    dve.wait_ge(multiplied, 2 + m0 + N_V)
                    for t in range(TT):
                        for c in range(4):
                            hh = hb[:, t, c * 512:(c + 1) * 512]
                            i = dve.scalar_tensor_tensor(hh, hh, ALPHA, PS[:, 4 * t + c, :], ALU.mult, ALU.add)
                        step(i)
                        norm_stats(dve, step, hb, t, asked)
                    for t in range(TT):
                        norm_apply(dve, step, hb, t, given, 0, par[0], par[1]).then_inc(ready, 1)

                @blk.tensor
                def _(pe):
                    def expert_slab(j, m, n, a, first, last_one):
                        pe.wait_ge(lo_ready, m + 1 if j is None else j * 2 + (m + 1))
                        if a == 0:
                            pe.wait_ge(wj_split, n + 1 if j is None else j + (n + 1))
                        for t in range(TT):
                            tok = slice(t * P, (t + 1) * P)
                            for c in range(2):
                                col = slice(c * 512, (c + 1) * 512)
                                last = mm3(pe, PS[:, 4 * t + 2 * a + c, :], (wj_hi[n % 2][:, tok], wj_lo[n % 2][:, tok]),
                                           (w_hi[m % 2][:, col], w_lo[m % 2][:, col]), first, last_one)
                        last.then_inc(multiplied, 1)
                    for u in range(2):
                        for a in range(2):
                            expert_slab(None, m0 + 2 * u + a, u, a, u == 0, False)
                    with loop(pe, N_KEYS - 4, 2) as j:
                        for u in range(2):
                            for a in range(2):
                                expert_slab(j, m0 + 4 + 2 * u + a, 2 + u, a, False, False)
                    for n in range(N_KEYS - 2, N_KEYS):
                        for a in range(2):
                            expert_slab(None, m0 + 2 * n + a, n, a, False, n == N_KEYS - 1)
        top.close()


NAMES = ["x", "ctx", "c_cols", "consts", "mod_cols", "lam_in", "w_mod_s", "w_in_a", "w_in_b", "rpb_e", "subln_g",
         "w_out_s", "final_g", "ln_in_g", "ln_in_b", "w_in2_s", "conv_cols", "w_gate_cols", "b_gate", "mh_g", "w_out2_s",
         "ln1_g", "ln1_b", "wq_s", "keys", "u_s", "v", "ln2_g", "ln2_b"]


def constants():
    import numpy as np
    c = np.zeros((P, C_ALL), np.float32)
    p = np.arange(P)
    c[p, C_IDENT + p] = 1
    c[:, C_ONES:C_ONES + P] = 1
    c[:, C_TRI:C_TRI + P] = np.where(p[:, None] <= p[None, :], 0.0, MASKED)
    c[:, C_IOTA:C_IOTA + P] = p
    f = p % 64
    partner = np.where(p % 32 < 16, p + 16, p - 16)
    c[partner, C_PERM + p] = 1
    inv = (np.float32(10000.0) ** (-np.arange(16, dtype=np.float32) / np.float32(16))).astype(np.float32)
    t = np.arange(T)
    pos = np.where((f < 32)[:, None], (t // 64)[None, :], (t % 64)[None, :]).astype(np.float32)
    ang = pos * inv[p % 16][:, None]
    c[:, C_COS:C_COS + T] = np.cos(ang)
    c[:, C_SIN:C_SIN + T] = np.sin(ang) * np.where(p % 32 < 16, -1, 1)[:, None]
    j, col = (p % 64)[:, None], np.arange(64)[None, :]
    c0 = np.clip(j - 8, 0, 48)
    c[:, C_NAMASK:C_NAMASK + 64] = np.where((col >= c0) & (col < c0 + 16), 0.0, MASKED)
    c[np.arange(8), C_EYE8 + np.arange(8)] = 1
    return c


def feature_slabs(w):
    import numpy as np
    n = w.shape[1] // P
    return np.ascontiguousarray(w.reshape(2, 8, P, n, P).transpose(3, 0, 2, 1, 4)).reshape(2 * n, P, SLAB)


def token_slabs(w):
    import numpy as np
    n = w.shape[1] // 512
    return np.ascontiguousarray(w.reshape(8, 2, P, n, 512).transpose(3, 0, 2, 1, 4)).reshape(8 * n, P, SLAB)


def cols(v):
    return v.reshape(-1, P).T


def lay_out(i):
    import numpy as np
    w_in, w2 = i["w_in"][0], i["w_in_2"][0]
    pad = np.pad(i["rpb"][0], ((0, 0), (0, 0), (48, 48)))
    rpb_e = np.stack([pad[:, :, 63 - j:127 - j] for j in range(64)], axis=1).reshape(HEADS, 64, 15 * 64)
    half = lambda o: np.concatenate([feature_slabs(w_in[:, o:o + 2 * WA]), token_slabs(w_in[:, o + 2 * WA:o + 4 * WA])])
    conv = feature_slabs(w2[:, 0:3 * WA]).reshape(3, 8, 2, P, SLAB).transpose(1, 0, 2, 3, 4).reshape(48, P, SLAB)
    return {
        "x": i["x"][0], "ctx": i["ctx"][0],
        "c_cols": np.stack([cols(i["c"][0]), cols(i["c_ctx"])], axis=2),
        "consts": constants(),
        "mod_cols": np.concatenate([cols(i["b_mod"][0]), cols(i["norm_g"][0])], axis=1),
        "lam_in": np.concatenate([i["lam_q1"][0], i["lam_k1"][0], i["lam_q2"][0], i["lam_k2"][0]])[None],
        "w_mod_s": feature_slabs(i["w_mod"][0]),
        "w_in_a": half(0), "w_in_b": half(4 * WA),
        "rpb_e": rpb_e, "subln_g": i["subln_g"],
        "w_out_s": token_slabs(i["w_out"][0]),
        "final_g": i["final_g"][None], "ln_in_g": i["ln_in_g_2"][None], "ln_in_b": i["ln_in_b_2"][None],
        "w_in2_s": np.concatenate([conv, feature_slabs(w2[:, 3 * WA:5 * WA]), token_slabs(w2[:, 5 * WA:7 * WA])]),
        "conv_cols": np.concatenate([cols(i["conv_w_2"][0, n]) for n in range(3)] + [cols(i["conv_b_2"][0])], axis=1),
        "w_gate_cols": w2[:, 7 * WA:].reshape(KT, P, 16).transpose(1, 0, 2).reshape(P, KT * 16),
        "b_gate": i["b_gate_2"], "mh_g": i["mh_norm_g_2"],
        "ln1_g": i["ln1_g_2"], "ln1_b": i["ln1_b_2"], "ln2_g": i["ln2_g_2"], "ln2_b": i["ln2_b_2"],
        "keys": i["peer_keys_2"][0].reshape(2 * HEADS, N_KEYS, P).transpose(2, 0, 1),
        "w_out2_s": token_slabs(i["w_out_2"][0]), "wq_s": feature_slabs(i["peer_wq_2"][0]),
        "u_s": np.ascontiguousarray(i["peer_u_2"][0].reshape(N_KEYS, N_KEYS, 2, 8, P).transpose(1, 2, 4, 3, 0)).reshape(2 * N_KEYS, P, SLAB),
        "v": i["peer_v_2"][0],
    }


def kernel(**inputs):
    import numpy as np
    import concourse.bacc as bacc
    from concourse.bass_utils import run_bass_kernel_spmd

    nc = bacc.Bacc("TRN2", target_bir_lowering=False, num_devices=1)
    laid = lay_out({k: np.asarray(v) for k, v in inputs.items()})
    arrays, io = {}, {}
    for name in NAMES:
        a = np.ascontiguousarray(laid[name])
        arrays[f"in_{name}"] = a
        io[name] = nc.dram_tensor(f"in_{name}", a.shape, mybir.dt.from_np(a.dtype), kind="ExternalInput").ap()
    io["out"] = nc.dram_tensor("out_0_dram", (T, D), mybir.dt.float32, kind="ExternalOutput").ap()
    peer_block_kernel(nc, io)
    r = run_bass_kernel_spmd(nc, [arrays], core_ids=[0])
    return r.results[0]["out_0_dram"].reshape(1, T, D)
```

```python
import concourse.bass as bass
from concourse import mybir
from contextlib import ExitStack, contextmanager

T = 256
D = 2048
P = 128
KT = D // P
TT = T // P
WA = 1024
HEADS = 8
SLAB = 1024
LAMBDA_INIT = 0.2
MASKED = -1e30
ALPHA = 2 ** 0.25
N_KEYS = 128
TOPK = 16

N_MOD, N_WIN_A, N_WIN_B, N_OUT, N_WIN2, N_OUT2, N_WQ, N_U, N_V = 96, 64, 64, 32, 112, 32, 32, 256, 256
NRAW = 4

C_IDENT, C_ONES, C_TRI, C_IOTA = 0, 128, 256, 384
C_PERM, C_COS, C_SIN, C_NAMASK, C_EYE8 = 512, 640, 896, 1152, 1216
C_KEEP, C_ALL = 512, 1224
H_OFFSET = 212960


@contextmanager
def loop(eng, count, step=1):
    with eng.Fori(0, count // step) as i:
        yield i * step if step > 1 else i


def peer_block_kernel(nc, io):
    F, R = mybir.dt.float32, mybir.dt.float32r
    U32 = mybir.dt.uint32
    ALU = mybir.AluOpType
    ACT = mybir.ActivationFunctionType
    X = mybir.AxisListType.X
    ds = bass.ds
    ctx = ExitStack()

    def lasting_sem(name):
        return ctx.enter_context(nc.semaphore(name))

    used, to_clear = [], []

    def sem(name):
        used.append(nc.alloc_semaphore(name=name))
        return used[-1]

    def clear_last_stage(pool):
        for s in to_clear:
            pool.sem_clear(s)

    @contextmanager
    def stage():
        with nc.Block() as block:
            yield block
        for s in to_clear:
            nc.release_semaphore(s)
        to_clear[:] = used
        used.clear()

    with ctx:
        def keep(name, shape, dt=F):
            return ctx.enter_context(nc.sbuf_tensor(name, shape, dt))

        raw = keep("raw", [P, NRAW, SLAB])
        w_hi = [keep(f"w_hi{i}", [P, SLAB], R) for i in range(2)]
        w_lo = [keep(f"w_lo{i}", [P, SLAB], R) for i in range(2)]
        raw_ready = [lasting_sem(f"raw_ready{i}") for i in range(NRAW)]
        hi_ready = lasting_sem("hi_ready")
        lo_ready = lasting_sem("lo_ready")
        multiplied = lasting_sem("multiplied")
        HALVES = [slice(0, SLAB // 2), slice(SLAB // 2, SLAB)]

        def halves(reg, m):
            return 2 * m if reg is None else reg * 2 + 2 * m

        def wait_multiplied(eng, reg, n):
            eng.wait_ge(multiplied, halves(reg, n) + 4)

        passed = lasting_sem("passed")

        def raw_wait(eng, slab):
            reg, off = slab
            if reg is None:
                eng.wait_ge(raw_ready[off % NRAW], 16 * (off // NRAW + 1))
            else:
                eng.wait_ge(raw_ready[off % NRAW], reg * 4 + 16 * (off // NRAW + 1))

        def load_slabs(sp, src, base, first, last):
            def one(reg, off):
                n = base + off if reg is None else reg + (base + off)
                src_at = off if reg is None else reg + off
                if base + off >= NRAW:
                    sp.wait_ge(lo_ready, n * 2 - 2 * (NRAW - 1))
                sp.dma_start(raw[:, off % NRAW, :], src(src_at)).then_inc(raw_ready[off % NRAW], 16)
            if last - first <= NRAW:
                for off in range(first, last):
                    one(None, off)
                return
            with loop(sp, last - first, NRAW) as i:
                for s in range(NRAW):
                    one(i, first + s)

        def round_slab(act, reg, m):
            raw_wait(act, (reg, m))
            for x, half in enumerate(HALVES):
                act.wait_ge(multiplied, halves(reg, m) + (x + 1))
                act.activation(w_hi[m % 2][:, half], raw[:, m % NRAW, half], ACT.Copy).then_inc(hi_ready, 1)

        def split_slab(dve, reg, m):
            for x, half in enumerate(HALVES):
                dve.wait_ge(hi_ready, halves(reg, m) + (x + 1))
                dve.tensor_tensor(w_lo[m % 2][:, half], raw[:, m % NRAW, half], w_hi[m % 2][:, half].bitcast(F),
                                  ALU.subtract).then_inc(lo_ready, 1)

        def carry(eng):
            eng.sem_inc(passed, 1)

        def mm3(pe, out, lhs, rhs, start, stop):
            pe.matmul(out, lhs[0], rhs[0], start=start, stop=False)
            pe.matmul(out, lhs[0], rhs[1], start=False, stop=False)
            return pe.matmul(out, lhs[1], rhs[0], start=False, stop=stop)

        def feature_slab(pe, out, reg, m, half, x_hi, x_lo, cols):
            for k in range(8):
                if k % 4 == 0:
                    pe.wait_ge(lo_ready, halves(reg, m) + (k // 4 + 1))
                c = slice(k * P, (k + 1) * P)
                kk = 8 * half + k
                last = mm3(pe, out, (w_hi[m % 2][:, c], w_lo[m % 2][:, c]),
                           (x_hi[:, kk, cols], x_lo[:, kk, cols]), kk == 0, kk == KT - 1)
                if k % 4 == 3:
                    last.then_inc(multiplied, 1)

        def token_slab(pe, outs, reg, m, g, x_hi, x_lo):
            for k in range(2):
                pe.wait_ge(lo_ready, halves(reg, m) + (k + 1))
                c = slice(k * 512, (k + 1) * 512)
                kk = 2 * g + k
                for t, out in enumerate(outs):
                    tok = slice(t * P, (t + 1) * P)
                    last = mm3(pe, out, (x_hi[:, kk, tok], x_lo[:, kk, tok]),
                               (w_hi[m % 2][:, c], w_lo[m % 2][:, c]), kk == 0, kk == KT - 1)
                last.then_inc(multiplied, 1)

        PS = ctx.enter_context(nc.psum_tensor("PS", [P, 8, 512], F))
        cst = keep("cst", [P, C_KEEP])
        ident = cst[:, C_IDENT:C_IDENT + P]
        h_dram = nc.dram_tensor("h_dram", (P, TT, D), F, kind="Internal").ap()
        x_tok = io["x"].rearrange("(t p) d -> p t d", p=P)
        small = lasting_sem("small")

        def small_load(eng, dst, src):
            eng.dma_start(dst, src).then_inc(small, 16)

        def bcast(row):
            return bass.AP(row.tensor, row.offset, [[0, P], [1, row.shape[-1]]])

        chains = {}

        def chain(eng, name):
            if name not in chains:
                chains[name] = [sem(name), 0]

            def step(instruction):
                chains[name][1] += 1
                instruction.then_inc(chains[name][0], 1)
                eng.wait_ge(chains[name][0], chains[name][1])
            return step

        src_mod = lambda n: io["w_mod_s"][n]
        src_a = lambda n: io["w_in_a"][n]
        src_b = lambda n: io["w_in_b"][n]
        src_out = lambda n: io["w_out_s"][n]
        src_in2 = lambda n: io["w_in2_s"][n]
        src_out2 = lambda n: io["w_out2_s"][n]
        src_wq = lambda n: io["wq_s"][n]
        src_u = lambda n: io["u_s"][n]
        v_view = io["v"].rearrange("(i j) (a c) -> (j a) i c", j=N_KEYS, a=2)
        src_v = lambda n: v_view[n]
        base = {}
        at = 0
        for name, n in (("mod", N_MOD), ("a", N_WIN_A), ("b", N_WIN_B), ("out", N_OUT), ("in2", N_WIN2),
                        ("out2", N_OUT2), ("wq", N_WQ), ("u", N_U), ("v", N_V)):
            base[name] = at
            at += n
        split_at = base

        def transpose_in(pe, src, sem_src, copied, done, banks=(0, 1)):
            for b in range(KT // 2):
                if b >= 2:
                    pe.wait_ge(copied, b - 1)
                for k in range(2):
                    for t in range(TT):
                        if sem_src is not None and b == 0 and k == 0:
                            pe.wait_ge(sem_src[0], sem_src[1][t])
                        last = pe.transpose(PS[:, banks[b % 2], (2 * k + t) * P:(2 * k + t + 1) * P],
                                            src[:, t, (2 * b + k) * P:(2 * b + k + 1) * P], ident)
                last.then_inc(done, 1)

        def transposed_round(act, done, dst_hi, rounded, banks=(0, 1)):
            for b in range(KT // 2):
                act.wait_ge(done, b + 1)
                act.activation(dst_hi[:, 2 * b:2 * b + 2, :], PS[:, banks[b % 2], :], ACT.Copy).then_inc(rounded, 1)

        def transposed_split(dve, dst_hi, dst_lo, rounded, copied, banks=(0, 1)):
            for b in range(KT // 2):
                dve.wait_ge(rounded, b + 1)
                dve.tensor_tensor(dst_lo[:, 2 * b:2 * b + 2, :], PS[:, banks[b % 2], :].rearrange("p (k t) -> p k t", k=2),
                                  dst_hi[:, 2 * b:2 * b + 2, :].bitcast(F), ALU.subtract).then_inc(copied, 1)

        h_buf = nc.alloc_sbuf_tensor_at("h_buf", [P, TT, D], F, offset=H_OFFSET)
        stats = keep("stats", [P, TT, 4, 6])
        mv = keep("mv", [P, TT, 8])

        def norm_stats(dve, step, y, t, asked):
            for c in range(4):
                i = dve.bn_stats(stats[:, t, c, :], y[:, t, c * 512:(c + 1) * 512])
            step(i)
            step(dve.bn_aggr(mv[:, t, 0:2], stats[:, t, :, :]))
            dve.tensor_scalar(mv[:, t, 2:3], mv[:, t, 1:2], 1e-5, None, ALU.add).then_inc(asked, 1)

        def norm_apply(dve, step, y, t, given, given_before, g, b):
            dve.wait_ge(given, given_before + t + 1)
            step(dve.reciprocal(mv[:, t, 4:5], mv[:, t, 3:4]))
            step(dve.tensor_scalar(y[:, t, :], y[:, t, :], mv[:, t, 0:1], mv[:, t, 4:5], ALU.subtract, ALU.mult))
            step(dve.tensor_tensor(y[:, t, :], y[:, t, :], g[:, :], ALU.mult))
            return dve.tensor_tensor(y[:, t, :], y[:, t, :], b[:, :], ALU.add)

        with ExitStack() as first:
            def buf(name, shape, dt=F, where=first):
                return where.enter_context(nc.sbuf_tensor(name, shape, dt))

            csta = buf("csta", [P, C_ALL - C_KEEP])
            perm = csta[:, C_PERM - C_KEEP:C_PERM - C_KEEP + P]
            cos_t = csta[:, C_COS - C_KEEP:C_COS - C_KEEP + T]
            sin_t = csta[:, C_SIN - C_KEEP:C_SIN - C_KEEP + T]
            na_mask = csta[:, C_NAMASK - C_KEEP:C_NAMASK - C_KEEP + 64]
            modT = buf("modT", [P, 96])
            lam = buf("lam", [P, 8])
            o_a = buf("o_a", [P, TT, WA])
            o_b = buf("o_b", [P, TT, WA])
            late = first.enter_context(ExitStack())
            x_hi = buf("x_hi", [P, KT, 2 * T], R, late)
            x_lo = buf("x_lo", [P, KT, 2 * T], R, late)

            with ExitStack() as ph:
                xs = buf("xs", [P, 4, D], F, ph)
                xT = buf("xT", [P, KT, 2 * T], F, ph)
                junk = xT[:, 4:8, :].rearrange("p a b -> p (a b)")
                cin = buf("cin", [P, KT, 2], F, ph)
                cex = buf("cex", [P, KT, 2], F, ph)
                csilu = buf("csilu", [P, KT, 2], F, ph)
                cc = xT[:, 0:4, :].rearrange("p a (b w c) -> p (a b) w c", b=4, w=2)
                cc_hi = buf("cc_hi", [P, KT, P], R, ph)
                cc_lo = buf("cc_lo", [P, KT, P], R, ph)
                mod_row = buf("mod_row", [P, 2, 512], F, ph)
                bm = buf("bm", [P, 48 + KT], F, ph)
                lamv = buf("lamv", [P, 4, 64], F, ph)
                lamp = buf("lamp", [P, 2, 64], F, ph)
                ms = buf("ms", [P, 4, 4], F, ph)
                ab = buf("ab", [P, 2, KT], F, ph)
                x_in = [sem(f"x_in{i}") for i in range(4)]
                c_in = sem("c_in")
                exp_c, silu_c, cc_round, cc_split, sq, rms_asked, rms_given, normed = (
                    sem(n) for n in ("exp_c", "silu_c", "cc_round", "cc_split", "sq", "rms_asked", "rms_given", "normed"))
                tr, tr_out, row_free, row_in, mod_tr, mod_out, lam_asked, lam_given, affine, x_round = (
                    sem(n) for n in ("tr", "tr_out", "row_free", "row_in", "mod_tr", "mod_out", "lam_asked", "lam_given",
                                     "affine", "x_round"))
                tr_outv = sem("tr_outv")
                with stage() as blk:
                    @blk.sync
                    def _(sp):
                        sp.dma_start(cin[:, :, :], io["c_cols"]).then_inc(c_in, 16)
                        load_slabs(sp, src_mod, 0, 0, NRAW)
                        load_slabs(sp, src_mod, 0, NRAW, N_MOD)
                        load_slabs(sp, src_a, base["a"], 0, NRAW)

                    @blk.gpsimd
                    def _(pool):
                        clear_last_stage(pool)
                        small_load(pool, cst[:, :], io["consts"][:, 0:C_KEEP])
                        small_load(pool, csta[:, :], io["consts"][:, C_KEEP:C_ALL])
                        small_load(pool, bm[:, :], io["mod_cols"])
                        small_load(pool, lamv[:, :, :].rearrange("p a b -> p (a b)"), bcast(io["lam_in"]))

                    @blk.scalar
                    def _(act):
                        for t in range(4):
                            act.dma_start(xs[:, t, :], io["x" if t < 2 else "ctx"][(t % 2) * P:(t % 2 + 1) * P, :])\
                               .then_inc(x_in[t], 16)
                        act.wait_ge(c_in, 16)
                        act.activation(cex[:, :, :], cin[:, :, :], ACT.Exp, scale=-1.0).then_inc(exp_c, 1)
                        act.wait_ge(silu_c, 1)
                        act.activation(cc_hi[:, :, :], cc[:, :, :, :].rearrange("p k w c -> p k (w c)"), ACT.Copy).then_inc(cc_round, 1)
                        act.wait_ge(lam_asked, 1)
                        act.activation(lam[:, 2:4], lam[:, 0:2], ACT.Exp).then_inc(lam_given, 1)
                        round_slab(act, None, 0)

                        def copy_row(reg, tile):
                            wait_multiplied(act, None if reg is None else reg * 16, 8 * tile + 8)
                            act.wait_ge(row_free, tile + 1 if reg is None else reg * 2 + (tile + 1))
                            act.activation(mod_row[:, tile % 2, :], PS[:, 6 + tile % 2, :], ACT.Copy).then_inc(row_in, 1)
                        act.sem_inc(row_free, 2)
                        for u in range(2):
                            for g in range(8):
                                round_slab(act, None, 8 * u + g + 1)
                                if g % 4 == 3:
                                    t = 2 * u + g // 4
                                    act.wait_ge(x_in[t], 16)
                                    if t:
                                        act.wait_ge(sq, t)
                                    act.activation(junk[:, :], xs[:, t, :], ACT.Square, accum_out=ms[:, t, 0:1]).then_inc(sq, 1)
                            copy_row(None, u)
                        for t in range(4):
                            act.wait_ge(rms_asked, t + 1)
                            act.activation(ms[:, t, 2:3], ms[:, t, 1:2], ACT.Sqrt).then_inc(rms_given, 1)
                        for k in range(0, KT, 2):
                            act.wait_ge(tr, k + 1)
                            act.activation(xT[:, k, :], PS[:, k % 4, :], ACT.Copy).then_inc(tr_out, 1)
                        with loop(act, 3) as q:
                            for u in range(2):
                                for g in range(8):
                                    round_slab(act, q * 16, 16 + 8 * u + g + 1)
                                copy_row(q, 2 + u)
                        with loop(act, 2) as q:
                            for u in range(2):
                                for g in range(8):
                                    round_slab(act, q * 16, 64 + 8 * u + g + 1)
                                    if g % 2:
                                        k = 4 * u + g // 2
                                        act.wait_ge(affine, q * 8 + (k + 1))
                                        act.activation(x_hi[:, q * 8 + k, :], xT[:, q * 8 + k, :], ACT.Copy).then_inc(x_round, 1)
                                copy_row(q, 8 + u)

                    @blk.vector
                    def _(dve):
                        step = chain(dve, "dve0")
                        dve.wait_ge(exp_c, 1)
                        step(dve.tensor_scalar(cex[:, :, :], cex[:, :, :], 1.0, None, ALU.add))
                        step(dve.reciprocal(cex[:, :, :], cex[:, :, :]))
                        step(dve.tensor_tensor(csilu[:, :, :], cin[:, :, :], cex[:, :, :], ALU.mult))
                        dve.tensor_copy(cc[:, :, :, :], csilu[:, :, :, None].broadcast_to([P, KT, 2, 64])).then_inc(silu_c, 1)
                        dve.wait_ge(cc_round, 1)
                        dve.tensor_tensor(cc_lo[:, :, :], cc[:, :, :, :].rearrange("p k w c -> p k (w c)"),
                                          cc_hi[:, :, :].bitcast(F), ALU.subtract).then_inc(cc_split, 1)
                        dve.wait_ge(small, 64)
                        step(dve.tensor_tensor(lamp[:, :, :], lamv[:, 0:4:2, :], lamv[:, 1:4:2, :], ALU.mult))
                        dve.tensor_reduce(lam[:, 0:2], lamp[:, :, :], X, ALU.add).then_inc(lam_asked, 1)
                        dve.wait_ge(lam_given, 1)
                        step(dve.tensor_tensor(lam[:, 4:5], lam[:, 3:4], lam[:, 2:3], ALU.subtract))
                        dve.tensor_scalar(lam[:, 7:8], lam[:, 4:5], -LAMBDA_INIT, None, ALU.add)
                        split_slab(dve, None, 0)
                        mt = modT[:, :].rearrange("p (a w) -> p a w", w=2)

                        def add_bias(reg, tile):
                            n = tile + 1 if reg is None else reg * 2 + (tile + 1)
                            at4 = slice(4 * tile, 4 * tile + 4) if reg is None else ds(reg * 8 + 4 * tile, 4)
                            dve.wait_ge(mod_tr, n)
                            both = PS[:, 4 + tile % 2, :].rearrange("p (a w c) -> p a w c", a=4, w=2)[:, :, :, 0]
                            dve.tensor_tensor(mt[:, at4, :], both, bm[:, at4][:, :, None].broadcast_to([P, 4, 2]), ALU.add)\
                               .then_inc(mod_out, 1)
                        for u in range(2):
                            for g in range(8):
                                split_slab(dve, None, 8 * u + g + 1)
                        for t in range(4):
                            dve.wait_ge(sq, t + 1)
                            dve.tensor_scalar(ms[:, t, 1:2], ms[:, t, 0:1], 1.0 / D, 1e-6, ALU.mult, ALU.add)\
                               .then_inc(rms_asked, 1)
                        for t in range(4):
                            dve.wait_ge(rms_given, t + 1)
                            step(dve.reciprocal(ms[:, t, 3:4], ms[:, t, 2:3]))
                            dve.tensor_scalar(xs[:, t, :], xs[:, t, :], ms[:, t, 3:4], None, ALU.mult).then_inc(normed, 1)
                        for u in range(2):
                            add_bias(None, u)
                        for k in range(1, KT, 2):
                            dve.wait_ge(tr, k + 1)
                            dve.tensor_copy(xT[:, k, :], PS[:, k % 4, :]).then_inc(tr_outv, 1)
                        with loop(dve, 3) as q:
                            for g in range(16):
                                split_slab(dve, q * 16, 16 + g + 1)
                            for u in range(2):
                                add_bias(q, 2 + u)
                        dve.wait_ge(mod_out, 8)
                        dve.wait_ge(tr_out, KT // 2)
                        dve.wait_ge(tr_outv, KT // 2)
                        for w in range(2):
                            i = dve.scalar_tensor_tensor(ab[:, w, :], mt[:, 16:32, w], 1.0, bm[:, 48:48 + KT],
                                                         ALU.add, ALU.mult)
                        step(i)
                        with loop(dve, 2) as q:
                            def lower(k):
                                kk = q * 8 + k
                                dve.wait_ge(x_round, q * 8 + (k + 1))
                                dve.tensor_tensor(x_lo[:, kk, :], xT[:, kk, :], x_hi[:, kk, :].bitcast(F), ALU.subtract)
                            for g in range(16):
                                split_slab(dve, q * 16, 64 + g + 1)
                                if g % 2:
                                    k = g // 2
                                    kk = q * 8 + k
                                    for w in range(2):
                                        part = xT[:, kk, w * T:(w + 1) * T]
                                        i = dve.tensor_scalar(part, part, ab[:, w, ds(kk, 1)], mt[:, kk, w:w + 1],
                                                              ALU.mult, ALU.add)
                                    i.then_inc(affine, 1)
                                    if k:
                                        lower(k - 1)
                            lower(7)
                            for u in range(2):
                                add_bias(q, 8 + u)

                    @blk.tensor
                    def _(pe):
                        pe.sem_inc(multiplied, 4)
                        pe.wait_ge(cc_split, 1)

                        def mod_pair(reg, pair):
                            for u in range(2):
                                tile = 2 * pair + u
                                if pair:
                                    pe.wait_ge(row_in, tile - 1 if reg is None else reg * 2 + (tile - 1))
                                for g in range(8):
                                    m = 8 * tile + g
                                    for k in range(2):
                                        pe.wait_ge(lo_ready, halves(None if reg is None else reg * 16, m) + (k + 1))
                                        c = slice(k * 512, (k + 1) * 512)
                                        kk = 2 * g + k
                                        mm3(pe, PS[:, 6 + u, :], (cc_hi[:, kk, :], cc_lo[:, kk, :]),
                                            (w_hi[m % 2][:, c], w_lo[m % 2][:, c]), kk == 0, kk == KT - 1).then_inc(multiplied, 1)

                        def mod_transposes(reg, pair):
                            for u in range(2):
                                tile = 2 * pair + u
                                pe.wait_ge(row_in, tile + 1 if reg is None else reg * 2 + (tile + 1))
                                if pair:
                                    pe.wait_ge(mod_out, tile - 1 if reg is None else reg * 2 + (tile - 1))
                                for c in range(4):
                                    last = pe.transpose(PS[:, 4 + u, c * P:(c + 1) * P], mod_row[:, u, c * P:(c + 1) * P], ident)
                                last.then_inc(mod_tr, 1)
                                pe.wait_ge(mod_tr, tile + 1 if reg is None else reg * 2 + (tile + 1))
                                pe.sem_inc(row_free, 1)
                        mod_pair(None, 0)
                        pe.wait_ge(small, 64)
                        mod_transposes(None, 0)
                        for k in range(KT):
                            if k >= 4:
                                pe.wait_ge(tr_out if k % 2 == 0 else tr_outv, k // 2 - 1)
                            for t in range(4):
                                if k == 0:
                                    pe.wait_ge(normed, t + 1)
                                last = pe.transpose(PS[:, k % 4, t * P:(t + 1) * P], xs[:, t, k * P:(k + 1) * P], ident)
                            last.then_inc(tr, 1)
                        with loop(pe, 5) as q:
                            mod_pair(q, 1)
                            mod_transposes(q, 1)

            def project(half_name, q_sb, k_sb, v_sb, g_sb, rope, nxt, ph, more_loads):
                n = half_name
                m0 = split_at[n]
                src = src_a if n == "a" else src_b
                acc_free, copied, permuted, perm_free = (sem(f"{x}_{n}") for x in ("acc_free", "copied", "permuted", "perm_free"))
                staged = buf(f"staged_{n}", [P, 2, T], F, ph)
                roped = buf(f"roped_{n}", [P, 2, 2, T], F, ph)
                with stage() as blk:
                    @blk.sync
                    def _(sp):
                        load_slabs(sp, src, base[n], NRAW, N_WIN_A)
                        load_slabs(sp, nxt[0], nxt[1], 0, NRAW)

                    @blk.gpsimd
                    def _(pool):
                        clear_last_stage(pool)
                        more_loads(pool)

                    @blk.scalar
                    def _(act):
                        act.sem_inc(acc_free, 2)
                        for part, dst, width in ((0, q_sb, T), (1, k_sb, 2 * T)):
                            m1 = m0 + 16 * part
                            with loop(act, HEADS, 2) as j:
                                for u in range(2):
                                    round_slab(act, j * 2, m1 + 2 * u + 1)
                                    round_slab(act, j * 2, m1 + 2 * u + 2)
                                    wait_multiplied(act, j * 2, m1 + 2 * u + 2)
                                    if not rope:
                                        act.activation(dst[:, j + u, :], PS[:, u, 0:width], ACT.Copy).then_inc(acc_free, 1)
                                        continue
                                    act.wait_ge(perm_free, j + (8 * part + u + 1))
                                    if part:
                                        act.activation(dst[:, j + u, T:2 * T], PS[:, u, T:2 * T], ACT.Copy)
                                    act.activation(staged[:, u, :], PS[:, u, 0:T], ACT.Copy).then_inc(acc_free, 1)
                        for part, dst, nt in ((2, v_sb, 4), (3, g_sb, 2)):
                            for c in range(2):
                                m1 = m0 + 16 * part + 8 * c
                                for g in range(8):
                                    round_slab(act, None, m1 + g + 1)
                                wait_multiplied(act, None, m1 + 8)
                                for t in range(nt):
                                    i = act.activation(dst[:, t, c * 512:(c + 1) * 512], PS[:, 4 * ((c + 1) % 2) + t, :], ACT.Copy)
                                i.then_inc(copied, 1)

                    @blk.vector
                    def _(dve):
                        if rope:
                            dve.sem_inc(perm_free, 2)
                        step = chain(dve, f"dve_{n}")
                        rotated = sem(f"rotated_{n}")
                        for part, dst in ((0, q_sb), (1, k_sb)):
                            m1 = m0 + 16 * part
                            with loop(dve, HEADS, 2) as j:
                                for s in range(4):
                                    split_slab(dve, j * 2, m1 + s + 1)
                                for u in range(2 if rope else 0):
                                    dve.wait_ge(permuted, j + (8 * part + u + 1))
                                    dve.tensor_tensor(roped[:, u, 0, :], staged[:, u, :], cos_t, ALU.mult)
                                    dve.tensor_tensor(roped[:, u, 1, :], PS[:, 2 + u, 0:T], sin_t, ALU.mult).then_inc(rotated, 1)
                                    dve.wait_ge(rotated, j + (8 * part + u + 1))
                                    dve.tensor_tensor(dst[:, j + u, 0:T], roped[:, u, 0, :], roped[:, u, 1, :], ALU.add)\
                                       .then_inc(perm_free, 1)
                        for g in range(32):
                            split_slab(dve, None, m0 + 32 + g + 1)

                    @blk.tensor
                    def _(pe):
                        for part, cols in ((0, slice(0, T)), (1, slice(0, 2 * T))):
                            m1 = m0 + 16 * part
                            with loop(pe, HEADS, 2) as j:
                                for u in range(2):
                                    pe.wait_ge(acc_free, j + (8 * part + u + 1))
                                    for half in range(2):
                                        feature_slab(pe, PS[:, u, cols], j * 2, m1 + 2 * u + half, half, x_hi, x_lo, cols)
                                for u in range(2 if rope else 0):
                                    pe.wait_ge(acc_free, j + (8 * part + u + 3))
                                    pe.matmul(PS[:, 2 + u, 0:T], perm, staged[:, u, :], start=True, stop=True)\
                                      .then_inc(permuted, 1)
                        for part, nt in ((2, 4), (3, 2)):
                            for c in range(2):
                                m1 = m0 + 16 * part + 8 * c
                                if part == 2 and c == 1:
                                    pe.wait_ge(acc_free, 18)
                                    if rope:
                                        pe.wait_ge(perm_free, 18)
                                if part == 3:
                                    pe.wait_ge(copied, c + 1)
                                b0 = 4 * ((c + 1) % 2)
                                for g in range(8):
                                    token_slab(pe, [PS[:, b0 + t, :] for t in range(nt)], None, m1 + g, g, x_hi, x_lo)

            def attend_a(q_sb, k_sb, v_sb, ph):
                qs = buf("qs_a", [P, 2, T], F, ph)
                ks = buf("ks_a", [P, 2, 2 * T], F, ph)
                pr = [buf(f"pr_a{i}", [P, 2, 512], F, ph) for i in range(2)]
                at_ = buf("at_a", [P, 2, 512], F, ph)
                atT = buf("atT_a", [P, 2, 512], F, ph)
                sm = buf("sm_a", [P, 2, 12], F, ph)
                names = ("head_in", "s_used", "scores", "mx", "nm", "exps", "recips", "recl", "p1s", "attn", "attnT", "attnT_sb",
                         "pv", "o_out")
                head_in, s_used, scores, mx, nm, exps, recips, recl, p1s, attn, attnT, attnT_sb, pv, o_out = (
                    sem("a_" + x) for x in names)
                with stage() as blk:
                    @blk.gpsimd
                    def _(pool):
                        clear_last_stage(pool)
                        pool.sem_inc(s_used, 4)
                        with loop(pool, HEADS, 2) as h:
                            for w in range(2):
                                pool.wait_ge(s_used, h * 2 + (2 * w + 2))
                                pool.tensor_copy(qs[:, w, :], q_sb[:, h + w, :])
                                pool.tensor_copy(ks[:, w, :], k_sb[:, h + w, :]).then_inc(head_in, 1)

                    @blk.tensor
                    def _(pe):
                        with loop(pe, HEADS, 2) as h:
                            def score(e):
                                w, t = e // 2, e % 2
                                if t == 0:
                                    pe.wait_ge(head_in, h + (w + 1))
                                if e >= 2:
                                    pe.wait_ge(exps, h * 4 + (2 * (e - 2) + 2))
                                for i in range(2):
                                    r = slice(64 * i, 64 * i + 64)
                                    last = pe.matmul(PS[:, 2 * t + i, :], qs[r, w, t * P:(t + 1) * P], ks[r, w, :],
                                                     start=True, stop=True)
                                last.then_inc(scores, 1)

                            def values(e):
                                w, t = e // 2, e % 2
                                pe.wait_ge(attn, h * 2 + (e + 1))
                                for c in range(4):
                                    last = pe.transpose(PS[:, 4 + t, c * P:(c + 1) * P], at_[:, t, c * P:(c + 1) * P], ident)
                                last.then_inc(attnT, 1)
                                pe.wait_ge(attnT_sb, h * 2 + (e + 1))
                                if e >= 2:
                                    pe.wait_ge(o_out, h * 2 + (e - 1))
                                for c in range(4):
                                    last = pe.matmul(PS[:, 6 + t, 0:P], atT[:, t, c * P:(c + 1) * P],
                                                     v_sb[:, c, ds(h * P + w * P, P)], start=(c == 0), stop=(c == 3))
                                last.then_inc(pv, 1)

                            score(0)
                            score(1)
                            values(0)
                            score(2)
                            values(1)
                            score(3)
                            values(2)
                            values(3)
                            pe.wait_ge(o_out, h * 2 + 4)
                            pe.sem_inc(s_used, 4)

                    @blk.vector
                    def _(dve):
                        with loop(dve, HEADS, 2) as h:
                            def maxima(e):
                                t = e % 2
                                dve.wait_ge(scores, h * 2 + (e + 1))
                                dve.tensor_reduce(sm[:, t, 0:2], PS[:, 2 * t:2 * t + 2, :], X, ALU.max).then_inc(mx, 1)
                                dve.wait_ge(mx, h * 2 + (e + 1))
                                dve.tensor_scalar(sm[:, t, 2:4], sm[:, t, 0:2], -0.125, None, ALU.mult).then_inc(nm, 1)

                            def weigh(e):
                                t = e % 2
                                dve.wait_ge(exps, h * 4 + (2 * e + 2))
                                dve.reciprocal(sm[:, t, 6:8], sm[:, t, 4:6]).then_inc(recips, 1)
                                dve.wait_ge(recips, h * 2 + (e + 1))
                                dve.tensor_tensor(sm[:, t, 8:9], sm[:, t, 7:8], lam[:, 7:8], ALU.mult).then_inc(recl, 1)
                                dve.wait_ge(recl, h * 2 + (e + 1))
                                dve.tensor_scalar(pr[t][:, 1, :], pr[t][:, 1, :], sm[:, t, 8:9], None, ALU.mult).then_inc(p1s, 1)
                                dve.wait_ge(p1s, h * 2 + (e + 1))
                                dve.scalar_tensor_tensor(at_[:, t, :], pr[t][:, 0, :], sm[:, t, 6:7], pr[t][:, 1, :],
                                                         ALU.mult, ALU.add).then_inc(attn, 1)
                            maxima(0)
                            maxima(1)
                            weigh(0)
                            maxima(2)
                            weigh(1)
                            maxima(3)
                            weigh(2)
                            weigh(3)

                    @blk.scalar
                    def _(act):
                        act.preload_act_table(ACT.Exp)
                        with loop(act, HEADS, 2) as h:
                            def exponentials(e):
                                t = e % 2
                                act.wait_ge(nm, h * 2 + (e + 1))
                                for i in range(2):
                                    act.activation(pr[t][:, i, :], PS[:, 2 * t + i, :], ACT.Exp, bias=sm[:, t, 2 + i:3 + i],
                                                   scale=0.125, accum_out=sm[:, t, 4 + i:5 + i]).then_inc(exps, 1)

                            def copy_t(e):
                                t = e % 2
                                act.wait_ge(attnT, h * 2 + (e + 1))
                                act.activation(atT[:, t, :], PS[:, 4 + t, :], ACT.Copy).then_inc(attnT_sb, 1)

                            def copy_o(e):
                                w, t = e // 2, e % 2
                                act.wait_ge(pv, h * 2 + (e + 1))
                                act.activation(o_a[:, t, ds(h * P + w * P, P)], PS[:, 6 + t, 0:P], ACT.Copy).then_inc(o_out, 1)
                            exponentials(0)
                            exponentials(1)
                            copy_t(0)
                            copy_o(0)
                            exponentials(2)
                            copy_t(1)
                            copy_o(1)
                            exponentials(3)
                            copy_t(2)
                            copy_o(2)
                            copy_t(3)
                            copy_o(3)

            def attend_b(q_sb, k_sb, v_sb, bias, ph):
                qs = buf("qs_b", [P, 2, T], F, ph)
                sc = buf("sc_b", [P, 2, 512], F, ph)
                at_ = buf("at_b", [P, 2, 512], F, ph)
                atT = buf("atT_b", [P, 2, 512], F, ph)
                sm = buf("sm_b", [P, 2, 4], F, ph)
                names = ("head_in", "s_used", "scores", "biased", "mx", "exps", "recips", "attnT", "attnT_sb", "pv", "o_out",
                         "masked")
                head_in, s_used, scores, biased, mx, exps, recips, attnT, attnT_sb, pv, o_out, masked = (
                    sem("b_" + x) for x in names)
                scale = float(P) ** -0.5
                with stage() as blk:
                    @blk.gpsimd
                    def _(pool):
                        clear_last_stage(pool)
                        pool.sem_inc(s_used, 4)
                        m = na_mask[:, None, :].broadcast_to([P, 4, 64])
                        for t in range(TT):
                            for h in range(HEADS):
                                b = bias[:, t, h, :].rearrange("p (r c) -> p r c", c=64)
                                i = pool.tensor_tensor(b, b, m, ALU.add)
                        i.then_inc(masked, 1)
                        with loop(pool, HEADS, 2) as h:
                            for w in range(2):
                                pool.wait_ge(s_used, h * 2 + (2 * w + 2))
                                pool.tensor_copy(qs[:, w, :], q_sb[:, h + w, :]).then_inc(head_in, 1)

                    @blk.tensor
                    def _(pe):
                        with loop(pe, HEADS, 2) as h:
                            def score(e):
                                w, t = e // 2, e % 2
                                if t == 0:
                                    pe.wait_ge(head_in, h + (w + 1))
                                if e >= 2:
                                    pe.wait_ge(biased, h * 2 + (e - 1))
                                pe.matmul(PS[:, t, :], qs[:, w, t * P:(t + 1) * P], k_sb[:, h + w, :],
                                          start=True, stop=True).then_inc(scores, 1)

                            def values(e):
                                w, t = e // 2, e % 2
                                pe.wait_ge(exps, h * 2 + (e + 1))
                                for c in range(4):
                                    last = pe.transpose(PS[:, 4 + t, c * P:(c + 1) * P], at_[:, t, c * P:(c + 1) * P], ident)
                                last.then_inc(attnT, 1)
                                pe.wait_ge(attnT_sb, h * 2 + (e + 1))
                                if e >= 2:
                                    pe.wait_ge(o_out, h * 2 + (e - 1))
                                for c in range(4):
                                    last = pe.matmul(PS[:, 6 + t, 0:P], atT[:, t, c * P:(c + 1) * P],
                                                     v_sb[:, c, ds(h * P + w * P, P)], start=(c == 0), stop=(c == 3))
                                last.then_inc(pv, 1)
                            score(0)
                            score(1)
                            values(0)
                            score(2)
                            values(1)
                            score(3)
                            values(2)
                            values(3)
                            pe.wait_ge(o_out, h * 2 + 4)
                            pe.sem_inc(s_used, 4)

                    @blk.vector
                    def _(dve):
                        dve.wait_ge(masked, 1)
                        with loop(dve, HEADS, 2) as h:
                            def add_bias(e):
                                w, t = e // 2, e % 2
                                dve.wait_ge(scores, h * 2 + (e + 1))
                                dve.scalar_tensor_tensor(sc[:, t, 0:T], PS[:, t, 0:T], scale, bias[:, t, h + w, :],
                                                         ALU.mult, ALU.add)
                                dve.tensor_scalar(sc[:, t, T:2 * T], PS[:, t, T:2 * T], scale, None, ALU.mult).then_inc(biased, 1)
                                dve.wait_ge(biased, h * 2 + (e + 1))
                                dve.tensor_reduce(sm[:, t, 0:1], sc[:, t, :], X, ALU.max, negate=True).then_inc(mx, 1)

                            def recip(e):
                                t = e % 2
                                dve.wait_ge(exps, h * 2 + (e + 1))
                                dve.reciprocal(sm[:, t, 2:3], sm[:, t, 1:2]).then_inc(recips, 1)
                            add_bias(0)
                            add_bias(1)
                            recip(0)
                            dve.wait_ge(exps, h * 2 + 1)
                            add_bias(2)
                            recip(1)
                            add_bias(3)
                            recip(2)
                            recip(3)

                    @blk.scalar
                    def _(act):
                        act.preload_act_table(ACT.Exp)
                        with loop(act, HEADS, 2) as h:
                            def exponential(e):
                                t = e % 2
                                act.wait_ge(mx, h * 2 + (e + 1))
                                act.activation(at_[:, t, :], sc[:, t, :], ACT.Exp, bias=sm[:, t, 0:1],
                                               accum_out=sm[:, t, 1:2]).then_inc(exps, 1)

                            def copy_t(e):
                                t = e % 2
                                act.wait_ge(attnT, h * 2 + (e + 1))
                                act.activation(atT[:, t, :], PS[:, 4 + t, :], ACT.Copy).then_inc(attnT_sb, 1)

                            def copy_o(e):
                                w, t = e // 2, e % 2
                                act.wait_ge(pv, h * 2 + (e + 1))
                                act.wait_ge(recips, h * 2 + (e + 1))
                                act.activation(o_b[:, t, ds(h * P + w * P, P)], PS[:, 6 + t, 0:P], ACT.Copy,
                                               scale=sm[:, t, 2:3]).then_inc(o_out, 1)
                            exponential(0)
                            exponential(1)
                            copy_t(0)
                            copy_o(0)
                            exponential(2)
                            copy_t(1)
                            copy_o(1)
                            exponential(3)
                            copy_t(2)
                            copy_o(2)
                            copy_t(3)
                            copy_o(3)

            def gate(g_sb, o_sb, norm, ph, n):
                ex = buf(f"ex_{n}", [P, TT, WA], F, ph)
                one, two, ssq, asked, given = (sem(f"{x}_{n}") for x in ("g_exp", "g_silu", "g_ssq", "g_asked", "g_given"))
                if norm:
                    ss = buf("ss", [P, 3, TT * HEADS], F, ph)
                    sub_g = buf("sub_g", [P, P], F, ph)
                    loaded = sem("sub_g_in")
                with stage() as blk:
                    @blk.gpsimd
                    def _(pool):
                        clear_last_stage(pool)
                        if norm:
                            pool.dma_start(sub_g[:, :], bcast(io["subln_g"])).then_inc(loaded, 16)

                    @blk.scalar
                    def _(act):
                        act.activation(ex[:, :, :], g_sb[:, :, :], ACT.Exp, scale=-1.0).then_inc(one, 1)
                        if norm:
                            act.wait_ge(asked, 1)
                            act.activation(ss[:, 2, :], ss[:, 1, :], ACT.Sqrt).then_inc(given, 1)

                    @blk.vector
                    def _(dve):
                        step = chain(dve, f"dve_gate_{n}")
                        if norm:
                            sq = buf("sq_o", [P, TT, WA], F, ph)
                            step(dve.tensor_tensor(sq[:, :, :], o_sb[:, :, :], o_sb[:, :, :], ALU.mult))
                            step(dve.tensor_reduce(ss[:, 0, :], sq[:, :, :].rearrange("p t (h c) -> p (t h) c", c=P), X, ALU.add))
                            dve.tensor_scalar(ss[:, 1, :], ss[:, 0, :], 1.0 / P, 1e-5, ALU.mult, ALU.add).then_inc(asked, 1)
                        dve.wait_ge(one, 1)
                        step(dve.tensor_scalar(ex[:, :, :], ex[:, :, :], 1.0, None, ALU.add))
                        step(dve.reciprocal(ex[:, :, :], ex[:, :, :]))
                        step(dve.tensor_tensor(ex[:, :, :], ex[:, :, :], g_sb[:, :, :], ALU.mult))
                        if norm:
                            dve.wait_ge(given, 1)
                            dve.wait_ge(loaded, 16)
                            step(dve.reciprocal(ss[:, 0, :], ss[:, 2, :]))
                            o3 = o_sb[:, :, :].rearrange("p t (h c) -> p (t h) c", c=P)
                            step(dve.tensor_tensor(o3, o3, ss[:, 0, :, None].broadcast_to([P, TT * HEADS, P]), ALU.mult))
                            step(dve.scalar_tensor_tensor(o3, o3, 1.0 - LAMBDA_INIT,
                                                          sub_g[:, None, :].broadcast_to([P, TT * HEADS, P]), ALU.mult, ALU.mult))
                        dve.tensor_tensor(o_sb[:, :, :], o_sb[:, :, :], ex[:, :, :], ALU.mult)

            for n in ("a", "b"):
                with ExitStack() as ph:
                    q_sb = buf(f"q_{n}", [P, HEADS, T], F, ph)
                    k_sb = buf(f"k_{n}", [P, HEADS, 2 * T], F, ph)
                    v_sb = buf(f"v_{n}", [P, 4, WA], F, ph)
                    g_sb = buf(f"g_{n}", [P, TT, WA], F, ph)
                    bias = None
                    if n == "b":
                        bias = buf("bias", [P, TT, HEADS, T], F, ph)
                        bias_in = sem("bias_in")

                    def more_loads(pool):
                        if n == "b":
                            for t in range(TT):
                                for r2 in range(2):
                                    r = 2 * t + r2
                                    pool.dma_start(bias[64 * r2:64 * r2 + 64, t, :, :],
                                                   io["rpb_e"][:, :, (7 - r) * 64:(11 - r) * 64].rearrange("h j c -> j h c"))\
                                        .then_inc(bias_in, 16)
                            pool.wait_ge(bias_in, 64)
                    nxt = (src_b, base["b"]) if n == "a" else (src_out, base["out"])
                    with ExitStack() as ph2:
                        project(n, q_sb, k_sb, v_sb, g_sb, n == "a", nxt, ph2, more_loads)
                    with ExitStack() as ph2:
                        if n == "a":
                            attend_a(q_sb, k_sb, v_sb, ph2)
                        else:
                            attend_b(q_sb, k_sb, v_sb, bias, ph2)
                    with ExitStack() as ph2:
                        gate(g_sb, o_a if n == "a" else o_b, n == "a", ph2, n)
            late.close()
            with ExitStack() as ph:
                oc_hi = buf("oc_hi", [P, KT, T], R, ph)
                oc_lo = buf("oc_lo", [P, KT, T], R, ph)
                gate_b = buf("gate_b", [P, D], F, ph)
                par = [buf(f"par{i}", [P, D], F, ph) for i in range(3)]
                diag = buf("diag", [P, 2, P], F, ph)
                tmp = buf("tmp1", [P, TT, 512], F, ph)
                junk = buf("junk1", [P, D], F, ph)
                tr, rnd, cp, diag_made, gate_mm, gate_out, xin, gated, resid, squared, asked, given, prod = (
                    sem(x + "_1") for x in ("tr", "rnd", "cp", "diag_made", "gate_mm", "gate_out", "xin", "gated", "resid",
                                            "squared", "asked", "given", "prod"))
                m0 = split_at["out"]
                with stage() as blk:
                    @blk.sync
                    def _(sp):
                        load_slabs(sp, src_out, base["out"], NRAW, N_OUT)
                        load_slabs(sp, src_in2, base["in2"], 0, NRAW)

                    @blk.gpsimd
                    def _(pool):
                        clear_last_stage(pool)
                        pool.dma_start(h_buf[:, :, :], x_tok).then_inc(xin, 16)
                        for i, name in enumerate(("final_g", "ln_in_g", "ln_in_b")):
                            pool.dma_start(par[i][:, :], bcast(io[name])).then_inc(xin, 16)

                    @blk.tensor
                    def _(pe):
                        both = [o_a, o_b]
                        for b in range(KT // 2):
                            if b >= 2:
                                pe.wait_ge(cp, b - 1)
                            for k in range(2):
                                for t in range(TT):
                                    kk = 2 * b + k
                                    src = both[kk // 8][:, t, (kk % 8) * P:(kk % 8 + 1) * P]
                                    last = pe.transpose(PS[:, b % 2, (2 * k + t) * P:(2 * k + t + 1) * P], src, ident)
                            last.then_inc(tr, 1)
                        for b in range(KT):
                            pe.wait_ge(diag_made, b + 1)
                            if b % 4 == 0 and b >= 8:
                                pe.wait_ge(gate_out, b // 4 - 1)
                            pe.matmul(PS[:, 2 + (b // 4) % 2, (b % 4) * P:(b % 4 + 1) * P],
                                      cst[:, C_ONES:C_ONES + P], diag[:, b % 2, :], start=True, stop=True).then_inc(gate_mm, 1)
                        pe.wait_ge(cp, 8)
                        with loop(pe, 4, 2) as c:
                            for u in range(2):
                                pe.wait_ge(gated, c + (u + 1))
                                for g in range(8):
                                    token_slab(pe, [PS[:, 4 + 2 * u + t, :] for t in range(TT)], c * 8, m0 + 8 * u + g, g,
                                               oc_hi, oc_lo)

                    @blk.scalar
                    def _(act):
                        for b in range(KT // 2):
                            act.wait_ge(tr, b + 1)
                            act.activation(oc_hi[:, 2 * b:2 * b + 2, :], PS[:, b % 2, :].rearrange("p (k t) -> p k t", k=2),
                                           ACT.Copy).then_inc(rnd, 1)
                        for q in range(4):
                            act.wait_ge(gate_mm, 4 * q + 4)
                            act.activation(gate_b[:, q * 512:(q + 1) * 512], PS[:, 2 + q % 2, :], ACT.Copy).then_inc(gate_out, 1)
                        with loop(act, N_OUT, NRAW) as i:
                            for s in range(NRAW):
                                round_slab(act, i, m0 + s + 1)
                        for t in range(TT):
                            act.wait_ge(resid, 4)
                            if t:
                                act.wait_ge(squared, t)
                            act.activation(junk[:, :], h_buf[:, t, :], ACT.Square, accum_out=mv[:, t, 5:6]).then_inc(squared, 1)
                        for n in range(2 * TT):
                            t = n % TT
                            act.wait_ge(asked, n + 1)
                            act.activation(mv[:, t, 3:4], mv[:, t, 2:3], ACT.Sqrt).then_inc(given, 1)

                    @blk.vector
                    def _(dve):
                        step = chain(dve, "dve_out1")
                        for b in range(KT // 2):
                            dve.wait_ge(rnd, b + 1)
                            s = slice(2 * b, 2 * b + 2)
                            dve.tensor_tensor(oc_lo[:, s, :], PS[:, b % 2, :].rearrange("p (k t) -> p k t", k=2),
                                              oc_hi[:, s, :].bitcast(F), ALU.subtract).then_inc(cp, 1)
                        mt = modT[:, :].rearrange("p (a w) -> p a w", w=2)
                        for b in range(KT):
                            if b >= 2:
                                dve.wait_ge(gate_mm, b - 1)
                            dve.tensor_scalar(diag[:, b % 2, :], ident, mt[:, 32 + b, 0:1], None, ALU.mult).then_inc(diag_made, 1)
                        dve.sem_inc(gated, 2)
                        dve.wait_ge(gate_out, 4)
                        dve.wait_ge(xin, 64)
                        with loop(dve, 4, 2) as c:
                            for u in range(2):
                                for g in range(8):
                                    split_slab(dve, c * 8, m0 + 8 * u + g + 1)
                                wait_multiplied(dve, c * 8, m0 + 8 * u + 8)
                                for t in range(TT):
                                    i = dve.tensor_tensor(tmp[:, t, :], PS[:, 4 + 2 * u + t, :],
                                                          gate_b[:, ds(c * 512 + u * 512, 512)], ALU.mult)
                                i.then_inc(gated, 1)
                                dve.wait_ge(gated, c + (u + 3))
                                for t in range(TT):
                                    hh = h_buf[:, t, ds(c * 512 + u * 512, 512)]
                                    i = dve.tensor_tensor(hh, hh, tmp[:, t, :], ALU.add)
                                i.then_inc(resid, 1)
                                dve.wait_ge(resid, c + (u + 1))
                        for t in range(TT):
                            dve.wait_ge(squared, t + 1)
                            dve.tensor_scalar(mv[:, t, 2:3], mv[:, t, 5:6], 1.0 / D, 1e-6, ALU.mult, ALU.add).then_inc(asked, 1)
                        for t in range(TT):
                            dve.wait_ge(given, t + 1)
                            step(dve.reciprocal(mv[:, t, 4:5], mv[:, t, 3:4]))
                            step(dve.scalar_tensor_tensor(h_buf[:, t, :], h_buf[:, t, :], mv[:, t, 4:5], par[0][:, :],
                                                          ALU.mult, ALU.mult))
                            norm_stats(dve, step, h_buf, t, asked)
                        for t in range(TT):
                            norm_apply(dve, step, h_buf, t, given, TT, par[1], par[2])

        second = ExitStack()
        ctx.enter_context(second)

        def buf2(name, shape, dt=F, where=second):
            return where.enter_context(nc.sbuf_tensor(name, shape, dt))

        mix_hi = buf2("mix_hi", [P, KT, T], R)
        mix_lo = buf2("mix_lo", [P, KT, T], R)
        cell = second.enter_context(ExitStack())
        q2 = buf2("q2", [P, HEADS, T], F, cell)
        k2 = buf2("k2", [P, HEADS, T], F, cell)
        v2 = buf2("v2", [P, TT, HEADS, P + 1], F, cell)
        o2 = buf2("o2", [P, TT, WA], F, cell)
        gates = buf2("gates", [P, TT, 16], F, cell)
        with ExitStack() as ph:
            h_hi = buf2("h_hi", [P, KT, T], R, ph)
            h_lo = buf2("h_lo", [P, KT, T], R, ph)
            wg = buf2("wg", [P, KT, 16], F, ph)
            wg_hi = buf2("wg_hi", [P, KT, 16], R, ph)
            wg_lo = buf2("wg_lo", [P, KT, 16], R, ph)
            bg = buf2("bg", [P, 16], F, ph)
            cv = buf2("cv", [P, 4, HEADS], F, ph)
            c_sb = buf2("c_sb", [P, 2, T], F, ph)
            z = buf2("z", [P, 2, T + 2], F, ph)
            yc = buf2("yc", [P, 2, 2, T], F, ph)
            tr, rnd, cp, par_in, wg_round, wg_split, gates_done, zeroed, c_copied, conv, conv_free, acc_free, vo_free = (
                sem(x + "_2") for x in ("tr", "rnd", "cp", "par_in", "wg_round", "wg_split", "gates_done", "zeroed", "c_copied",
                                        "conv", "conv_free", "acc_free", "vo_free"))
            m0 = split_at["in2"]
            with stage() as blk:
                @blk.sync
                def _(sp):
                    load_slabs(sp, src_in2, base["in2"], NRAW, N_WIN2)
                    load_slabs(sp, src_out2, base["out2"], 0, NRAW)

                @blk.gpsimd
                def _(pool):
                    clear_last_stage(pool)
                    pool.dma_start(cv[:, :, :].rearrange("p a b -> p (a b)"), io["conv_cols"]).then_inc(par_in, 16)
                    pool.dma_start(wg[:, :, :].rearrange("p a b -> p (a b)"), io["w_gate_cols"]).then_inc(par_in, 16)
                    pool.dma_start(bg[:, :], bcast(io["b_gate"])).then_inc(par_in, 16)
                    pool.memset(z[:, :, 0:2], 0.0)
                    pool.memset(v2[:, :, :, P:P + 1], 1.0).then_inc(zeroed, 1)

                @blk.tensor
                def _(pe):
                    transpose_in(pe, h_buf, None, cp, tr, banks=(6, 7))
                    pe.wait_ge(cp, 8)
                    with loop(pe, HEADS, 2) as j:
                        for u in range(2):
                            pe.wait_ge(conv_free, j * 3 + (3 * u + 3))
                            for part in range(3):
                                for half in range(2):
                                    feature_slab(pe, PS[:, 3 * u + part, 0:T], j * 6, m0 + 6 * u + 2 * part + half, half,
                                                 h_hi, h_lo, slice(0, T))
                    with loop(pe, 2 * HEADS, 2) as j:
                        for u in range(2):
                            pe.wait_ge(acc_free, j + (u + 1))
                            for half in range(2):
                                feature_slab(pe, PS[:, 6 + u, 0:T], j * 2, m0 + 48 + 2 * u + half, half, h_hi, h_lo, slice(0, T))
                    pe.wait_ge(acc_free, 2 * HEADS + 1)
                    pe.wait_ge(wg_split, 1)
                    for t in range(TT):
                        tok = slice(t * P, (t + 1) * P)
                        for k in range(KT):
                            last = mm3(pe, PS[:, 6, t * 16:t * 16 + 16], (h_hi[:, k, tok], h_lo[:, k, tok]),
                                       (wg_hi[:, k, :], wg_lo[:, k, :]), k == 0, k == KT - 1)
                    last.then_inc(gates_done, 1)
                    pe.wait_ge(conv_free, 6 + 3 * HEADS)
                    for c in range(4):
                        if c >= 2:
                            pe.wait_ge(vo_free, c - 1)
                        for g in range(8):
                            token_slab(pe, [PS[:, 2 * (c % 2) + t, :] for t in range(TT)], None, m0 + 80 + 8 * c + g, g, h_hi, h_lo)

                @blk.scalar
                def _(act):
                    transposed_round(act, tr, h_hi, rnd, banks=(6, 7))
                    act.sem_inc(acc_free, 2)
                    act.wait_ge(par_in, 48)
                    act.activation(wg_hi[:, :, :], wg[:, :, :], ACT.Copy).then_inc(wg_round, 1)
                    with loop(act, HEADS, 2) as j:
                        for u in range(2):
                            for s in range(6):
                                round_slab(act, j * 6, m0 + 6 * u + s + 1)
                            wait_multiplied(act, j * 6, m0 + 6 * u + 4)
                            act.wait_ge(conv_free, j * 3 + (3 * u + 3))
                            act.activation(c_sb[:, u, :], PS[:, 3 * u + 1, 0:T], ACT.Copy).then_inc(c_copied, 1)
                    for part, dst in ((0, q2), (1, k2)):
                        with loop(act, HEADS, 2) as j:
                            for u in range(2):
                                for s in range(2):
                                    round_slab(act, j * 2, m0 + 48 + 16 * part + 2 * u + s + 1)
                                wait_multiplied(act, j * 2, m0 + 48 + 16 * part + 2 * u + 2)
                                act.activation(dst[:, j + u, :], PS[:, 6 + u, 0:T], ACT.Copy).then_inc(acc_free, 1)
                    for c in range(4):
                        m1 = m0 + 80 + 8 * c
                        for g in range(8):
                            round_slab(act, None, m1 + g + 1)
                        wait_multiplied(act, None, m1 + 8)
                        if c < 2:
                            act.wait_ge(zeroed, 1)
                        for t in range(TT):
                            if c < 2:
                                i = act.activation(v2[:, t, 4 * c:4 * c + 4, 0:P],
                                                   PS[:, 2 * (c % 2) + t, :].rearrange("p (h e) -> p h e", h=4), ACT.Copy)
                            else:
                                i = act.activation(o2[:, t, (c - 2) * 512:(c - 1) * 512], PS[:, 2 * (c % 2) + t, :], ACT.Copy)
                        i.then_inc(vo_free, 1)

                @blk.vector
                def _(dve):
                    step = chain(dve, "dve_in2")
                    transposed_split(dve, h_hi, h_lo, rnd, cp, banks=(6, 7))
                    dve.wait_ge(wg_round, 1)
                    dve.tensor_tensor(wg_lo[:, :, :], wg[:, :, :], wg_hi[:, :, :].bitcast(F), ALU.subtract).then_inc(wg_split, 1)
                    dve.sem_inc(conv_free, 6)
                    dve.wait_ge(zeroed, 1)
                    with loop(dve, HEADS, 2) as j:
                        for u in range(2):
                            for s in range(6):
                                split_slab(dve, j * 6, m0 + 6 * u + s + 1)
                            dve.wait_ge(c_copied, j + (u + 1))
                            wait_multiplied(dve, j * 6, m0 + 6 * u + 6)
                            y = yc[:, u, 0, :]

                            def tap(n):
                                return cv[:, n, ds(j + u, 1)]
                            n = 6 * u
                            dve.tensor_tensor(z[:, u, 2:T + 2], c_sb[:, u, :], PS[:, 3 * u + 2, 0:T], ALU.mult).then_inc(conv, 1)
                            dve.wait_ge(conv, j * 6 + (n + 1))
                            dve.tensor_scalar(y, z[:, u, 2:T + 2], tap(2), tap(3), ALU.mult, ALU.add).then_inc(conv, 1)
                            dve.wait_ge(conv, j * 6 + (n + 2))
                            dve.scalar_tensor_tensor(y, z[:, u, 1:T + 1], tap(1), y, ALU.mult, ALU.add).then_inc(conv, 1)
                            dve.wait_ge(conv, j * 6 + (n + 3))
                            dve.scalar_tensor_tensor(y, z[:, u, 0:T], tap(0), y, ALU.mult, ALU.add).then_inc(conv, 1)
                            dve.wait_ge(conv, j * 6 + (n + 4))
                            dve.tensor_tensor(yc[:, u, 1, :], y, PS[:, 3 * u, 0:T], ALU.mult).then_inc(conv, 1)
                            dve.wait_ge(conv, j * 6 + (n + 5))
                            dve.tensor_copy(mix_hi[:, j + u, :], yc[:, u, 1, :]).then_inc(conv, 1)
                            dve.wait_ge(conv, j * 6 + (n + 6))
                            dve.tensor_tensor(mix_lo[:, j + u, :], yc[:, u, 1, :], mix_hi[:, j + u, :].bitcast(F), ALU.subtract)\
                               .then_inc(conv_free, 3)
                    with loop(dve, 32, NRAW) as i:
                        for s in range(NRAW):
                            split_slab(dve, i, m0 + 48 + s + 1)
                    dve.wait_ge(gates_done, 1)
                    for t in range(TT):
                        dve.tensor_tensor(gates[:, t, :], PS[:, 6, t * 16:t * 16 + 16], bg[:, :], ALU.add)
                    with loop(dve, 32, NRAW) as i:
                        for s in range(NRAW):
                            split_slab(dve, i, m0 + 80 + s + 1)

        with ExitStack() as ph:
            lg = buf2("lg", [P, TT, 5, HEADS], F, ph)
            row = buf2("row", [HEADS, 8, T], F, ph)
            neg = buf2("neg", [HEADS, HEADS, T], F, ph)
            colb = buf2("colb", [P, TT, 2, HEADS], F, ph)
            qk = buf2("qk", [P, 2, 2, T], F, ph)
            ee = buf2("ee", [P, 2, 3, P], F, ph)
            ss = buf2("ss2", [P, 2, 3, P], F, ph)
            num = buf2("num", [P, 2, TT, P + 1], F, ph)
            den = buf2("den", [P, 2, 3, TT], F, ph)
            hm = buf2("hm", [P, TT, HEADS, P], F, ph)
            eye8 = buf2("eye8", [HEADS, HEADS], F, ph)
            mh_g = buf2("mh_g", [P, WA], F, ph)
            st = buf2("st", [P, TT, HEADS, 6], F, ph)
            hv = buf2("hv", [P, TT * HEADS, 6], F, ph)
            ex = buf2("ex2", [P, TT, WA], F, ph)
            (g_abs, g_exp, g_ln, g_dve, g_tr, g_rows, g_b, g_em, g_trb, g_col, par_in, head_in, s_used, scores, tri, exps, wts, nums,
             num_sb, dens, hms, o_exp, asked, given, ymr, tr, rnd, cp, neg_made) = (
                sem(x + "_3") for x in ("g_abs", "g_exp", "g_ln", "g_dve", "g_tr", "g_rows", "g_b", "g_em", "g_trb", "g_col",
                                        "par_in", "head_in", "s_used", "scores", "tri", "exps", "wts", "nums", "num_sb", "dens",
                                        "hms", "o_exp", "asked", "given", "ymr", "tr", "rnd", "cp", "neg_made"))
            scale = float(P) ** -0.5
            with stage() as blk:
                @blk.gpsimd
                def _(pool):
                    clear_last_stage(pool)
                    pool.dma_start(eye8[:, :], io["consts"][0:HEADS, C_EYE8:C_EYE8 + HEADS]).then_inc(par_in, 16)
                    pool.dma_start(mh_g[:, :], bcast(io["mh_g"])).then_inc(par_in, 16)
                    pool.sem_inc(s_used, 2)
                    with loop(pool, HEADS, 2) as h:
                        for w in range(2):
                            pool.wait_ge(s_used, h + (w + 1))
                            pool.tensor_copy(qk[:, w, 0, :], q2[:, h + w, :])
                            pool.tensor_copy(qk[:, w, 1, :], k2[:, h + w, :]).then_inc(head_in, 1)

                @blk.scalar
                def _(act):
                    act.preload_act_table_set("natural_log_exp_and_others")
                    act.activation(ex[:, :, :], o2[:, :, :], ACT.Exp, scale=-1.0).then_inc(o_exp, 1)
                    act.wait_ge(g_abs, 1)
                    act.activation(lg[:, :, 2, :], lg[:, :, 1, :], ACT.Exp).then_inc(g_exp, 1)
                    act.wait_ge(g_exp, 1)
                    act.activation(lg[:, :, 3, :], lg[:, :, 2, :], ACT.Ln, bias=cst[:, C_ONES:C_ONES + 1]).then_inc(g_ln, 1)
                    act.wait_ge(g_tr, 1)
                    act.activation(row[:, 0:2, :], PS[0:HEADS, 7, :].rearrange("p (a t) -> p a t", a=2), ACT.Copy).then_inc(g_rows, 1)
                    act.wait_ge(g_b, 1)
                    act.activation(row[:, 6, :], row[:, 6, :], ACT.Exp, scale=-1.0).then_inc(g_em, 1)
                    act.wait_ge(g_trb, 1)
                    act.activation(colb[:, :, :, :].rearrange("p t a h -> p (t a h)"), PS[:, 7, 0:32], ACT.Copy).then_inc(g_col, 1)
                    act.wait_ge(g_col, 1)
                    with loop(act, HEADS, 2) as h:
                        for w in range(2):
                            act.wait_ge(tri, h + (w + 1))
                            a0, a1 = colb[:, 0, 0, ds(h + w, 1)], colb[:, 1, 0, ds(h + w, 1)]
                            act.activation(ee[:, w, 0, :], ee[:, w, 0, :], ACT.Exp, bias=a0)
                            act.activation(ee[:, w, 1, :], PS[:, 2 + w, P:T], ACT.Exp, bias=a0)
                            act.activation(ee[:, w, 2, :], ee[:, w, 2, :], ACT.Exp, bias=a1).then_inc(exps, 1)
                            act.wait_ge(nums, h + (w + 1))
                            act.activation(num[:, w, :, :], PS[:, 4 + w, 0:2 * (P + 1)].rearrange("p (t e) -> p t e", t=2),
                                           ACT.Copy).then_inc(num_sb, 1)
                    act.wait_ge(asked, 1)
                    act.activation(hv[:, :, 3], hv[:, :, 2], ACT.Sqrt).then_inc(given, 1)
                    for b in range(4):
                        act.wait_ge(tr, b + 1)
                        act.activation(mix_hi[:, 8 + 2 * b:10 + 2 * b, :], PS[:, b % 2, :].rearrange("p (k t) -> p k t", k=2),
                                       ACT.Copy).then_inc(rnd, 1)

                @blk.tensor
                def _(pe):
                    pe.wait_ge(g_dve, 1)
                    for a in range(2):
                        for t in range(TT):
                            last = pe.transpose(PS[0:HEADS, 7, a * T + t * P:a * T + (t + 1) * P], lg[:, t, 4 * a, :], ident)
                    last.then_inc(g_tr, 1)
                    pe.wait_ge(g_em, 1)
                    pe.wait_ge(par_in, 32)
                    for t in range(TT):
                        for a, r in ((0, 3), (1, 6)):
                            last = pe.transpose(PS[:, 7, (2 * t + a) * HEADS:(2 * t + a + 1) * HEADS],
                                                row[:, r, t * P:(t + 1) * P], eye8[:, :])
                    last.then_inc(g_trb, 1)
                    pe.wait_ge(g_col, 1)
                    pe.wait_ge(neg_made, 1)

                    def values(h, w):
                        pe.wait_ge(wts, h + (w + 1))
                        if True:
                            pe.wait_ge(s_used, h + (w + 1))
                        v0, v1 = v2[:, 0, h + w, :], v2[:, 1, h + w, :]
                        pe.matmul(PS[:, 4 + w, 0:P + 1], ss[:, w, 0, :], v0, start=True, stop=True)
                        pe.matmul(PS[:, 4 + w, P + 1:2 * P + 2], ss[:, w, 1, :], v0, start=True, stop=False)
                        pe.matmul(PS[:, 4 + w, P + 1:2 * P + 2], ss[:, w, 2, :], v1, start=False, stop=True).then_inc(nums, 1)
                    with loop(pe, HEADS, 2) as h:
                        for w in range(2):
                            pe.wait_ge(head_in, h + (w + 1))
                            q, k = qk[:, w, 0, :], qk[:, w, 1, :]
                            pe.matmul(PS[:, w, 0:T], k[:, 0:P], q, start=True, stop=True)
                            pe.matmul(PS[:, w, T:T + P], k[:, P:T], q[:, P:T], start=True, stop=True)
                            pe.matmul(PS[:, 2 + w, 0:T], cst[0:HEADS, C_ONES:C_ONES + P], neg[:, h + w, :],
                                      start=True, stop=True).then_inc(scores, 1)
                        for w in range(2):
                            values(h, w)
                    for b in range(4):
                        pe.wait_ge(ymr, 1)
                        if b >= 2:
                            pe.wait_ge(cp, b - 1)
                        for k in range(2):
                            for t in range(TT):
                                last = pe.transpose(PS[:, b % 2, (2 * k + t) * P:(2 * k + t + 1) * P],
                                                    hm[:, t, 2 * b + k, :], ident)
                        last.then_inc(tr, 1)

                @blk.vector
                def _(dve):
                    step = chain(dve, "dve_cell")
                    gi, gf = gates[:, :, 0:HEADS], gates[:, :, HEADS:16]
                    step(dve.tensor_scalar(lg[:, :, 1, :], gf, -1.0, None, ALU.mult))
                    step(dve.tensor_tensor(lg[:, :, 1, :], lg[:, :, 1, :], gf, ALU.min))
                    dve.tensor_copy(lg[:, :, 0, :], gi).then_inc(g_abs, 1)
                    dve.wait_ge(g_ln, 1)
                    step(dve.tensor_scalar(lg[:, :, 4, :], gf, 0.0, None, ALU.min))
                    dve.tensor_tensor(lg[:, :, 4, :], lg[:, :, 4, :], lg[:, :, 3, :], ALU.subtract).then_inc(g_dve, 1)
                    step(dve.memset(row[:, 7, :], 1.0))
                    dve.wait_ge(g_rows, 1)
                    one = row[:, 7, :]
                    step(dve.tensor_tensor_scan(row[:, 2, :], one, row[:, 1, :], 0.0, ALU.mult, ALU.add))
                    step(dve.tensor_tensor(row[:, 3, :], row[:, 0, :], row[:, 2, :], ALU.subtract))
                    step(dve.tensor_tensor_scan(row[:, 4, :], one, row[:, 3, :], 0.0, ALU.mult, ALU.max))
                    step(dve.tensor_scalar(row[:, 5, :], row[:, 4, :], -1.0, None, ALU.mult))
                    dve.tensor_tensor(row[:, 6, :], row[:, 4, :], row[:, 2, :], ALU.add).then_inc(g_b, 1)
                    dve.wait_ge(par_in, 32)
                    for h in range(HEADS):
                        i = dve.tensor_scalar(neg[:, h, :], row[:, 5, :], eye8[:, h:h + 1], None, ALU.mult)
                    i.then_inc(neg_made, 1)
                    dve.wait_ge(g_col, 1)
                    tri_m = cst[:, C_TRI:C_TRI + P]
                    with loop(dve, HEADS, 2) as h:
                        for w in range(2):
                            dve.wait_ge(scores, h + (w + 1))
                            dve.tensor_tensor(ee[:, w, 0, :], PS[:, 2 + w, 0:P], tri_m, ALU.add)
                            dve.tensor_tensor(ee[:, w, 2, :], PS[:, 2 + w, P:T], tri_m, ALU.add).then_inc(tri, 1)
                        for w in range(2):
                            dve.wait_ge(exps, h + (w + 1))
                            dve.scalar_tensor_tensor(ss[:, w, :, :].rearrange("p b t -> p (b t)"), PS[:, w, 0:3 * P], scale,
                                                     ee[:, w, :, :].rearrange("p b t -> p (b t)"), ALU.mult, ALU.mult).then_inc(wts, 1)
                        for w in range(2):
                            dve.wait_ge(num_sb, h + (w + 1))
                            d = num[:, w, :, P]
                            dve.scalar_tensor_tensor(den[:, w, 0, :], d, -1.0, d, ALU.mult, ALU.max).then_inc(dens, 1)
                            dve.wait_ge(dens, h * 3 + (3 * w + 1))
                            dve.tensor_tensor(den[:, w, 1, :], den[:, w, 0, :], colb[:, :, 1, ds(h + w, 1)].rearrange("p t o -> p (t o)"),
                                              ALU.max).then_inc(dens, 1)
                            dve.wait_ge(dens, h * 3 + (3 * w + 2))
                            dve.reciprocal(den[:, w, 2, :], den[:, w, 1, :]).then_inc(dens, 1)
                            dve.wait_ge(dens, h * 3 + (3 * w + 3))
                            for t in range(TT):
                                i = dve.tensor_scalar(hm[:, t, h + w, :], num[:, w, t, 0:P], den[:, w, 2, t:t + 1], None, ALU.mult)
                            i.then_inc(hms, 1)
                            dve.wait_ge(hms, h + (w + 1))
                            dve.sem_inc(s_used, 1)
                    for t in range(TT):
                        for h in range(HEADS):
                            i = dve.bn_stats(st[:, t, h, :], hm[:, t, h, :])
                    step(i)
                    for n in range(TT * HEADS):
                        i = dve.bn_aggr(hv[:, n, 0:2], st[:, n // HEADS, n % HEADS, :])
                    step(i)
                    dve.tensor_scalar(hv[:, :, 2], hv[:, :, 1], 1e-5, None, ALU.add).then_inc(asked, 1)
                    dve.wait_ge(o_exp, 1)
                    step(dve.tensor_scalar(ex[:, :, :], ex[:, :, :], 1.0, None, ALU.add))
                    step(dve.reciprocal(ex[:, :, :], ex[:, :, :]))
                    step(dve.tensor_tensor(ex[:, :, :], ex[:, :, :], mh_g[:, None, :].broadcast_to([P, TT, WA]), ALU.mult))
                    dve.wait_ge(given, 1)
                    step(dve.reciprocal(hv[:, :, 4], hv[:, :, 3]))
                    for n in range(TT * HEADS):
                        hh = hm[:, n // HEADS, n % HEADS, :]
                        i = dve.tensor_scalar(hh, hh, hv[:, n, 0:1], hv[:, n, 4:5], ALU.subtract, ALU.mult)
                    step(i)
                    flat = hm[:, :, :, :].rearrange("p t h e -> p t (h e)")
                    dve.tensor_tensor(flat, flat, ex[:, :, :], ALU.mult).then_inc(ymr, 1)
                    for b in range(4):
                        dve.wait_ge(rnd, b + 1)
                        s = slice(8 + 2 * b, 10 + 2 * b)
                        dve.tensor_tensor(mix_lo[:, s, :], PS[:, b % 2, :].rearrange("p (k t) -> p k t", k=2),
                                          mix_hi[:, s, :].bitcast(F), ALU.subtract).then_inc(cp, 1)
        cell.close()

        with ExitStack() as ph:
            par = [buf2(f"parb{i}", [P, D], F, ph) for i in range(2)]
            par_in, acc_free, resid, asked, given, stored, ready = (
                sem(x + "_4") for x in ("par_in", "acc_free", "resid", "asked", "given", "stored", "ready"))
            m0 = split_at["out2"]
            with stage() as blk:
                @blk.sync
                def _(sp):
                    load_slabs(sp, src_out2, base["out2"], NRAW, N_OUT2)
                    load_slabs(sp, src_wq, base["wq"], 0, NRAW)
                    sp.wait_ge(ready, 2)
                    sp.dma_start(h_dram, h_buf[:, :, :]).then_inc(stored, 16)
                    sp.wait_ge(stored, 16)

                @blk.gpsimd
                def _(pool):
                    clear_last_stage(pool)
                    for i, name in enumerate(("ln1_g", "ln1_b")):
                        pool.dma_start(par[i][:, :], bcast(io[name])).then_inc(par_in, 16)

                @blk.tensor
                def _(pe):
                    with loop(pe, 4, 2) as c:
                        for u in range(2):
                            pe.wait_ge(acc_free, c + (u + 1))
                            for g in range(8):
                                token_slab(pe, [PS[:, 2 * u + t, :] for t in range(TT)], c * 8, m0 + 8 * u + g, g, mix_hi, mix_lo)

                @blk.scalar
                def _(act):
                    with loop(act, N_OUT2, NRAW) as i:
                        for s in range(NRAW):
                            round_slab(act, i, m0 + s + 1)
                    for t in range(TT):
                        act.wait_ge(asked, t + 1)
                        act.activation(mv[:, t, 3:4], mv[:, t, 2:3], ACT.Sqrt).then_inc(given, 1)

                @blk.vector
                def _(dve):
                    step = chain(dve, "dve_out2")
                    dve.sem_inc(acc_free, 2)
                    with loop(dve, 4, 2) as c:
                        for u in range(2):
                            for g in range(8):
                                split_slab(dve, c * 8, m0 + 8 * u + g + 1)
                            wait_multiplied(dve, c * 8, m0 + 8 * u + 8)
                            for t in range(TT):
                                hh = h_buf[:, t, ds(c * 512 + u * 512, 512)]
                                i = dve.scalar_tensor_tensor(hh, hh, ALPHA, PS[:, 2 * u + t, :], ALU.mult, ALU.add)
                            i.then_inc(acc_free, 1)
                    dve.wait_ge(acc_free, 6)
                    dve.wait_ge(par_in, 32)
                    for t in range(TT):
                        norm_stats(dve, step, h_buf, t, asked)
                    for t in range(TT):
                        norm_apply(dve, step, h_buf, t, given, 0, par[0], par[1]).then_inc(ready, 1)
        second.close()

        top = ExitStack()
        ctx.enter_context(top)

        def buf3(name, shape, dt=F, where=top):
            return where.enter_context(nc.sbuf_tensor(name, shape, dt))
        pick_at = nc.sbuf_base
        pick = buf3("pick", [P, 3, T])
        hT = top.enter_context(ExitStack())
        h_hi_at = nc.sbuf_base
        h_hi = buf3("h2_hi", [P, KT, T], R, hT)
        h_lo = buf3("h2_lo", [P, KT, T], R, hT)

        wt_at = nc.sbuf_base
        wt = buf3("wt", [P, N_KEYS, T])

        def top_step(dve, k, src, n, tk, count):
            dve.wait_ge(tk, count)
            carry(dve)
            for t in range(TT):
                if k == 0:
                    i = dve.max(t8[:, t, 0:8], src[t])
                elif k == 1:
                    dve.max_index(i8[:, t, 0:8], t8[:, t, 0:8], src[t])
                    i = dve.match_replace(rest[:, t, 0:n], t8[:, t, 0:8], src[t], -3.0e38)
                elif k == 2:
                    i = dve.max(t8[:, t, 8:16], rest[:, t, 0:n])
                else:
                    i = dve.max_index(i8[:, t, 8:16], t8[:, t, 8:16], rest[:, t, 0:n])
            i.then_inc(tk, 1)

        with ExitStack() as ph:
            sv = nc.alloc_sbuf_tensor_at("sv", [P, TT, 2 * HEADS, TOPK], F, offset=pick_at)
            si = buf3("si", [P, TT, 2 * HEADS, TOPK], F, ph)
            gt = buf3("gt", [P, TT, HEADS, TOPK], F, ph)
            gs = buf3("gs", [P, TT, HEADS, 2], F, ph)
            eid = buf3("eid", [P, TT, 2, HEADS, TOPK], F, ph)
            t8 = buf3("t8", [P, TT, TOPK], F, ph)
            i8 = buf3("i8", [P, TT, TOPK], U32, ph)
            eq = buf3("eq", [P, TT, 2, 256], F, ph)
            rest, cand = eq[:, :, 0, :], eq[:, :, 1, :]
            abu = buf3("abu", [P, TT, 2, TOPK], U32, ph)
            abf = buf3("abf", [P, TT, 2, TOPK], F, ph)

            keys = nc.alloc_sbuf_tensor_at("keys", [P, 2 * HEADS, N_KEYS], F, offset=wt_at)
            qp = nc.alloc_sbuf_tensor_at("qp", [P, 2, T], F, offset=wt_at + 2 * HEADS * N_KEYS * 4)
            tr, rnd, cp, keys_in, acc_free, s_done, s_free, tk = (
                sem(x + "_5") for x in ("tr", "rnd", "cp", "keys_in", "acc_free", "s_done", "s_free", "tk"))
            m0 = split_at["wq"]
            with stage() as blk:
                @blk.sync
                def _(sp):
                    sp.dma_start(keys[:, :, :], io["keys"]).then_inc(keys_in, 16)
                    load_slabs(sp, src_wq, base["wq"], NRAW, N_WQ)
                    load_slabs(sp, src_u, base["u"], 0, NRAW)

                @blk.gpsimd
                def _(pool):
                    clear_last_stage(pool)

                @blk.tensor
                def _(pe):
                    transpose_in(pe, h_buf, None, cp, tr, banks=(0, 1))
                    pe.wait_ge(cp, 8)

                    def query(reg, n):
                        r2 = None if reg is None else reg * 2
                        pe.wait_ge(acc_free, n + 1 if reg is None else reg + (n + 1))
                        for half in range(2):
                            feature_slab(pe, PS[:, 2 + n % 2, 0:T], r2, m0 + 2 * n + half, half, h_hi, h_lo, slice(0, T))

                    def score(reg, n):
                        pe.wait_ge(acc_free, n + 3 if reg is None else reg + (n + 3))
                        pe.wait_ge(s_free, n + 1 if reg is None else reg + (n + 1))
                        for t in range(TT):
                            last = pe.matmul(PS[:, 4 + n % 2, t * N_KEYS:(t + 1) * N_KEYS], qp[:, n % 2, t * P:(t + 1) * P],
                                             keys[:, n if reg is None else reg + n, :], start=True, stop=True)
                        last.then_inc(s_done, 1)
                    query(None, 0)
                    query(None, 1)
                    pe.wait_ge(keys_in, 16)
                    score(None, 0)
                    with loop(pe, 2 * HEADS - 2, 2) as j:
                        for u in range(2):
                            query(j, 2 + u)
                            score(j, 1 + u)
                    score(None, 2 * HEADS - 1)

                @blk.scalar
                def _(act):
                    transposed_round(act, tr, h_hi, rnd, banks=(0, 1))
                    act.sem_inc(acc_free, 2)
                    with loop(act, 2 * HEADS, 2) as j:
                        for u in range(2):
                            for s in range(2):
                                round_slab(act, j * 2, m0 + 2 * u + s + 1)
                            wait_multiplied(act, j * 2, m0 + 2 * u + 2)
                            act.activation(qp[:, u, :], PS[:, 2 + u, 0:T], ACT.Copy).then_inc(acc_free, 1)

                @blk.vector
                def _(dve):
                    transposed_split(dve, h_hi, h_lo, rnd, cp, banks=(0, 1))
                    dve.sem_inc(s_free, 2)
                    dve.sem_inc(tk, 1)
                    for s in range(4):
                        split_slab(dve, None, m0 + s + 1)

                    def rank(reg, n):
                        r2 = None if reg is None else reg * 2
                        done = 5 * n + 1 if reg is None else reg * 5 + (5 * n + 1)
                        src = [PS[:, 4 + n % 2, t * N_KEYS:(t + 1) * N_KEYS] for t in range(TT)]
                        if reg is not None:
                            split_slab(dve, r2, m0 + 2 * n + 5)
                        dve.wait_ge(s_done, n + 1 if reg is None else reg + (n + 1))
                        top_step(dve, 0, src, N_KEYS, tk, done)
                        top_step(dve, 1, src, N_KEYS, tk, done + 1)
                        if reg is not None:
                            split_slab(dve, r2, m0 + 2 * n + 6)
                        top_step(dve, 2, src, N_KEYS, tk, done + 2)
                        dve.sem_inc(s_free, 1)
                        top_step(dve, 3, src, N_KEYS, tk, done + 3)
                        dve.wait_ge(tk, done + 4)
                        at = n if reg is None else reg + n
                        dve.tensor_copy(sv[:, :, at, :], t8[:, :, :])
                        dve.tensor_copy(si[:, :, at, :], i8[:, :, :]).then_inc(tk, 1)
                    with loop(dve, 2 * HEADS - 2, 2) as j:
                        for u in range(2):
                            rank(j, u)
                    for n in range(2 * HEADS - 2, 2 * HEADS):
                        rank(None, n)
                    dve.wait_ge(tk, 5 * 2 * HEADS + 1)

            tk, sh, g_exp, g_ready, p_tr, acc_free = (
                sem(x + "_u") for x in ("tk", "sh", "g_exp", "g_ready", "p_tr", "acc_free"))
            m0 = split_at["u"]
            HEAD_SLABS = 8
            J1 = HEADS * HEAD_SLABS // 2
            J2 = J1 + 2
            with stage() as blk:
                @blk.sync
                def _(sp):
                    load_slabs(sp, src_u, base["u"], NRAW, N_U)
                    load_slabs(sp, src_v, base["v"], 0, NRAW)

                @blk.gpsimd
                def _(pool):
                    clear_last_stage(pool)

                @blk.tensor
                def _(pe):
                    def experts(reg, j):
                        pe.wait_ge(acc_free, j + 1 if reg is None else reg + (j + 1))
                        r2 = None if reg is None else reg * 2
                        for half in range(2):
                            feature_slab(pe, PS[:, j % 2, 0:T], r2, m0 + 2 * j + half, half, h_hi, h_lo, slice(0, T))
                    with loop(pe, J1, 2) as j:
                        for u in range(2):
                            experts(j, u)
                    for j in range(J1, J2):
                        experts(None, j)
                    pe.wait_ge(g_ready, 1)
                    for a in range(3):
                        for t in range(TT):
                            src = gt[:, t, :, :] if a == 2 else eid[:, t, a, :, :]
                            last = pe.transpose(PS[:, 2 + a, t * P:(t + 1) * P], src.rearrange("p h k -> p (h k)"), ident)
                    last.then_inc(p_tr, 1)
                    with loop(pe, N_KEYS - J2, 2) as j:
                        for u in range(2):
                            experts(j, J2 + u)

                @blk.scalar
                def _(act):
                    def activate(reg, j):
                        r2 = None if reg is None else reg * 2
                        wait_multiplied(act, r2, m0 + 2 * j + 2)
                        act.activation(wt[:, j if reg is None else reg + j, :], PS[:, j % 2, 0:T], ACT.Gelu).then_inc(acc_free, 1)
                    act.preload_act_table(ACT.Gelu)
                    act.sem_inc(acc_free, 2)
                    with loop(act, J1, 2) as j:
                        for u in range(2):
                            for s in range(2):
                                round_slab(act, j * 2, m0 + 2 * u + s + 1)
                            activate(j, u)
                    for j in range(J1, J2):
                        for s in range(2):
                            round_slab(act, None, m0 + 2 * j + s + 1)
                        if j == J1:
                            act.wait_ge(sh, 1)
                            act.activation(gt[:, :, :, :], gt[:, :, :, :], ACT.Exp).then_inc(g_exp, 1)
                        activate(None, j)
                    act.wait_ge(p_tr, 1)
                    act.activation(pick[:, :, :], PS[:, 2:5, 0:T], ACT.Copy)
                    with loop(act, N_KEYS - J2, 2) as j:
                        for u in range(2):
                            for s in range(2):
                                round_slab(act, j * 2, m0 + 2 * (J2 + u) + s + 1)
                            activate(j, J2 + u)

                @blk.vector
                def _(dve):
                    step = chain(dve, "dve_top")
                    per = 10
                    iota16 = cst[:, C_IOTA:C_IOTA + TOPK]
                    src = [cand[:, t, :] for t in range(TT)]
                    both = [(t, half) for t in range(TT) for half in range(2)]

                    def square(t, half):
                        return eq[:, t, half, :].rearrange("p (k a) -> p k a", k=TOPK)
                    dve.sem_inc(tk, 1)
                    with loop(dve, HEADS) as h:
                        def written(k):
                            dve.wait_ge(tk, h * per + (k + 1))
                        def split(s):
                            split_slab(dve, h * HEAD_SLABS, m0 + s + 1)
                        written(0)
                        for t in range(TT):
                            s0 = sv[:, t, h * 2, :][:, :, None].broadcast_to([P, TOPK, TOPK])
                            s1 = sv[:, t, h * 2 + 1, :][:, None, :].broadcast_to([P, TOPK, TOPK])
                            i = dve.tensor_tensor(cand[:, t, :].rearrange("p (a b) -> p a b", a=TOPK), s0, s1, ALU.add)
                        i.then_inc(tk, 1)
                        split(0)
                        top_step(dve, 0, src, 256, tk, h * per + 2)
                        split(1)
                        top_step(dve, 1, src, 256, tk, h * per + 3)
                        split(2)
                        top_step(dve, 2, src, 256, tk, h * per + 4)
                        top_step(dve, 3, src, 256, tk, h * per + 5)
                        split(3)
                        written(5)
                        dve.tensor_copy(gt[:, :, h, :], t8[:, :, :])
                        dve.tensor_scalar(abu[:, :, 0, :], i8[:, :, :], 4, None, ALU.logical_shift_right)
                        dve.tensor_scalar(abu[:, :, 1, :], i8[:, :, :], 15, None, ALU.bitwise_and).then_inc(tk, 1)
                        written(6)
                        dve.tensor_copy(abf[:, :, :, :], abu[:, :, :, :]).then_inc(tk, 1)
                        split(4)
                        written(7)
                        for t, half in both:
                            i = dve.tensor_tensor(square(t, half), abf[:, t, half, :][:, :, None].broadcast_to([P, TOPK, TOPK]),
                                                  iota16[:, None, :].broadcast_to([P, TOPK, TOPK]), ALU.is_equal)
                        i.then_inc(tk, 1)
                        split(5)
                        written(8)
                        for t, half in both:
                            key = si[:, t, h * 2 + half, :][:, None, :].broadcast_to([P, TOPK, TOPK])
                            i = dve.tensor_tensor(square(t, half), square(t, half), key, ALU.mult)
                        i.then_inc(tk, 1)
                        split(6)
                        written(9)
                        for t, half in both:
                            i = dve.tensor_reduce(eid[:, t, half, h, :], square(t, half), X, ALU.add)
                        i.then_inc(tk, 1)
                        split(7)
                    dve.wait_ge(tk, HEADS * per + 1)
                    step(dve.tensor_copy(gs[:, :, :, 0], gt[:, :, :, 0]))
                    for t in range(TT):
                        i = dve.tensor_tensor(gt[:, t, :, :], gt[:, t, :, :], gs[:, t, :, 0:1].broadcast_to([P, HEADS, TOPK]),
                                              ALU.subtract)
                    i.then_inc(sh, 1)
                    for s in range(2):
                        split_slab(dve, None, m0 + 2 * J1 + s + 1)
                    dve.wait_ge(g_exp, 1)
                    step(dve.tensor_reduce(gs[:, :, :, 0], gt[:, :, :, :], X, ALU.add))
                    step(dve.reciprocal(gs[:, :, :, 1], gs[:, :, :, 0]))
                    for t in range(TT):
                        i = dve.tensor_tensor(gt[:, t, :, :], gt[:, t, :, :], gs[:, t, :, 1:2].broadcast_to([P, HEADS, TOPK]),
                                              ALU.mult)
                    i.then_inc(g_ready, 1)
                    for s in range(2, 4):
                        split_slab(dve, None, m0 + 2 * J1 + s + 1)
                    with loop(dve, N_U - 2 * J2, NRAW) as i:
                        for s in range(NRAW):
                            split_slab(dve, i, m0 + 2 * J2 + s + 1)

        GT = 4
        with ExitStack() as ph:
            row_hot = buf3("row_hot", [P, 2, GT, N_KEYS], F, ph)
            col_hot = buf3("col_hot", [P, 2, GT, N_KEYS], F, ph)
            col_of = buf3("col_of", [P, 2, GT], F, ph)
            far = buf3("far", [P, 2, GT // 2, N_KEYS], F, ph)
            rows_made, cols_made, cols_made_act, dense, weighed, col_in, squared = (
                sem(x + "_g") for x in ("rows_made", "cols_made", "cols_made_act", "dense", "weighed", "col_in", "squared"))
            iota = cst[:, C_IOTA:C_IOTA + N_KEYS]
            NG = T // GT
            with stage() as blk:
                @blk.gpsimd
                def _(pool):
                    clear_last_stage(pool)
                    pool.sem_inc(dense, 2)
                    with loop(pool, NG, 2) as g:
                        for u in range(2):
                            pool.tensor_copy(col_of[:, u, :], pick[:, 1, ds(g * GT + u * GT, GT)]).then_inc(col_in, 1)
                            pool.wait_ge(dense, g + (u + 1))
                            pool.wait_ge(col_in, g + (u + 1))
                            carry(pool)
                            for t in range(GT // 2):
                                i = pool.tensor_scalar(col_hot[:, u, t, :], iota, col_of[:, u, t:t + 1], None, ALU.is_equal)
                            i.then_inc(cols_made, 1)

                @blk.scalar
                def _(act):
                    with loop(act, NG, 2) as g:
                        for u in range(2):
                            for t in range(GT // 2):
                                i = act.activation(far[:, u, t, :], iota, ACT.Square, scale=-1.0,
                                                   bias=pick[:, 1, ds(g * GT + (u * GT + GT // 2 + t), 1)])
                            i.then_inc(squared, 1)
                            act.wait_ge(dense, g + (u + 1))
                            act.wait_ge(squared, g + (u + 1))
                            act.activation(col_hot[:, u, GT // 2:, :], far[:, u, :, :], ACT.Relu, scale=-1.0, bias=1.0)\
                               .then_inc(cols_made_act, 1)

                @blk.vector
                def _(dve):
                    def rows(reg, n):
                        for t in range(GT):
                            at = n * GT + t
                            tok = slice(at, at + 1) if reg is None else ds(reg * GT + at, 1)
                            i = dve.tensor_scalar(row_hot[:, n % 2, t, :], iota, pick[:, 0, tok], pick[:, 2, tok],
                                                  ALU.is_equal, ALU.mult)
                        i.then_inc(rows_made, 1)

                    def multiply(reg, n):
                        dve.wait_ge(dense, n + 3 if reg is None else reg + (n + 3))
                        at = slice(n * GT, n * GT + GT) if reg is None else ds(reg * GT + n * GT, GT)
                        dve.tensor_tensor(wt[:, :, at], wt[:, :, at], PS[:, 2 + n % 2, :].rearrange("p (t j) -> p j t", t=GT),
                                          ALU.mult).then_inc(weighed, 1)
                    rows(None, 0)
                    rows(None, 1)
                    with loop(dve, NG - 2, 2) as g:
                        for u in range(2):
                            multiply(g, u)
                            rows(g, u + 2)
                    multiply(None, NG - 2)
                    multiply(None, NG - 1)

                @blk.tensor
                def _(pe):
                    pe.sem_inc(weighed, 2)
                    with loop(pe, NG, 2) as g:
                        for u in range(2):
                            pe.wait_ge(weighed, g + (u + 1))
                            pe.wait_ge(rows_made, g + (u + 1))
                            pe.wait_ge(cols_made, g + (u + 1))
                            pe.wait_ge(cols_made_act, g + (u + 1))
                            for t in range(GT):
                                last = pe.matmul(PS[:, 2 + u, t * N_KEYS:(t + 1) * N_KEYS], row_hot[:, u, t, :],
                                                 col_hot[:, u, t, :], start=True, stop=True)
                            last.then_inc(dense, 1)

        with ExitStack() as ph:
            wj_hi = [buf3(f"wj_hi{i}", [P, T], R, ph) for i in range(2)]
            wj_lo = [buf3(f"wj_lo{i}", [P, T], R, ph) for i in range(2)]
            hb = nc.alloc_sbuf_tensor_at("hb", [P, TT, D], F, offset=h_hi_at)
            par = [nc.alloc_sbuf_tensor_at(f"parc{i}", [P, D], F, offset=h_hi_at + (TT + i) * D * 4) for i in range(2)]
            wj_round, wj_split, late_in, ff_done, asked, given, ready, out_done = (
                sem(x + "_6") for x in ("wj_round", "wj_split", "late_in", "ff_done", "asked", "given", "ready", "out_done"))
            m0 = split_at["v"]
            with stage() as blk:
                @blk.sync
                def _(sp):
                    load_slabs(sp, src_v, base["v"], NRAW, N_V)
                    for t in range(TT):
                        sp.wait_ge(ready, t + 1)
                        sp.dma_start(io["out"][t * P:(t + 1) * P, :], hb[:, t, :]).then_inc(out_done, 16)
                    sp.wait_ge(out_done, 32)

                @blk.gpsimd
                def _(pool):
                    clear_last_stage(pool)
                    pool.dma_start(hb[:, :, :], h_dram).then_inc(late_in, 16)
                    for i, name in enumerate(("ln2_g", "ln2_b")):
                        pool.dma_start(par[i][:, :], bcast(io[name])).then_inc(late_in, 16)

                def split_weights(act, dve, j, u):
                    n = u if j is None else j + u
                    if act is not None:
                        wait_multiplied(act, None if j is None else j * 2, m0 - 4 + 2 * u + 2)
                        act.activation(wj_hi[u % 2][:, :], wt[:, n, :], ACT.Copy).then_inc(wj_round, 1)
                    if dve is not None:
                        dve.wait_ge(wj_round, n + 1)
                        dve.tensor_tensor(wj_lo[u % 2][:, :], wt[:, n, :], wj_hi[u % 2][:, :].bitcast(F), ALU.subtract)\
                           .then_inc(wj_split, 1)

                @blk.scalar
                def _(act):
                    def pair(j, last):
                        for u in range(2):
                            split_weights(act, None, j, u)
                            for s in range(2):
                                if not (last and u == 1 and s == 1):
                                    round_slab(act, None if j is None else j * 2, m0 + 2 * u + s + 1)
                    with loop(act, N_KEYS - 2, 2) as j:
                        pair(j, False)
                    for u in range(2):
                        split_weights(act, None, None, N_KEYS - 2 + u)
                        for s in range(2 - u):
                            round_slab(act, None, m0 + 2 * (N_KEYS - 2 + u) + s + 1)
                    for t in range(TT):
                        act.wait_ge(asked, t + 1)
                        act.activation(mv[:, t, 3:4], mv[:, t, 2:3], ACT.Sqrt).then_inc(given, 1)

                @blk.vector
                def _(dve):
                    step = chain(dve, "dve_last")
                    with loop(dve, N_KEYS - 2, 2) as j:
                        for u in range(2):
                            split_weights(None, dve, j, u)
                            for s in range(2):
                                split_slab(dve, j * 2, m0 + 2 * u + s + 1)
                    for u in range(2):
                        split_weights(None, dve, None, N_KEYS - 2 + u)
                        for s in range(2 - u):
                            split_slab(dve, None, m0 + 2 * (N_KEYS - 2 + u) + s + 1)
                    dve.wait_ge(late_in, 48)
                    wait_multiplied(dve, None, m0 + N_V)
                    for t in range(TT):
                        for c in range(4):
                            hh = hb[:, t, c * 512:(c + 1) * 512]
                            i = dve.scalar_tensor_tensor(hh, hh, ALPHA, PS[:, 4 * t + c, :], ALU.mult, ALU.add)
                        step(i)
                        norm_stats(dve, step, hb, t, asked)
                    for t in range(TT):
                        norm_apply(dve, step, hb, t, given, 0, par[0], par[1]).then_inc(ready, 1)

                @blk.tensor
                def _(pe):
                    def expert_slab(j, m, n, a, first, last_one):
                        if a == 0:
                            pe.wait_ge(wj_split, n + 1 if j is None else j + (n + 1))
                        for c in range(2):
                            pe.wait_ge(lo_ready, halves(None if j is None else j * 2, m) + (c + 1))
                            col = slice(c * 512, (c + 1) * 512)
                            for t in range(TT):
                                tok = slice(t * P, (t + 1) * P)
                                last = mm3(pe, PS[:, 4 * t + 2 * a + c, :], (wj_hi[n % 2][:, tok], wj_lo[n % 2][:, tok]),
                                           (w_hi[m % 2][:, col], w_lo[m % 2][:, col]), first, last_one)
                            last.then_inc(multiplied, 1)
                    for u in range(2):
                        for a in range(2):
                            expert_slab(None, m0 + 2 * u + a, u, a, u == 0, False)
                    with loop(pe, N_KEYS - 4, 2) as j:
                        for u in range(2):
                            for a in range(2):
                                expert_slab(j, m0 + 4 + 2 * u + a, 2 + u, a, False, False)
                    for n in range(N_KEYS - 2, N_KEYS):
                        for a in range(2):
                            expert_slab(None, m0 + 2 * n + a, n, a, False, n == N_KEYS - 1)
        top.close()


NAMES = ["x", "ctx", "c_cols", "consts", "mod_cols", "lam_in", "w_mod_s", "w_in_a", "w_in_b", "rpb_e", "subln_g",
         "w_out_s", "final_g", "ln_in_g", "ln_in_b", "w_in2_s", "conv_cols", "w_gate_cols", "b_gate", "mh_g", "w_out2_s",
         "ln1_g", "ln1_b", "wq_s", "keys", "u_s", "v", "ln2_g", "ln2_b"]


def constants():
    import numpy as np
    c = np.zeros((P, C_ALL), np.float32)
    p = np.arange(P)
    c[p, C_IDENT + p] = 1
    c[:, C_ONES:C_ONES + P] = 1
    c[:, C_TRI:C_TRI + P] = np.where(p[:, None] <= p[None, :], 0.0, MASKED)
    c[:, C_IOTA:C_IOTA + P] = p
    f = p % 64
    partner = np.where(p % 32 < 16, p + 16, p - 16)
    c[partner, C_PERM + p] = 1
    inv = (np.float32(10000.0) ** (-np.arange(16, dtype=np.float32) / np.float32(16))).astype(np.float32)
    t = np.arange(T)
    pos = np.where((f < 32)[:, None], (t // 64)[None, :], (t % 64)[None, :]).astype(np.float32)
    ang = pos * inv[p % 16][:, None]
    c[:, C_COS:C_COS + T] = np.cos(ang)
    c[:, C_SIN:C_SIN + T] = np.sin(ang) * np.where(p % 32 < 16, -1, 1)[:, None]
    j, col = (p % 64)[:, None], np.arange(64)[None, :]
    c0 = np.clip(j - 8, 0, 48)
    c[:, C_NAMASK:C_NAMASK + 64] = np.where((col >= c0) & (col < c0 + 16), 0.0, MASKED)
    c[np.arange(8), C_EYE8 + np.arange(8)] = 1
    return c


def feature_slabs(w):
    import numpy as np
    n = w.shape[1] // P
    return np.ascontiguousarray(w.reshape(2, 8, P, n, P).transpose(3, 0, 2, 1, 4)).reshape(2 * n, P, SLAB)


def token_slabs(w):
    import numpy as np
    n = w.shape[1] // 512
    return np.ascontiguousarray(w.reshape(8, 2, P, n, 512).transpose(3, 0, 2, 1, 4)).reshape(8 * n, P, SLAB)


def cols(v):
    return v.reshape(-1, P).T


def lay_out(i):
    import numpy as np
    w_in, w2 = i["w_in"][0], i["w_in_2"][0]
    pad = np.pad(i["rpb"][0], ((0, 0), (0, 0), (48, 48)))
    rpb_e = np.stack([pad[:, :, 63 - j:127 - j] for j in range(64)], axis=1).reshape(HEADS, 64, 15 * 64)
    half = lambda o: np.concatenate([feature_slabs(w_in[:, o:o + 2 * WA]), token_slabs(w_in[:, o + 2 * WA:o + 4 * WA])])
    conv = feature_slabs(w2[:, 0:3 * WA]).reshape(3, 8, 2, P, SLAB).transpose(1, 0, 2, 3, 4).reshape(48, P, SLAB)
    return {
        "x": i["x"][0], "ctx": i["ctx"][0],
        "c_cols": np.stack([cols(i["c"][0]), cols(i["c_ctx"])], axis=2),
        "consts": constants(),
        "mod_cols": np.concatenate([cols(i["b_mod"][0]), cols(i["norm_g"][0])], axis=1),
        "lam_in": np.concatenate([i["lam_q1"][0], i["lam_k1"][0], i["lam_q2"][0], i["lam_k2"][0]])[None],
        "w_mod_s": token_slabs(i["w_mod"][0]),
        "w_in_a": half(0), "w_in_b": half(4 * WA),
        "rpb_e": rpb_e, "subln_g": i["subln_g"],
        "w_out_s": token_slabs(i["w_out"][0]),
        "final_g": i["final_g"][None], "ln_in_g": i["ln_in_g_2"][None], "ln_in_b": i["ln_in_b_2"][None],
        "w_in2_s": np.concatenate([conv, feature_slabs(w2[:, 3 * WA:5 * WA]), token_slabs(w2[:, 5 * WA:7 * WA])]),
        "conv_cols": np.concatenate([cols(i["conv_w_2"][0, n]) for n in range(3)] + [cols(i["conv_b_2"][0])], axis=1),
        "w_gate_cols": w2[:, 7 * WA:].reshape(KT, P, 16).transpose(1, 0, 2).reshape(P, KT * 16),
        "b_gate": i["b_gate_2"], "mh_g": i["mh_norm_g_2"],
        "ln1_g": i["ln1_g_2"], "ln1_b": i["ln1_b_2"], "ln2_g": i["ln2_g_2"], "ln2_b": i["ln2_b_2"],
        "keys": i["peer_keys_2"][0].reshape(2 * HEADS, N_KEYS, P).transpose(2, 0, 1),
        "w_out2_s": token_slabs(i["w_out_2"][0]), "wq_s": feature_slabs(i["peer_wq_2"][0]),
        "u_s": np.ascontiguousarray(i["peer_u_2"][0].reshape(N_KEYS, N_KEYS, 2, 8, P).transpose(1, 2, 4, 3, 0)).reshape(2 * N_KEYS, P, SLAB),
        "v": i["peer_v_2"][0],
    }


def kernel(**inputs):
    import numpy as np
    import concourse.bacc as bacc
    from concourse.bass_utils import run_bass_kernel_spmd

    nc = bacc.Bacc("TRN2", target_bir_lowering=False, num_devices=1)
    laid = lay_out({k: np.asarray(v) for k, v in inputs.items()})
    arrays, io = {}, {}
    for name in NAMES:
        a = np.ascontiguousarray(laid[name])
        arrays[f"in_{name}"] = a
        io[name] = nc.dram_tensor(f"in_{name}", a.shape, mybir.dt.from_np(a.dtype), kind="ExternalInput").ap()
    io["out"] = nc.dram_tensor("out_0_dram", (T, D), mybir.dt.float32, kind="ExternalOutput").ap()
    peer_block_kernel(nc, io)
    r = run_bass_kernel_spmd(nc, [arrays], core_ids=[0])
    return r.results[0]["out_0_dram"].reshape(1, T, D)
```

```python
import concourse.bass as bass
from concourse import mybir
from contextlib import ExitStack, contextmanager

T = 256
D = 2048
P = 128
KT = D // P
TT = T // P
WA = 1024
HEADS = 8
SLAB = 1024
LAMBDA_INIT = 0.2
MASKED = -1e30
ALPHA = 2 ** 0.25
N_KEYS = 128
TOPK = 16

N_MOD, N_WIN_A, N_WIN_B, N_OUT, N_WIN2, N_OUT2, N_WQ, N_U, N_V = 96, 64, 64, 32, 112, 32, 32, 256, 256
NRAW = 4

C_IDENT, C_ONES, C_TRI, C_IOTA = 0, 128, 256, 384
C_PERM, C_COS, C_SIN, C_NAMASK, C_EYE8 = 512, 640, 896, 1152, 1216
C_KEEP, C_ALL = 512, 1224
H_OFFSET = 212960


@contextmanager
def loop(eng, count, step=1):
    with eng.Fori(0, count // step) as i:
        yield i * step if step > 1 else i


def peer_block_kernel(nc, io):
    F, R = mybir.dt.float32, mybir.dt.float32r
    U32 = mybir.dt.uint32
    ALU = mybir.AluOpType
    ACT = mybir.ActivationFunctionType
    X = mybir.AxisListType.X
    ds = bass.ds
    ctx = ExitStack()

    def lasting_sem(name):
        return ctx.enter_context(nc.semaphore(name))

    used, to_clear = [], []

    def sem(name):
        used.append(nc.alloc_semaphore(name=name))
        return used[-1]

    def clear_last_stage(pool):
        for s in to_clear:
            pool.sem_clear(s)

    @contextmanager
    def stage():
        with nc.Block() as block:
            yield block
        for s in to_clear:
            nc.release_semaphore(s)
        to_clear[:] = used
        used.clear()

    with ctx:
        def keep(name, shape, dt=F):
            return ctx.enter_context(nc.sbuf_tensor(name, shape, dt))

        raw = keep("raw", [P, NRAW, SLAB])
        w_hi = [keep(f"w_hi{i}", [P, SLAB], R) for i in range(2)]
        w_lo = [keep(f"w_lo{i}", [P, SLAB], R) for i in range(2)]
        raw_ready = [lasting_sem(f"raw_ready{i}") for i in range(NRAW)]
        hi_ready = lasting_sem("hi_ready")
        lo_ready = lasting_sem("lo_ready")
        multiplied = lasting_sem("multiplied")
        HALVES = [slice(0, SLAB // 2), slice(SLAB // 2, SLAB)]

        def halves(reg, m):
            return 2 * m if reg is None else reg * 2 + 2 * m

        def past(reg, n, scale=1):
            return n if reg is None else (reg if scale == 1 else reg * scale) + n

        def pairs(eng, before, body, items=2 * HEADS):
            before()
            step = 2 * items // HEADS
            with loop(eng, HEADS - 2, 2) as h:
                for e in range(step):
                    body(h, e)
            for e in range(items - step, items):
                body(None, e)

        def wait_multiplied(eng, reg, n):
            eng.wait_ge(multiplied, halves(reg, n) + 4)

        passed = lasting_sem("passed")

        def raw_wait(eng, slab):
            reg, off = slab
            if reg is None:
                eng.wait_ge(raw_ready[off % NRAW], 16 * (off // NRAW + 1))
            else:
                eng.wait_ge(raw_ready[off % NRAW], reg * 4 + 16 * (off // NRAW + 1))

        def load_slabs(sp, src, base, first, last):
            def one(reg, off):
                n = base + off if reg is None else reg + (base + off)
                src_at = off if reg is None else reg + off
                if base + off >= NRAW:
                    sp.wait_ge(lo_ready, n * 2 - 2 * (NRAW - 1))
                sp.dma_start(raw[:, off % NRAW, :], src(src_at)).then_inc(raw_ready[off % NRAW], 16)
            if last - first <= NRAW:
                for off in range(first, last):
                    one(None, off)
                return
            with loop(sp, last - first, NRAW) as i:
                for s in range(NRAW):
                    one(i, first + s)

        def round_slab(act, reg, m):
            raw_wait(act, (reg, m))
            for x, half in enumerate(HALVES):
                act.wait_ge(multiplied, halves(reg, m) + (x + 1))
                act.activation(w_hi[m % 2][:, half], raw[:, m % NRAW, half], ACT.Copy).then_inc(hi_ready, 1)

        def split_slab(dve, reg, m):
            for x, half in enumerate(HALVES):
                dve.wait_ge(hi_ready, halves(reg, m) + (x + 1))
                dve.tensor_tensor(w_lo[m % 2][:, half], raw[:, m % NRAW, half], w_hi[m % 2][:, half].bitcast(F),
                                  ALU.subtract).then_inc(lo_ready, 1)

        def carry(eng):
            eng.sem_inc(passed, 1)

        def mm3(pe, out, lhs, rhs, start, stop):
            pe.matmul(out, lhs[0], rhs[0], start=start, stop=False)
            pe.matmul(out, lhs[0], rhs[1], start=False, stop=False)
            return pe.matmul(out, lhs[1], rhs[0], start=False, stop=stop)

        def feature_slab(pe, out, reg, m, half, x_hi, x_lo, cols):
            for k in range(8):
                if k % 4 == 0:
                    pe.wait_ge(lo_ready, halves(reg, m) + (k // 4 + 1))
                c = slice(k * P, (k + 1) * P)
                kk = 8 * half + k
                last = mm3(pe, out, (w_hi[m % 2][:, c], w_lo[m % 2][:, c]),
                           (x_hi[:, kk, cols], x_lo[:, kk, cols]), kk == 0, kk == KT - 1)
                if k % 4 == 3:
                    last.then_inc(multiplied, 1)

        def token_slab(pe, outs, reg, m, g, x_hi, x_lo):
            for k in range(2):
                pe.wait_ge(lo_ready, halves(reg, m) + (k + 1))
                c = slice(k * 512, (k + 1) * 512)
                kk = 2 * g + k
                for t, out in enumerate(outs):
                    tok = slice(t * P, (t + 1) * P)
                    last = mm3(pe, out, (x_hi[:, kk, tok], x_lo[:, kk, tok]),
                               (w_hi[m % 2][:, c], w_lo[m % 2][:, c]), kk == 0, kk == KT - 1)
                last.then_inc(multiplied, 1)

        PS = ctx.enter_context(nc.psum_tensor("PS", [P, 8, 512], F))
        cst = keep("cst", [P, C_KEEP])
        ident = cst[:, C_IDENT:C_IDENT + P]
        h_dram = nc.dram_tensor("h_dram", (P, TT, D), F, kind="Internal").ap()
        x_tok = io["x"].rearrange("(t p) d -> p t d", p=P)
        h_stored = lasting_sem("h_stored")
        small = lasting_sem("small")

        def small_load(eng, dst, src):
            eng.dma_start(dst, src).then_inc(small, 16)

        def bcast(row):
            return bass.AP(row.tensor, row.offset, [[0, P], [1, row.shape[-1]]])

        chains = {}

        def chain(eng, name):
            if name not in chains:
                chains[name] = [sem(name), 0]

            def step(instruction):
                chains[name][1] += 1
                instruction.then_inc(chains[name][0], 1)
                eng.wait_ge(chains[name][0], chains[name][1])
            return step

        src_mod = lambda n: io["w_mod_s"][n]
        src_a = lambda n: io["w_in_a"][n]
        src_b = lambda n: io["w_in_b"][n]
        src_out = lambda n: io["w_out_s"][n]
        src_in2 = lambda n: io["w_in2_s"][n]
        src_out2 = lambda n: io["w_out2_s"][n]
        src_wq = lambda n: io["wq_s"][n]
        src_u = lambda n: io["u_s"][n]
        v_view = io["v"].rearrange("(i j) (a c) -> (j a) i c", j=N_KEYS, a=2)
        src_v = lambda n: v_view[n]
        base = {}
        at = 0
        for name, n in (("mod", N_MOD), ("a", N_WIN_A), ("b", N_WIN_B), ("out", N_OUT), ("in2", N_WIN2),
                        ("out2", N_OUT2), ("wq", N_WQ), ("u", N_U), ("v", N_V)):
            base[name] = at
            at += n

        def transpose_in(pe, src, sem_src, copied, done, banks=(0, 1)):
            for b in range(KT // 2):
                if b >= 2:
                    pe.wait_ge(copied, b - 1)
                for k in range(2):
                    for t in range(TT):
                        if sem_src is not None and b == 0 and k == 0:
                            pe.wait_ge(sem_src[0], sem_src[1][t])
                        last = pe.transpose(PS[:, banks[b % 2], (2 * k + t) * P:(2 * k + t + 1) * P],
                                            src[:, t, (2 * b + k) * P:(2 * b + k + 1) * P], ident)
                last.then_inc(done, 1)

        def transposed_round(act, done, dst_hi, rounded, banks=(0, 1)):
            for b in range(KT // 2):
                act.wait_ge(done, b + 1)
                act.activation(dst_hi[:, 2 * b:2 * b + 2, :], PS[:, banks[b % 2], :], ACT.Copy).then_inc(rounded, 1)

        def transposed_split(dve, dst_hi, dst_lo, rounded, copied, banks=(0, 1)):
            for b in range(KT // 2):
                dve.wait_ge(rounded, b + 1)
                dve.tensor_tensor(dst_lo[:, 2 * b:2 * b + 2, :], PS[:, banks[b % 2], :].rearrange("p (k t) -> p k t", k=2),
                                  dst_hi[:, 2 * b:2 * b + 2, :].bitcast(F), ALU.subtract).then_inc(copied, 1)

        h_buf = nc.alloc_sbuf_tensor_at("h_buf", [P, TT, D], F, offset=H_OFFSET)
        stats = keep("stats", [P, TT, 4, 6])
        mv = keep("mv", [P, TT, 8])

        def norm_stats(dve, step, y, t, asked):
            for c in range(4):
                i = dve.bn_stats(stats[:, t, c, :], y[:, t, c * 512:(c + 1) * 512])
            step(i)
            step(dve.bn_aggr(mv[:, t, 0:2], stats[:, t, :, :]))
            dve.tensor_scalar(mv[:, t, 2:3], mv[:, t, 1:2], 1e-5, None, ALU.add).then_inc(asked, 1)

        def norm_apply(dve, step, y, t, given, given_before, g, b):
            dve.wait_ge(given, given_before + t + 1)
            dve.reciprocal(mv[:, t, 4:5], mv[:, t, 3:4])
            step(dve.scalar_tensor_tensor(y[:, t, :], y[:, t, :], mv[:, t, 0:1], g[:, :], ALU.subtract, ALU.mult))
            return dve.scalar_tensor_tensor(y[:, t, :], y[:, t, :], mv[:, t, 4:5], b[:, :], ALU.mult, ALU.add)

        with ExitStack() as first:
            def buf(name, shape, dt=F, where=first):
                return where.enter_context(nc.sbuf_tensor(name, shape, dt))

            csta = buf("csta", [P, C_ALL - C_KEEP])
            perm = csta[:, C_PERM - C_KEEP:C_PERM - C_KEEP + P]
            cos_t = csta[:, C_COS - C_KEEP:C_COS - C_KEEP + T]
            sin_t = csta[:, C_SIN - C_KEEP:C_SIN - C_KEEP + T]
            na_mask = csta[:, C_NAMASK - C_KEEP:C_NAMASK - C_KEEP + 64]
            modT = buf("modT", [P, 96])
            lam = buf("lam", [P, 8])
            o_a = buf("o_a", [P, TT, WA])
            o_b = buf("o_b", [P, TT, WA])
            late = first.enter_context(ExitStack())
            x_hi = buf("x_hi", [P, KT, 2 * T], R, late)
            x_lo = buf("x_lo", [P, KT, 2 * T], R, late)

            with ExitStack() as ph:
                xs = buf("xs", [P, 4, D], F, ph)
                xT = buf("xT", [P, KT, 2 * T], F, ph)
                junk = xT[:, 4:8, :].rearrange("p a b -> p (a b)")
                cin = buf("cin", [P, KT, 2], F, ph)
                cex = buf("cex", [P, KT, 2], F, ph)
                csilu = buf("csilu", [P, KT, 2], F, ph)
                cc = xT[:, 0:4, :].rearrange("p a (b w c) -> p (a b) w c", b=4, w=2)
                cc_hi = buf("cc_hi", [P, KT, P], R, ph)
                cc_lo = buf("cc_lo", [P, KT, P], R, ph)
                mod_row = buf("mod_row", [P, 2, 512], F, ph)
                bm = buf("bm", [P, 48 + KT], F, ph)
                lamv = buf("lamv", [P, 4, 64], F, ph)
                lamp = buf("lamp", [P, 2, 64], F, ph)
                ms = buf("ms", [P, 4, 4], F, ph)
                ab = buf("ab", [P, 2, KT], F, ph)
                x_in = [sem(f"x_in{i}") for i in range(4)]
                c_in = sem("c_in")
                exp_c, silu_c, cc_round, cc_split, sq, rms_asked, rms_given, normed = (
                    sem(n) for n in ("exp_c", "silu_c", "cc_round", "cc_split", "sq", "rms_asked", "rms_given", "normed"))
                tr, tr_out, row_free, row_in, mod_tr, mod_out, lam_asked, lam_given, affine, x_round = (
                    sem(n) for n in ("tr", "tr_out", "row_free", "row_in", "mod_tr", "mod_out", "lam_asked", "lam_given",
                                     "affine", "x_round"))
                tr_outv = sem("tr_outv")
                with stage() as blk:
                    @blk.sync
                    def _(sp):
                        sp.dma_start(cin[:, :, :], io["c_cols"]).then_inc(c_in, 16)
                        load_slabs(sp, src_mod, 0, 0, NRAW)
                        load_slabs(sp, src_mod, 0, NRAW, N_MOD)
                        load_slabs(sp, src_a, base["a"], 0, NRAW)

                    @blk.gpsimd
                    def _(pool):
                        clear_last_stage(pool)
                        small_load(pool, cst[:, :], io["consts"][:, 0:C_KEEP])
                        small_load(pool, csta[:, :], io["consts"][:, C_KEEP:C_ALL])
                        small_load(pool, bm[:, :], io["mod_cols"])
                        small_load(pool, lamv[:, :, :].rearrange("p a b -> p (a b)"), bcast(io["lam_in"]))
                        with loop(pool, KT) as k:
                            pool.wait_ge(x_round, k + 1)
                            pool.tensor_tensor(x_lo[:, k, :], xT[:, k, :], x_hi[:, k, :].bitcast(F), ALU.subtract)

                    @blk.scalar
                    def _(act):
                        for t in range(4):
                            act.dma_start(xs[:, t, :], io["x" if t < 2 else "ctx"][(t % 2) * P:(t % 2 + 1) * P, :])\
                               .then_inc(x_in[t], 16)
                        act.wait_ge(c_in, 16)
                        act.activation(cex[:, :, :], cin[:, :, :], ACT.Exp, scale=-1.0).then_inc(exp_c, 1)
                        act.wait_ge(silu_c, 1)
                        act.activation(cc_hi[:, :, :], cc[:, :, :, :].rearrange("p k w c -> p k (w c)"), ACT.Copy).then_inc(cc_round, 1)
                        round_slab(act, None, 0)

                        def copy_row(reg, tile):
                            wait_multiplied(act, None if reg is None else reg * 16, 8 * tile + 8)
                            act.wait_ge(row_free, tile + 1 if reg is None else reg * 2 + (tile + 1))
                            act.activation(mod_row[:, tile % 2, :], PS[:, 6 + tile % 2, :], ACT.Copy).then_inc(row_in, 1)
                        act.sem_inc(row_free, 2)
                        for u in range(2):
                            for g in range(8):
                                round_slab(act, None, 8 * u + g + 1)
                                if g % 4 == 3:
                                    t = 2 * u + g // 4
                                    act.wait_ge(x_in[t], 16)
                                    if t:
                                        act.wait_ge(sq, t)
                                    act.activation(junk[:, :], xs[:, t, :], ACT.Square, accum_out=ms[:, t, 0:1]).then_inc(sq, 1)
                            copy_row(None, u)
                        for t in range(4):
                            act.wait_ge(rms_asked, t + 1)
                            act.activation(ms[:, t, 2:3], ms[:, t, 1:2], ACT.Sqrt).then_inc(rms_given, 1)
                        for k in range(0, KT, 2):
                            act.wait_ge(tr, k + 1)
                            act.activation(xT[:, k, :], PS[:, k % 4, :], ACT.Copy).then_inc(tr_out, 1)
                        act.wait_ge(lam_asked, 1)
                        act.activation(lam[:, 2:4], lam[:, 0:2], ACT.Exp).then_inc(lam_given, 1)
                        with loop(act, 3) as q:
                            for u in range(2):
                                for g in range(8):
                                    round_slab(act, q * 16, 16 + 8 * u + g + 1)
                                copy_row(q, 2 + u)
                        with loop(act, 2) as q:
                            def upper(k):
                                act.wait_ge(affine, q * 8 + (k + 1))
                                act.activation(x_hi[:, q * 8 + k, :], xT[:, q * 8 + k, :], ACT.Copy).then_inc(x_round, 1)
                            for u in range(2):
                                for g in range(8):
                                    round_slab(act, q * 16, 64 + 8 * u + g + 1)
                                    if g % 2 and 4 * u + g // 2:
                                        upper(4 * u + g // 2 - 1)
                                copy_row(q, 8 + u)
                            upper(7)

                    @blk.vector
                    def _(dve):
                        step = chain(dve, "dve0")
                        dve.wait_ge(exp_c, 1)
                        step(dve.tensor_scalar(cex[:, :, :], cex[:, :, :], 1.0, None, ALU.add))
                        step(dve.reciprocal(cex[:, :, :], cex[:, :, :]))
                        step(dve.tensor_tensor(csilu[:, :, :], cin[:, :, :], cex[:, :, :], ALU.mult))
                        dve.tensor_copy(cc[:, :, :, :], csilu[:, :, :, None].broadcast_to([P, KT, 2, 64])).then_inc(silu_c, 1)
                        dve.wait_ge(cc_round, 1)
                        dve.tensor_tensor(cc_lo[:, :, :], cc[:, :, :, :].rearrange("p k w c -> p k (w c)"),
                                          cc_hi[:, :, :].bitcast(F), ALU.subtract).then_inc(cc_split, 1)
                        split_slab(dve, None, 0)
                        mt = modT[:, :].rearrange("p (a w) -> p a w", w=2)

                        def add_bias(reg, tile):
                            n = tile + 1 if reg is None else reg * 2 + (tile + 1)
                            at4 = slice(4 * tile, 4 * tile + 4) if reg is None else ds(reg * 8 + 4 * tile, 4)
                            dve.wait_ge(mod_tr, n)
                            both = PS[:, 4 + tile % 2, :].rearrange("p (a w c) -> p a w c", a=4, w=2)[:, :, :, 0]
                            dve.tensor_tensor(mt[:, at4, :], both, bm[:, at4][:, :, None].broadcast_to([P, 4, 2]), ALU.add)\
                               .then_inc(mod_out, 1)
                        for u in range(2):
                            for g in range(8):
                                split_slab(dve, None, 8 * u + g + 1)
                        for t in range(4):
                            dve.wait_ge(sq, t + 1)
                            dve.tensor_scalar(ms[:, t, 1:2], ms[:, t, 0:1], 1.0 / D, 1e-6, ALU.mult, ALU.add)\
                               .then_inc(rms_asked, 1)
                        for t in range(4):
                            dve.wait_ge(rms_given, t + 1)
                            step(dve.reciprocal(ms[:, t, 3:4], ms[:, t, 2:3]))
                            dve.tensor_scalar(xs[:, t, :], xs[:, t, :], ms[:, t, 3:4], None, ALU.mult).then_inc(normed, 1)
                        dve.wait_ge(small, 64)
                        for u in range(2):
                            add_bias(None, u)
                        for k in range(1, KT, 2):
                            dve.wait_ge(tr, k + 1)
                            dve.tensor_copy(xT[:, k, :], PS[:, k % 4, :]).then_inc(tr_outv, 1)
                        step(dve.tensor_tensor(lamp[:, :, :], lamv[:, 0:4:2, :], lamv[:, 1:4:2, :], ALU.mult))
                        dve.tensor_reduce(lam[:, 0:2], lamp[:, :, :], X, ALU.add).then_inc(lam_asked, 1)
                        dve.wait_ge(lam_given, 1)
                        step(dve.tensor_tensor(lam[:, 4:5], lam[:, 3:4], lam[:, 2:3], ALU.subtract))
                        dve.tensor_scalar(lam[:, 7:8], lam[:, 4:5], -LAMBDA_INIT, None, ALU.add)
                        with loop(dve, 3) as q:
                            for g in range(16):
                                split_slab(dve, q * 16, 16 + g + 1)
                            for u in range(2):
                                add_bias(q, 2 + u)
                        dve.wait_ge(mod_out, 8)
                        dve.wait_ge(tr_out, KT // 2)
                        dve.wait_ge(tr_outv, KT // 2)
                        for w in range(2):
                            i = dve.scalar_tensor_tensor(ab[:, w, :], mt[:, 16:32, w], 1.0, bm[:, 48:48 + KT],
                                                         ALU.add, ALU.mult)
                        step(i)
                        with loop(dve, 2) as q:
                            for g in range(16):
                                split_slab(dve, q * 16, 64 + g + 1)
                                if g % 2:
                                    k = g // 2
                                    kk = q * 8 + k
                                    for w in range(2):
                                        part = xT[:, kk, w * T:(w + 1) * T]
                                        i = dve.tensor_scalar(part, part, ab[:, w, ds(kk, 1)], mt[:, kk, w:w + 1],
                                                              ALU.mult, ALU.add)
                                    i.then_inc(affine, 1)
                            for u in range(2):
                                add_bias(q, 8 + u)

                    @blk.tensor
                    def _(pe):
                        pe.sem_inc(multiplied, 4)
                        pe.wait_ge(cc_split, 1)

                        def mod_pair(reg, pair):
                            for u in range(2):
                                tile = 2 * pair + u
                                if pair:
                                    pe.wait_ge(row_in, tile - 1 if reg is None else reg * 2 + (tile - 1))
                                for g in range(8):
                                    m = 8 * tile + g
                                    for k in range(2):
                                        pe.wait_ge(lo_ready, halves(None if reg is None else reg * 16, m) + (k + 1))
                                        c = slice(k * 512, (k + 1) * 512)
                                        kk = 2 * g + k
                                        mm3(pe, PS[:, 6 + u, :], (cc_hi[:, kk, :], cc_lo[:, kk, :]),
                                            (w_hi[m % 2][:, c], w_lo[m % 2][:, c]), kk == 0, kk == KT - 1).then_inc(multiplied, 1)

                        def mod_transposes(reg, pair):
                            for u in range(2):
                                tile = 2 * pair + u
                                pe.wait_ge(row_in, tile + 1 if reg is None else reg * 2 + (tile + 1))
                                if pair:
                                    pe.wait_ge(mod_out, tile - 1 if reg is None else reg * 2 + (tile - 1))
                                for c in range(4):
                                    last = pe.transpose(PS[:, 4 + u, c * P:(c + 1) * P], mod_row[:, u, c * P:(c + 1) * P], ident)
                                last.then_inc(mod_tr, 1)
                                pe.wait_ge(mod_tr, tile + 1 if reg is None else reg * 2 + (tile + 1))
                                pe.sem_inc(row_free, 1)
                        mod_pair(None, 0)
                        pe.wait_ge(small, 64)
                        mod_transposes(None, 0)
                        for k in range(KT):
                            if k >= 4:
                                pe.wait_ge(tr_out if k % 2 == 0 else tr_outv, k // 2 - 1)
                            for t in range(4):
                                if k == 0:
                                    pe.wait_ge(normed, t + 1)
                                last = pe.transpose(PS[:, k % 4, t * P:(t + 1) * P], xs[:, t, k * P:(k + 1) * P], ident)
                            last.then_inc(tr, 1)
                        with loop(pe, 5) as q:
                            mod_pair(q, 1)
                            mod_transposes(q, 1)

            def project(half_name, q_sb, k_sb, v_sb, g_sb, rope, nxt, ph, more_loads):
                n = half_name
                m0 = base[n]
                src = src_a if n == "a" else src_b
                acc_free, copied, permuted, perm_free = (sem(f"{x}_{n}") for x in ("acc_free", "copied", "permuted", "perm_free"))
                staged = buf(f"staged_{n}", [P, 2, T], F, ph)
                roped = buf(f"roped_{n}", [P, 2, 2, T], F, ph)
                with stage() as blk:
                    @blk.sync
                    def _(sp):
                        load_slabs(sp, src, base[n], NRAW, N_WIN_A)
                        load_slabs(sp, nxt[0], nxt[1], 0, NRAW)

                    @blk.gpsimd
                    def _(pool):
                        clear_last_stage(pool)
                        more_loads(pool)

                    @blk.scalar
                    def _(act):
                        act.sem_inc(acc_free, 2)
                        for part, dst, width in ((0, q_sb, T), (1, k_sb, 2 * T)):
                            m1 = m0 + 16 * part
                            with loop(act, HEADS, 2) as j:
                                for u in range(2):
                                    round_slab(act, j * 2, m1 + 2 * u + 1)
                                    round_slab(act, j * 2, m1 + 2 * u + 2)
                                    wait_multiplied(act, j * 2, m1 + 2 * u + 2)
                                    if not rope:
                                        act.activation(dst[:, j + u, :], PS[:, u, 0:width], ACT.Copy).then_inc(acc_free, 1)
                                        continue
                                    act.wait_ge(perm_free, j + (8 * part + u + 1))
                                    if part:
                                        act.activation(dst[:, j + u, T:2 * T], PS[:, u, T:2 * T], ACT.Copy)
                                    act.activation(staged[:, u, :], PS[:, u, 0:T], ACT.Copy).then_inc(acc_free, 1)
                        for part, dst, nt in ((2, v_sb, 4), (3, g_sb, 2)):
                            for c in range(2):
                                m1 = m0 + 16 * part + 8 * c
                                for g in range(8):
                                    round_slab(act, None, m1 + g + 1)
                                wait_multiplied(act, None, m1 + 8)
                                for t in range(nt):
                                    i = act.activation(dst[:, t, c * 512:(c + 1) * 512], PS[:, 4 * ((c + 1) % 2) + t, :],
                                                       ACT.Copy if part == 2 else ACT.Silu)
                                i.then_inc(copied, 1)

                    @blk.vector
                    def _(dve):
                        if rope:
                            dve.sem_inc(perm_free, 2)
                        step = chain(dve, f"dve_{n}")
                        rotated = sem(f"rotated_{n}")
                        for part, dst in ((0, q_sb), (1, k_sb)):
                            m1 = m0 + 16 * part
                            with loop(dve, HEADS, 2) as j:
                                for s in range(4):
                                    split_slab(dve, j * 2, m1 + s + 1)
                                for u in range(2 if rope else 0):
                                    dve.wait_ge(permuted, j + (8 * part + u + 1))
                                    dve.tensor_tensor(roped[:, u, 0, :], staged[:, u, :], cos_t, ALU.mult)
                                    dve.tensor_tensor(roped[:, u, 1, :], PS[:, 2 + u, 0:T], sin_t, ALU.mult).then_inc(rotated, 1)
                                    dve.wait_ge(rotated, j + (8 * part + u + 1))
                                    dve.tensor_tensor(dst[:, j + u, 0:T], roped[:, u, 0, :], roped[:, u, 1, :], ALU.add)\
                                       .then_inc(perm_free, 1)
                        for g in range(32):
                            split_slab(dve, None, m0 + 32 + g + 1)

                    @blk.tensor
                    def _(pe):
                        for part, cols in ((0, slice(0, T)), (1, slice(0, 2 * T))):
                            m1 = m0 + 16 * part
                            with loop(pe, HEADS, 2) as j:
                                for u in range(2):
                                    pe.wait_ge(acc_free, j + (8 * part + u + 1))
                                    for half in range(2):
                                        feature_slab(pe, PS[:, u, cols], j * 2, m1 + 2 * u + half, half, x_hi, x_lo, cols)
                                for u in range(2 if rope else 0):
                                    pe.wait_ge(acc_free, j + (8 * part + u + 3))
                                    pe.matmul(PS[:, 2 + u, 0:T], perm, staged[:, u, :], start=True, stop=True)\
                                      .then_inc(permuted, 1)
                        for part, nt in ((2, 4), (3, 2)):
                            for c in range(2):
                                m1 = m0 + 16 * part + 8 * c
                                if part == 2 and c == 1:
                                    pe.wait_ge(acc_free, 18)
                                    if rope:
                                        pe.wait_ge(perm_free, 18)
                                if part == 3:
                                    pe.wait_ge(copied, c + 1)
                                b0 = 4 * ((c + 1) % 2)
                                for g in range(8):
                                    token_slab(pe, [PS[:, b0 + t, :] for t in range(nt)], None, m1 + g, g, x_hi, x_lo)

            def attend_a(q_sb, k_sb, v_sb, g_sb, ph):
                qs = buf("qs_a", [P, 2, T], F, ph)
                ks = buf("ks_a", [P, 2, 2 * T], F, ph)
                pr = [buf(f"pr_a{i}", [P, 2, 512], F, ph) for i in range(2)]
                at_ = buf("at_a", [P, 2, 512], F, ph)
                atT = buf("atT_a", [P, 2, 512], F, ph)
                sm = buf("sm_a", [P, 2, 12], F, ph)
                junk = buf("junk_a", [P, P], F, ph)
                ss = buf("ss", [P, 3, HEADS, TT], F, ph)
                sub_g = buf("sub_g", [P, P], F, ph)
                names = ("head_in", "scores", "mx", "nm", "exps", "recips", "recl", "p1s", "attn", "attnT", "attnT_sb",
                         "pv", "o_out", "o_squared", "sub_g_in", "weighted", "mean", "root", "root_r")
                (head_in, scores, mx, nm, exps, recips, recl, p1s, attn, attnT, attnT_sb, pv, o_out, o_squared, sub_g_in,
                 weighted, mean, root, root_r) = (
                    sem("a_" + x) for x in names)
                with stage() as blk:
                    @blk.gpsimd
                    def _(pool):
                        clear_last_stage(pool)
                        pool.dma_start(sub_g[:, :], bcast(io["subln_g"])).then_inc(sub_g_in, 16)
                        def stage_head(reg, n):
                            pool.tensor_copy(qs[:, n % 2, :], q_sb[:, past(reg, n), :])
                            pool.tensor_copy(ks[:, n % 2, :], k_sb[:, past(reg, n), :]).then_inc(head_in, 1)
                        stage_head(None, 0)
                        stage_head(None, 1)
                        with loop(pool, HEADS - 2, 2) as h:
                            for n in range(2, 4):
                                pool.wait_ge(scores, h * 2 + 2 * (n - 1))
                                stage_head(h, n)
                        pool.wait_ge(sub_g_in, 16)
                        g3 = g_sb[:, :, :].rearrange("p t (h c) -> p (t h) c", c=P)
                        pool.tensor_tensor(g3, g3, sub_g[:, None, :].broadcast_to([P, TT * HEADS, P]), ALU.mult).then_inc(weighted, 1)

                    @blk.tensor
                    def _(pe):
                        def score(reg, e):
                            w, t = e // 2 % 2, e % 2
                            if t == 0:
                                pe.wait_ge(head_in, past(reg, e // 2 + 1))
                            if e >= 2:
                                pe.wait_ge(exps, past(reg, 2 * (e - 2) + 2, 4))
                            for i in range(2):
                                r = slice(64 * i, 64 * i + 64)
                                last = pe.matmul(PS[:, 2 * t + i, :], qs[r, w, t * P:(t + 1) * P], ks[r, w, :],
                                                 start=True, stop=True)
                            last.then_inc(scores, 1)

                        def start():
                            pe.sem_inc(o_out, 2)
                            score(None, 0)
                            score(None, 1)

                        def item(reg, e):
                            t = e % 2
                            pe.wait_ge(attn, past(reg, e + 1, 2))
                            for c in range(4):
                                last = pe.transpose(PS[:, 4 + t, c * P:(c + 1) * P], at_[:, t, c * P:(c + 1) * P], ident)
                            last.then_inc(attnT, 1)
                            if reg is not None or e + 2 < 2 * HEADS:
                                score(reg, e + 2)
                            pe.wait_ge(attnT_sb, past(reg, e + 1, 2))
                            pe.wait_ge(o_out, past(reg, e + 1, 2))
                            for c in range(4):
                                head = e // 2 * P
                                feats = slice(head, head + P) if reg is None else ds(reg * P + head, P)
                                last = pe.matmul(PS[:, 6 + t, 0:P], atT[:, t, c * P:(c + 1) * P], v_sb[:, c, feats],
                                                 start=(c == 0), stop=(c == 3))
                            last.then_inc(pv, 1)
                        pairs(pe, start, item)

                    @blk.vector
                    def _(dve):
                        def maxima(reg, e):
                            t = e % 2
                            dve.wait_ge(scores, past(reg, e + 1, 2))
                            dve.tensor_reduce(sm[:, t, 0:2], PS[:, 2 * t:2 * t + 2, :], X, ALU.max).then_inc(mx, 1)
                            dve.wait_ge(mx, past(reg, e + 1, 2))
                            dve.tensor_scalar(sm[:, t, 2:4], sm[:, t, 0:2], -0.125, None, ALU.mult).then_inc(nm, 1)

                        def weigh(reg, e):
                            t = e % 2
                            dve.wait_ge(exps, past(reg, 2 * e + 2, 4))
                            dve.reciprocal(sm[:, t, 6:8], sm[:, t, 4:6]).then_inc(recips, 1)
                            dve.wait_ge(recips, past(reg, e + 1, 2))
                            dve.tensor_tensor(sm[:, t, 8:9], sm[:, t, 7:8], lam[:, 7:8], ALU.mult).then_inc(recl, 1)
                            dve.wait_ge(recl, past(reg, e + 1, 2))
                            dve.tensor_scalar(pr[t][:, 1, :], pr[t][:, 1, :], sm[:, t, 8:9], None, ALU.mult).then_inc(p1s, 1)
                            dve.wait_ge(p1s, past(reg, e + 1, 2))
                            dve.scalar_tensor_tensor(at_[:, t, :], pr[t][:, 0, :], sm[:, t, 6:7], pr[t][:, 1, :],
                                                     ALU.mult, ALU.add).then_inc(attn, 1)

                        def item(reg, e):
                            if reg is not None or e + 1 < 2 * HEADS:
                                weigh(reg, e + 1)
                            if reg is not None or e + 2 < 2 * HEADS:
                                maxima(reg, e + 2)

                        def start():
                            maxima(None, 0)
                            maxima(None, 1)
                            weigh(None, 0)
                        pairs(dve, start, item)
                        dve.wait_ge(o_squared, 1 + 2 * HEADS)
                        dve.wait_ge(o_out, 2 + 2 * HEADS)
                        part = (1.0 - LAMBDA_INIT) ** 2
                        dve.tensor_scalar(ss[:, 1, :, :], ss[:, 0, :, :], 1.0 / P / part, 1e-5 / part, ALU.mult, ALU.add)\
                           .then_inc(mean, 1)
                        dve.wait_ge(weighted, 1)
                        dve.wait_ge(root, 1)
                        dve.reciprocal(ss[:, 2, :, :], ss[:, 0, :, :]).then_inc(root_r, 1)
                        dve.wait_ge(root_r, 1)
                        for e in range(2 * HEADS):
                            head, t = e // 2, e % 2
                            o = o_a[:, t, head * P:(head + 1) * P]
                            dve.scalar_tensor_tensor(o, o, ss[:, 2, head, t:t + 1], g_sb[:, t, head * P:(head + 1) * P],
                                                     ALU.mult, ALU.mult)

                    @blk.scalar
                    def _(act):
                        act.preload_act_table(ACT.Exp)

                        def exponentials(reg, e):
                            t = e % 2
                            act.wait_ge(nm, past(reg, e + 1, 2))
                            for i in range(2):
                                act.activation(pr[t][:, i, :], PS[:, 2 * t + i, :], ACT.Exp, bias=sm[:, t, 2 + i:3 + i],
                                               scale=0.125, accum_out=sm[:, t, 4 + i:5 + i]).then_inc(exps, 1)

                        def item(reg, e):
                            t = e % 2
                            act.wait_ge(attnT, past(reg, e + 1, 2))
                            act.activation(atT[:, t, :], PS[:, 4 + t, :], ACT.Copy).then_inc(attnT_sb, 1)
                            act.wait_ge(pv, past(reg, e + 1, 2))
                            head = e // 2 * P
                            feats = slice(head, head + P) if reg is None else ds(reg * P + head, P)
                            act.wait_ge(o_squared, past(reg, e + 1, 2))
                            act.activation(junk[:, :], PS[:, 6 + t, 0:P], ACT.Square,
                                           accum_out=ss[:, 0, past(reg, e // 2), t:t + 1]).then_inc(o_squared, 1)
                            act.activation(o_a[:, t, feats], PS[:, 6 + t, 0:P], ACT.Copy).then_inc(o_out, 1)
                            if reg is not None or e + 2 < 2 * HEADS:
                                exponentials(reg, e + 2)

                        def start():
                            exponentials(None, 0)
                            exponentials(None, 1)
                            act.sem_inc(o_squared, 1)
                        pairs(act, start, item)
                        act.wait_ge(mean, 1)
                        act.activation(ss[:, 0, :, :], ss[:, 1, :, :], ACT.Sqrt).then_inc(root, 1)

            def attend_b(q_sb, k_sb, v_sb, g_sb, bias, ph):
                qs = buf("qs_b", [P, 2, T], F, ph)
                sc = buf("sc_b", [P, 2, 512], F, ph)
                at_ = buf("at_b", [P, 2, 512], F, ph)
                atT = buf("atT_b", [P, 2, 512], F, ph)
                sm = buf("sm_b", [P, 2, 4], F, ph)
                names = ("head_in", "scores", "biased", "mx", "exps", "recips", "attnT", "attnT_sb", "pv", "o_out")
                head_in, scores, biased, mx, exps, recips, attnT, attnT_sb, pv, o_out = (
                    sem("b_" + x) for x in names)
                scale = float(P) ** -0.5
                with stage() as blk:
                    @blk.gpsimd
                    def _(pool):
                        clear_last_stage(pool)

                        def stage_head(reg, n):
                            pool.tensor_copy(qs[:, n % 2, :], q_sb[:, past(reg, n), :]).then_inc(head_in, 1)
                        stage_head(None, 0)
                        stage_head(None, 1)
                        with loop(pool, HEADS - 2, 2) as h:
                            for n in range(2, 4):
                                pool.wait_ge(scores, h * 2 + 2 * (n - 1))
                                stage_head(h, n)

                    @blk.tensor
                    def _(pe):
                        def score(reg, e):
                            w, t = e // 2 % 2, e % 2
                            if t == 0:
                                pe.wait_ge(head_in, past(reg, e // 2 + 1))
                            if e >= 2:
                                pe.wait_ge(biased, past(reg, e - 1, 2))
                            pe.matmul(PS[:, t, :], qs[:, w, t * P:(t + 1) * P], k_sb[:, past(reg, e // 2), :],
                                      start=True, stop=True).then_inc(scores, 1)

                        def start():
                            pe.sem_inc(o_out, 2)
                            score(None, 0)
                            score(None, 1)

                        def item(reg, e):
                            t = e % 2
                            pe.wait_ge(exps, past(reg, e + 1, 2))
                            for c in range(4):
                                last = pe.transpose(PS[:, 4 + t, c * P:(c + 1) * P], at_[:, t, c * P:(c + 1) * P], ident)
                            last.then_inc(attnT, 1)
                            if reg is not None or e + 2 < 2 * HEADS:
                                score(reg, e + 2)
                            pe.wait_ge(attnT_sb, past(reg, e + 1, 2))
                            pe.wait_ge(o_out, past(reg, e + 1, 2))
                            for c in range(4):
                                head = e // 2 * P
                                feats = slice(head, head + P) if reg is None else ds(reg * P + head, P)
                                last = pe.matmul(PS[:, 6 + t, 0:P], atT[:, t, c * P:(c + 1) * P], v_sb[:, c, feats],
                                                 start=(c == 0), stop=(c == 3))
                            last.then_inc(pv, 1)
                        pairs(pe, start, item)

                    @blk.vector
                    def _(dve):
                        def add_bias(reg, e):
                            t = e % 2
                            dve.wait_ge(scores, past(reg, e + 1, 2))
                            dve.scalar_tensor_tensor(sc[:, t, 0:T], PS[:, t, 0:T], scale, bias[:, t, past(reg, e // 2), :],
                                                     ALU.mult, ALU.add)
                            dve.tensor_scalar(sc[:, t, T:2 * T], PS[:, t, T:2 * T], scale, None, ALU.mult).then_inc(biased, 1)
                            dve.wait_ge(biased, past(reg, e + 1, 2))
                            dve.tensor_reduce(sm[:, t, 0:1], sc[:, t, :], X, ALU.max, negate=True).then_inc(mx, 1)

                        def item(reg, e):
                            t = e % 2
                            dve.wait_ge(exps, past(reg, e + 1, 2))
                            dve.reciprocal(sm[:, t, 2:3], sm[:, t, 1:2]).then_inc(recips, 1)
                            if reg is not None or e + 2 < 2 * HEADS:
                                add_bias(reg, e + 2)

                        def start():
                            add_bias(None, 0)
                            add_bias(None, 1)
                        pairs(dve, start, item)
                        for t in range(TT):
                            dve.wait_ge(o_out, 2 + 2 * HEADS - 1 + t)
                            dve.tensor_tensor(o_b[:, t, :], o_b[:, t, :], g_sb[:, t, :], ALU.mult)

                    @blk.scalar
                    def _(act):
                        act.preload_act_table(ACT.Exp)

                        def exponential(reg, e):
                            t = e % 2
                            act.wait_ge(mx, past(reg, e + 1, 2))
                            act.activation(at_[:, t, :], sc[:, t, :], ACT.Exp, bias=sm[:, t, 0:1],
                                           accum_out=sm[:, t, 1:2]).then_inc(exps, 1)

                        def item(reg, e):
                            t = e % 2
                            act.wait_ge(attnT, past(reg, e + 1, 2))
                            act.activation(atT[:, t, :], PS[:, 4 + t, :], ACT.Copy).then_inc(attnT_sb, 1)
                            act.wait_ge(pv, past(reg, e + 1, 2))
                            act.wait_ge(recips, past(reg, e + 1, 2))
                            head = e // 2 * P
                            feats = slice(head, head + P) if reg is None else ds(reg * P + head, P)
                            act.activation(o_b[:, t, feats], PS[:, 6 + t, 0:P], ACT.Copy,
                                           scale=sm[:, t, 2:3]).then_inc(o_out, 1)
                            if reg is not None or e + 2 < 2 * HEADS:
                                exponential(reg, e + 2)

                        def start():
                            exponential(None, 0)
                            exponential(None, 1)
                        pairs(act, start, item)

            for n in ("a", "b"):
                with ExitStack() as ph:
                    q_sb = buf(f"q_{n}", [P, HEADS, T], F, ph)
                    k_sb = buf(f"k_{n}", [P, HEADS, 2 * T], F, ph)
                    v_sb = buf(f"v_{n}", [P, 4, WA], F, ph)
                    g_sb = buf(f"g_{n}", [P, TT, WA], F, ph)
                    bias = None
                    if n == "b":
                        bias = buf("bias", [P, TT, HEADS, T], F, ph)
                        bias_in = sem("bias_in")

                    def more_loads(pool):
                        if n == "b":
                            for t in range(TT):
                                for r2 in range(2):
                                    r = 2 * t + r2
                                    pool.dma_start(bias[64 * r2:64 * r2 + 64, t, :, :],
                                                   io["rpb_e"][:, :, (7 - r) * 64:(11 - r) * 64].rearrange("h j c -> j h c"))\
                                        .then_inc(bias_in, 16)
                            pool.wait_ge(bias_in, 64)
                            m = na_mask[:, None, :].broadcast_to([P, 4, 64])
                            for t in range(TT):
                                for h in range(HEADS):
                                    b = bias[:, t, h, :].rearrange("p (r c) -> p r c", c=64)
                                    pool.tensor_tensor(b, b, m, ALU.add)
                    nxt = (src_b, base["b"]) if n == "a" else (src_out, base["out"])
                    with ExitStack() as ph2:
                        project(n, q_sb, k_sb, v_sb, g_sb, n == "a", nxt, ph2, more_loads)
                    with ExitStack() as ph2:
                        if n == "a":
                            attend_a(q_sb, k_sb, v_sb, g_sb, ph2)
                        else:
                            attend_b(q_sb, k_sb, v_sb, g_sb, bias, ph2)
            late.close()
            with ExitStack() as ph:
                oc_hi = buf("oc_hi", [P, KT, T], R, ph)
                oc_lo = buf("oc_lo", [P, KT, T], R, ph)
                gate_b = buf("gate_b", [P, D], F, ph)
                par = [buf(f"par{i}", [P, D], F, ph) for i in range(3)]
                diag = buf("diag", [P, 2, P], F, ph)
                tmp = buf("tmp1", [P, TT, 512], F, ph)
                junk = buf("junk1", [P, D], F, ph)
                tr, rnd, cp, diag_made, gate_mm, gate_out, xin, gated, resid, squared, asked, given, prod = (
                    sem(x + "_1") for x in ("tr", "rnd", "cp", "diag_made", "gate_mm", "gate_out", "xin", "gated", "resid",
                                            "squared", "asked", "given", "prod"))
                m0 = base["out"]
                with stage() as blk:
                    @blk.sync
                    def _(sp):
                        load_slabs(sp, src_out, base["out"], NRAW, N_OUT)
                        load_slabs(sp, src_in2, base["in2"], 0, NRAW)

                    @blk.gpsimd
                    def _(pool):
                        clear_last_stage(pool)
                        pool.dma_start(h_buf[:, :, :], x_tok).then_inc(xin, 16)
                        for i, name in enumerate(("final_g", "ln_in_g", "ln_in_b")):
                            pool.dma_start(par[i][:, :], bcast(io[name])).then_inc(xin, 16)

                    @blk.tensor
                    def _(pe):
                        both = [o_a, o_b]
                        for b in range(KT // 2):
                            if b >= 2:
                                pe.wait_ge(cp, b - 1)
                            for k in range(2):
                                for t in range(TT):
                                    kk = 2 * b + k
                                    src = both[kk // 8][:, t, (kk % 8) * P:(kk % 8 + 1) * P]
                                    last = pe.transpose(PS[:, b % 2, (2 * k + t) * P:(2 * k + t + 1) * P], src, ident)
                            last.then_inc(tr, 1)
                        for b in range(KT):
                            pe.wait_ge(diag_made, b + 1)
                            if b % 4 == 0 and b >= 8:
                                pe.wait_ge(gate_out, b // 4 - 1)
                            pe.matmul(PS[:, 2 + (b // 4) % 2, (b % 4) * P:(b % 4 + 1) * P],
                                      cst[:, C_ONES:C_ONES + P], diag[:, b % 2, :], start=True, stop=True).then_inc(gate_mm, 1)
                        pe.wait_ge(cp, 8)
                        with loop(pe, 4, 2) as c:
                            for u in range(2):
                                pe.wait_ge(gated, c + (u + 1))
                                for g in range(8):
                                    token_slab(pe, [PS[:, 4 + 2 * u + t, :] for t in range(TT)], c * 8, m0 + 8 * u + g, g,
                                               oc_hi, oc_lo)

                    @blk.scalar
                    def _(act):
                        for b in range(KT // 2):
                            act.wait_ge(tr, b + 1)
                            act.activation(oc_hi[:, 2 * b:2 * b + 2, :], PS[:, b % 2, :].rearrange("p (k t) -> p k t", k=2),
                                           ACT.Copy).then_inc(rnd, 1)
                        for q in range(4):
                            act.wait_ge(gate_mm, 4 * q + 4)
                            act.activation(gate_b[:, q * 512:(q + 1) * 512], PS[:, 2 + q % 2, :], ACT.Copy).then_inc(gate_out, 1)
                        with loop(act, N_OUT, NRAW) as i:
                            for s in range(NRAW):
                                round_slab(act, i, m0 + s + 1)

                        def root(n):
                            act.wait_ge(asked, n + 1)
                            act.activation(mv[:, n % TT, 3:4], mv[:, n % TT, 2:3], ACT.Sqrt).then_inc(given, 1)
                        act.preload_act_table(ACT.Sqrt)
                        act.wait_ge(resid, 4)
                        for t in range(TT):
                            if t:
                                act.wait_ge(squared, t)
                            act.activation(junk[:, :], h_buf[:, t, :], ACT.Square, accum_out=mv[:, t, 5:6]).then_inc(squared, 1)
                            root(t)
                        for n in range(TT, 2 * TT):
                            root(n)

                    @blk.vector
                    def _(dve):
                        step = chain(dve, "dve_out1")
                        for b in range(KT // 2):
                            dve.wait_ge(rnd, b + 1)
                            s = slice(2 * b, 2 * b + 2)
                            dve.tensor_tensor(oc_lo[:, s, :], PS[:, b % 2, :].rearrange("p (k t) -> p k t", k=2),
                                              oc_hi[:, s, :].bitcast(F), ALU.subtract).then_inc(cp, 1)
                        mt = modT[:, :].rearrange("p (a w) -> p a w", w=2)
                        for b in range(KT):
                            if b >= 2:
                                dve.wait_ge(gate_mm, b - 1)
                            dve.tensor_scalar(diag[:, b % 2, :], ident, mt[:, 32 + b, 0:1], None, ALU.mult).then_inc(diag_made, 1)
                        dve.sem_inc(gated, 2)
                        dve.wait_ge(gate_out, 4)
                        dve.wait_ge(xin, 64)
                        with loop(dve, 4, 2) as c:
                            for u in range(2):
                                for g in range(8):
                                    split_slab(dve, c * 8, m0 + 8 * u + g + 1)
                                wait_multiplied(dve, c * 8, m0 + 8 * u + 8)
                                for t in range(TT):
                                    i = dve.tensor_tensor(tmp[:, t, :], PS[:, 4 + 2 * u + t, :],
                                                          gate_b[:, ds(c * 512 + u * 512, 512)], ALU.mult)
                                i.then_inc(gated, 1)
                                dve.wait_ge(gated, c + (u + 3))
                                for t in range(TT):
                                    hh = h_buf[:, t, ds(c * 512 + u * 512, 512)]
                                    i = dve.tensor_tensor(hh, hh, tmp[:, t, :], ALU.add)
                                i.then_inc(resid, 1)
                                dve.wait_ge(resid, c + (u + 1))

                        def mean_square(t):
                            dve.wait_ge(squared, t + 1)
                            dve.tensor_scalar(mv[:, t, 2:3], mv[:, t, 5:6], 1.0 / D, 1e-6, ALU.mult, ALU.add).then_inc(asked, 1)

                        def rms_norm(t):
                            dve.wait_ge(given, t + 1)
                            step(dve.reciprocal(mv[:, t, 4:5], mv[:, t, 3:4]))
                            return dve.scalar_tensor_tensor(h_buf[:, t, :], h_buf[:, t, :], mv[:, t, 4:5], par[0][:, :],
                                                            ALU.mult, ALU.mult)
                        mean_square(0)
                        rms_norm(0)
                        mean_square(1)
                        step(rms_norm(1))
                        for t in range(TT):
                            norm_stats(dve, step, h_buf, t, asked)
                        for t in range(TT):
                            norm_apply(dve, step, h_buf, t, given, TT, par[1], par[2])

        second = ExitStack()
        ctx.enter_context(second)

        def buf2(name, shape, dt=F, where=second):
            return where.enter_context(nc.sbuf_tensor(name, shape, dt))

        mix_hi = buf2("mix_hi", [P, KT, T], R)
        mix_lo = buf2("mix_lo", [P, KT, T], R)
        cell = second.enter_context(ExitStack())
        q2 = buf2("q2", [P, HEADS, T], F, cell)
        k2 = buf2("k2", [P, HEADS, T], F, cell)
        v2 = buf2("v2", [P, TT, HEADS, P + 1], F, cell)
        o2 = buf2("o2", [P, TT, WA], F, cell)
        gates = buf2("gates", [P, TT, 16], F, cell)
        with ExitStack() as ph:
            h_hi = buf2("h_hi", [P, KT, T], R, ph)
            h_lo = buf2("h_lo", [P, KT, T], R, ph)
            wg = buf2("wg", [P, KT, 16], F, ph)
            wg_parts = buf2("wg_parts", [P, KT, 32], R, ph)
            wg_hi, wg_lo = wg_parts[:, :, 0:16], wg_parts[:, :, 16:32]
            bg = buf2("bg", [P, 16], F, ph)
            cv = buf2("cv", [P, 4, HEADS], F, ph)
            c_sb = buf2("c_sb", [P, 2, T], F, ph)
            z = buf2("z", [P, 2, T + 2], F, ph)
            yc = buf2("yc", [P, 2, 2, T], F, ph)
            tr, rnd, cp, par_in, wg_round, wg_split, gates_done, zeroed, c_copied, conv, conv_free, acc_free, vo_free = (
                sem(x + "_2") for x in ("tr", "rnd", "cp", "par_in", "wg_round", "wg_split", "gates_done", "zeroed", "c_copied",
                                        "conv", "conv_free", "acc_free", "vo_free"))
            m0 = base["in2"]
            with stage() as blk:
                @blk.sync
                def _(sp):
                    load_slabs(sp, src_in2, base["in2"], NRAW, N_WIN2)
                    load_slabs(sp, src_out2, base["out2"], 0, NRAW)

                @blk.gpsimd
                def _(pool):
                    clear_last_stage(pool)
                    pool.dma_start(cv[:, :, :].rearrange("p a b -> p (a b)"), io["conv_cols"]).then_inc(par_in, 16)
                    pool.dma_start(wg[:, :, :].rearrange("p a b -> p (a b)"), io["w_gate_cols"]).then_inc(par_in, 16)
                    pool.dma_start(bg[:, :], bcast(io["b_gate"])).then_inc(par_in, 16)
                    pool.memset(z[:, :, 0:2], 0.0)
                    pool.memset(v2[:, :, :, P:P + 1], 1.0).then_inc(zeroed, 1)

                @blk.tensor
                def _(pe):
                    transpose_in(pe, h_buf, None, cp, tr, banks=(6, 7))
                    pe.wait_ge(cp, 8)
                    with loop(pe, HEADS, 2) as j:
                        for u in range(2):
                            pe.wait_ge(conv_free, j * 3 + (3 * u + 3))
                            for part in range(3):
                                for half in range(2):
                                    feature_slab(pe, PS[:, 3 * u + part, 0:T], j * 6, m0 + 6 * u + 2 * part + half, half,
                                                 h_hi, h_lo, slice(0, T))
                    with loop(pe, 2 * HEADS, 2) as j:
                        for u in range(2):
                            pe.wait_ge(acc_free, j + (u + 1))
                            for half in range(2):
                                feature_slab(pe, PS[:, 6 + u, 0:T], j * 2, m0 + 48 + 2 * u + half, half, h_hi, h_lo, slice(0, T))
                    pe.wait_ge(acc_free, 2 * HEADS + 1)
                    pe.wait_ge(wg_split, 1)
                    for t in range(TT):
                        tok = slice(t * P, (t + 1) * P)
                        for k in range(KT):
                            at = t * 32

                            def both():
                                return pe.matmul(PS[:, 6, at:at + 32], h_hi[:, k, tok], wg_parts[:, k, :], start=(k == 0),
                                                 stop=(k == KT - 1))
                            if k == 0:
                                both()
                            pe.matmul(PS[:, 6, at:at + 16], h_lo[:, k, tok], wg_hi[:, k, :], start=False, stop=False)
                            if k:
                                last = both()
                    last.then_inc(gates_done, 1)
                    pe.wait_ge(conv_free, 6 + 3 * HEADS)
                    for c in range(4):
                        if c >= 2:
                            pe.wait_ge(vo_free, c - 1)
                        for g in range(8):
                            token_slab(pe, [PS[:, 2 * (c % 2) + t, :] for t in range(TT)], None, m0 + 80 + 8 * c + g, g, h_hi, h_lo)

                @blk.scalar
                def _(act):
                    transposed_round(act, tr, h_hi, rnd, banks=(6, 7))
                    act.sem_inc(acc_free, 2)
                    act.wait_ge(par_in, 48)
                    act.activation(wg_hi[:, :, :], wg[:, :, :], ACT.Copy).then_inc(wg_round, 1)
                    with loop(act, HEADS, 2) as j:
                        for u in range(2):
                            for s in range(6):
                                round_slab(act, j * 6, m0 + 6 * u + s + 1)
                            wait_multiplied(act, j * 6, m0 + 6 * u + 4)
                            act.wait_ge(conv_free, j * 3 + (3 * u + 3))
                            act.activation(c_sb[:, u, :], PS[:, 3 * u + 1, 0:T], ACT.Copy).then_inc(c_copied, 1)
                    for part, dst in ((0, q2), (1, k2)):
                        with loop(act, HEADS, 2) as j:
                            for u in range(2):
                                for s in range(2):
                                    round_slab(act, j * 2, m0 + 48 + 16 * part + 2 * u + s + 1)
                                wait_multiplied(act, j * 2, m0 + 48 + 16 * part + 2 * u + 2)
                                act.activation(dst[:, j + u, :], PS[:, 6 + u, 0:T], ACT.Copy).then_inc(acc_free, 1)
                    for c in range(4):
                        m1 = m0 + 80 + 8 * c
                        for g in range(8):
                            round_slab(act, None, m1 + g + 1)
                        wait_multiplied(act, None, m1 + 8)
                        if c < 2:
                            act.wait_ge(zeroed, 1)
                        for t in range(TT):
                            if c < 2:
                                i = act.activation(v2[:, t, 4 * c:4 * c + 4, 0:P],
                                                   PS[:, 2 * (c % 2) + t, :].rearrange("p (h e) -> p h e", h=4), ACT.Copy)
                            else:
                                i = act.activation(o2[:, t, (c - 2) * 512:(c - 1) * 512], PS[:, 2 * (c % 2) + t, :], ACT.Sigmoid)
                        i.then_inc(vo_free, 1)

                @blk.vector
                def _(dve):
                    step = chain(dve, "dve_in2")
                    transposed_split(dve, h_hi, h_lo, rnd, cp, banks=(6, 7))
                    dve.wait_ge(wg_round, 1)
                    dve.tensor_tensor(wg_lo[:, :, :], wg[:, :, :], wg_hi[:, :, :].bitcast(F), ALU.subtract).then_inc(wg_split, 1)
                    dve.sem_inc(conv_free, 6)
                    dve.wait_ge(zeroed, 1)
                    split_slab(dve, None, m0 + 1)
                    with loop(dve, HEADS, 2) as j:
                        for u in range(2):
                            for s in range(6):
                                split_slab(dve, j * 6, m0 + 6 * u + s + 2)
                            dve.wait_ge(c_copied, j + (u + 1))
                            wait_multiplied(dve, j * 6, m0 + 6 * u + 6)
                            y = yc[:, u, 0, :]

                            def tap(n):
                                return cv[:, n, ds(j + u, 1)]
                            n = 6 * u
                            dve.tensor_tensor(z[:, u, 2:T + 2], c_sb[:, u, :], PS[:, 3 * u + 2, 0:T], ALU.mult).then_inc(conv, 1)
                            dve.wait_ge(conv, j * 6 + (n + 1))
                            dve.tensor_scalar(y, z[:, u, 2:T + 2], tap(2), tap(3), ALU.mult, ALU.add).then_inc(conv, 1)
                            dve.wait_ge(conv, j * 6 + (n + 2))
                            dve.scalar_tensor_tensor(y, z[:, u, 1:T + 1], tap(1), y, ALU.mult, ALU.add).then_inc(conv, 1)
                            dve.wait_ge(conv, j * 6 + (n + 3))
                            dve.scalar_tensor_tensor(y, z[:, u, 0:T], tap(0), y, ALU.mult, ALU.add).then_inc(conv, 1)
                            dve.wait_ge(conv, j * 6 + (n + 4))
                            dve.tensor_tensor(yc[:, u, 1, :], y, PS[:, 3 * u, 0:T], ALU.mult).then_inc(conv, 1)
                            dve.wait_ge(conv, j * 6 + (n + 5))
                            dve.tensor_copy(mix_hi[:, j + u, :], yc[:, u, 1, :]).then_inc(conv, 1)
                            dve.wait_ge(conv, j * 6 + (n + 6))
                            dve.tensor_tensor(mix_lo[:, j + u, :], yc[:, u, 1, :], mix_hi[:, j + u, :].bitcast(F), ALU.subtract)\
                               .then_inc(conv_free, 3)
                    with loop(dve, 32, NRAW) as i:
                        for s in range(NRAW):
                            split_slab(dve, i, m0 + 48 + s + 2)
                    dve.wait_ge(gates_done, 1)
                    for t in range(TT):
                        i = dve.tensor_tensor(gates[:, t, :], PS[:, 6, t * 32:t * 32 + 16], bg[:, :], ALU.add)
                    step(i)
                    for t in range(TT):
                        dve.tensor_tensor(gates[:, t, :], gates[:, t, :], PS[:, 6, t * 32 + 16:t * 32 + 32], ALU.add)
                    with loop(dve, 28, NRAW) as i:
                        for s in range(NRAW):
                            split_slab(dve, i, m0 + 80 + s + 2)
                    for s in range(28, 31):
                        split_slab(dve, None, m0 + 80 + s + 2)

        with ExitStack() as ph:
            lg = buf2("lg", [P, TT, 5, HEADS], F, ph)
            row = buf2("row", [HEADS, 8, T], F, ph)
            neg = buf2("neg", [HEADS, HEADS, T], F, ph)
            colb = buf2("colb", [P, TT, 2, HEADS], F, ph)
            qk = buf2("qk", [P, 2, 2, T], F, ph)
            ee = buf2("ee", [P, 2, 3, P], F, ph)
            ss = buf2("ss2", [P, 2, 3, P], F, ph)
            num = buf2("num", [P, 2, TT, P + 1], F, ph)
            den = buf2("den", [P, 2, 3, TT], F, ph)
            hm = buf2("hm", [P, TT, HEADS, P], F, ph)
            eye8 = buf2("eye8", [HEADS, HEADS], F, ph)
            mh_g = buf2("mh_g", [P, WA], F, ph)
            st = buf2("st", [P, TT, HEADS, 6], F, ph)
            hv = buf2("hv", [P, TT * HEADS, 6], F, ph)
            (g_abs, g_exp, g_ln, g_dve, g_tr, g_rows, g_b, g_em, g_trb, g_col, par_in, head_in, scores, tri, exps, wts, nums,
             num_sb, dens, hms, o_gate, centred, asked, given, ymr, tr, rnd, cp, neg_made) = (
                sem(x + "_3") for x in ("g_abs", "g_exp", "g_ln", "g_dve", "g_tr", "g_rows", "g_b", "g_em", "g_trb", "g_col",
                                        "par_in", "head_in", "scores", "tri", "exps", "wts", "nums", "num_sb", "dens",
                                        "hms", "o_gate", "centred", "asked", "given", "ymr", "tr", "rnd", "cp", "neg_made"))
            scale = float(P) ** -0.5
            with stage() as blk:
                @blk.gpsimd
                def _(pool):
                    clear_last_stage(pool)
                    pool.dma_start(eye8[:, :], io["consts"][0:HEADS, C_EYE8:C_EYE8 + HEADS]).then_inc(par_in, 16)
                    pool.dma_start(mh_g[:, :], bcast(io["mh_g"])).then_inc(par_in, 16)

                    def stage_head(reg, n):
                        pool.tensor_copy(qk[:, n % 2, 0, :], q2[:, past(reg, n), :])
                        pool.tensor_copy(qk[:, n % 2, 1, :], k2[:, past(reg, n), :]).then_inc(head_in, 1)
                    stage_head(None, 0)
                    stage_head(None, 1)
                    pool.wait_ge(par_in, 32)
                    pool.tensor_tensor(o2[:, :, :], o2[:, :, :], mh_g[:, None, :].broadcast_to([P, TT, WA]), ALU.mult)\
                        .then_inc(o_gate, 1)
                    with loop(pool, HEADS - 2, 2) as h:
                        for n in range(2, 4):
                            pool.wait_ge(scores, h + (n - 1))
                            stage_head(h, n)

                @blk.scalar
                def _(act):
                    act.preload_act_table_set("natural_log_exp_and_others")
                    act.wait_ge(g_abs, 1)
                    act.activation(lg[:, :, 2, :], lg[:, :, 1, :], ACT.Exp).then_inc(g_exp, 1)
                    act.wait_ge(g_exp, 1)
                    act.activation(lg[:, :, 3, :], lg[:, :, 2, :], ACT.Ln, bias=cst[:, C_ONES:C_ONES + 1]).then_inc(g_ln, 1)
                    act.wait_ge(g_tr, 1)
                    act.activation(row[:, 0:2, :], PS[0:HEADS, 7, :].rearrange("p (a t) -> p a t", a=2), ACT.Copy).then_inc(g_rows, 1)
                    act.wait_ge(g_b, 1)
                    act.activation(row[:, 6, :], row[:, 6, :], ACT.Exp, scale=-1.0).then_inc(g_em, 1)
                    act.wait_ge(g_trb, 1)
                    act.activation(colb[:, :, :, :].rearrange("p t a h -> p (t a h)"), PS[:, 7, 0:32], ACT.Copy).then_inc(g_col, 1)
                    act.wait_ge(g_col, 1)

                    def exponentials(reg, e):
                        w = e % 2
                        act.wait_ge(tri, past(reg, e + 1))
                        head = slice(e, e + 1) if reg is None else ds(reg + e, 1)
                        a0, a1 = colb[:, 0, 0, head], colb[:, 1, 0, head]
                        act.activation(ee[:, w, 0, :], ee[:, w, 0, :], ACT.Exp, bias=a0)
                        act.activation(ee[:, w, 1, :], PS[:, 2 + w, P:T], ACT.Exp, bias=a0)
                        act.activation(ee[:, w, 2, :], ee[:, w, 2, :], ACT.Exp, bias=a1).then_inc(exps, 1)

                    def item(reg, e):
                        w = e % 2
                        act.wait_ge(nums, past(reg, e + 1))
                        act.activation(num[:, w, :, :], PS[:, 4 + w, 0:2 * (P + 1)].rearrange("p (t e) -> p t e", t=2),
                                       ACT.Copy).then_inc(num_sb, 1)
                        if reg is not None or e + 2 < HEADS:
                            exponentials(reg, e + 2)

                    def start():
                        exponentials(None, 0)
                        exponentials(None, 1)
                    pairs(act, start, item, HEADS)
                    act.wait_ge(asked, 1)
                    act.activation(hv[:, :, 3], hv[:, :, 2], ACT.Sqrt).then_inc(given, 1)
                    for b in range(4):
                        act.wait_ge(tr, b + 1)
                        act.activation(mix_hi[:, 8 + 2 * b:10 + 2 * b, :], PS[:, b % 2, :].rearrange("p (k t) -> p k t", k=2),
                                       ACT.Copy).then_inc(rnd, 1)

                @blk.tensor
                def _(pe):
                    pe.wait_ge(g_dve, 1)
                    for a in range(2):
                        for t in range(TT):
                            last = pe.transpose(PS[0:HEADS, 7, a * T + t * P:a * T + (t + 1) * P], lg[:, t, 4 * a, :], ident)
                    last.then_inc(g_tr, 1)
                    pe.wait_ge(g_em, 1)
                    pe.wait_ge(par_in, 32)
                    for t in range(TT):
                        for a, r in ((0, 3), (1, 6)):
                            last = pe.transpose(PS[:, 7, (2 * t + a) * HEADS:(2 * t + a + 1) * HEADS],
                                                row[:, r, t * P:(t + 1) * P], eye8[:, :])
                    last.then_inc(g_trb, 1)
                    pe.wait_ge(g_col, 1)
                    pe.wait_ge(neg_made, 1)

                    def score(reg, e):
                        w = e % 2
                        pe.wait_ge(head_in, past(reg, e + 1))
                        q, k = qk[:, w, 0, :], qk[:, w, 1, :]
                        pe.matmul(PS[:, w, 0:T], k[:, 0:P], q, start=True, stop=True)
                        pe.matmul(PS[:, w, T:T + P], k[:, P:T], q[:, P:T], start=True, stop=True)
                        pe.matmul(PS[:, 2 + w, 0:T], cst[0:HEADS, C_ONES:C_ONES + P], neg[:, past(reg, e), :],
                                  start=True, stop=True).then_inc(scores, 1)

                    def item(reg, e):
                        w = e % 2
                        pe.wait_ge(wts, past(reg, e + 1))
                        if reg is not None or e + 2 < HEADS:
                            score(reg, e + 2)
                        pe.wait_ge(hms, past(reg, e + 1))
                        v0, v1 = v2[:, 0, past(reg, e), :], v2[:, 1, past(reg, e), :]
                        pe.matmul(PS[:, 4 + w, 0:P + 1], ss[:, w, 0, :], v0, start=True, stop=True)
                        pe.matmul(PS[:, 4 + w, P + 1:2 * P + 2], ss[:, w, 1, :], v0, start=True, stop=False)
                        pe.matmul(PS[:, 4 + w, P + 1:2 * P + 2], ss[:, w, 2, :], v1, start=False, stop=True).then_inc(nums, 1)

                    def start():
                        pe.sem_inc(hms, 2)
                        score(None, 0)
                        score(None, 1)
                    pairs(pe, start, item, HEADS)
                    for b in range(4):
                        pe.wait_ge(ymr, 1)
                        if b >= 2:
                            pe.wait_ge(cp, b - 1)
                        for k in range(2):
                            for t in range(TT):
                                last = pe.transpose(PS[:, b % 2, (2 * k + t) * P:(2 * k + t + 1) * P],
                                                    hm[:, t, 2 * b + k, :], ident)
                        last.then_inc(tr, 1)

                @blk.vector
                def _(dve):
                    step = chain(dve, "dve_cell")
                    gi, gf = gates[:, :, 0:HEADS], gates[:, :, HEADS:16]
                    step(dve.tensor_scalar(lg[:, :, 1, :], gf, -1.0, None, ALU.mult))
                    step(dve.tensor_tensor(lg[:, :, 1, :], lg[:, :, 1, :], gf, ALU.min))
                    dve.tensor_copy(lg[:, :, 0, :], gi).then_inc(g_abs, 1)
                    dve.wait_ge(g_ln, 1)
                    step(dve.tensor_scalar(lg[:, :, 4, :], gf, 0.0, None, ALU.min))
                    dve.tensor_tensor(lg[:, :, 4, :], lg[:, :, 4, :], lg[:, :, 3, :], ALU.subtract).then_inc(g_dve, 1)
                    step(dve.memset(row[:, 7, :], 1.0))
                    dve.wait_ge(g_rows, 1)
                    one = row[:, 7, :]
                    step(dve.tensor_tensor_scan(row[:, 2, :], one, row[:, 1, :], 0.0, ALU.mult, ALU.add))
                    step(dve.tensor_tensor(row[:, 3, :], row[:, 0, :], row[:, 2, :], ALU.subtract))
                    step(dve.tensor_tensor_scan(row[:, 4, :], one, row[:, 3, :], 0.0, ALU.mult, ALU.max))
                    step(dve.tensor_scalar(row[:, 5, :], row[:, 4, :], -1.0, None, ALU.mult))
                    dve.tensor_tensor(row[:, 6, :], row[:, 4, :], row[:, 2, :], ALU.add).then_inc(g_b, 1)
                    dve.wait_ge(par_in, 32)
                    for h in range(HEADS):
                        i = dve.tensor_scalar(neg[:, h, :], row[:, 5, :], eye8[:, h:h + 1], None, ALU.mult)
                    i.then_inc(neg_made, 1)
                    dve.wait_ge(g_col, 1)
                    tri_m = cst[:, C_TRI:C_TRI + P]

                    def mask(reg, e):
                        w = e % 2
                        dve.wait_ge(scores, past(reg, e + 1))
                        dve.tensor_tensor(ee[:, w, 0, :], PS[:, 2 + w, 0:P], tri_m, ALU.add)
                        dve.tensor_tensor(ee[:, w, 2, :], PS[:, 2 + w, P:T], tri_m, ALU.add).then_inc(tri, 1)

                    def weigh(reg, e):
                        w = e % 2
                        dve.wait_ge(exps, past(reg, e + 1))
                        dve.scalar_tensor_tensor(ss[:, w, :, :].rearrange("p b t -> p (b t)"), PS[:, w, 0:3 * P], scale,
                                                 ee[:, w, :, :].rearrange("p b t -> p (b t)"), ALU.mult, ALU.mult).then_inc(wts, 1)

                    def item(reg, e):
                        w = e % 2
                        if reg is not None or e + 1 < HEADS:
                            weigh(reg, e + 1)
                        if reg is not None or e + 2 < HEADS:
                            mask(reg, e + 2)
                        dve.wait_ge(num_sb, past(reg, e + 1))
                        d = num[:, w, :, P]
                        dve.scalar_tensor_tensor(den[:, w, 0, :], d, -1.0, d, ALU.mult, ALU.max).then_inc(dens, 1)
                        dve.wait_ge(dens, past(reg, 3 * e + 1, 3))
                        head = slice(e, e + 1) if reg is None else ds(reg + e, 1)
                        dve.tensor_tensor(den[:, w, 1, :], den[:, w, 0, :], colb[:, :, 1, head].rearrange("p t o -> p (t o)"),
                                          ALU.max).then_inc(dens, 1)
                        dve.wait_ge(dens, past(reg, 3 * e + 2, 3))
                        dve.reciprocal(den[:, w, 2, :], den[:, w, 1, :]).then_inc(dens, 1)
                        dve.wait_ge(dens, past(reg, 3 * e + 3, 3))
                        for t in range(TT):
                            i = dve.tensor_scalar(hm[:, t, past(reg, e), :], num[:, w, t, 0:P], den[:, w, 2, t:t + 1], None, ALU.mult)
                        i.then_inc(hms, 1)

                    def start():
                        mask(None, 0)
                        mask(None, 1)
                        weigh(None, 0)
                    pairs(dve, start, item, HEADS)
                    dve.wait_ge(hms, 2 + HEADS)
                    for t in range(TT):
                        for h in range(HEADS):
                            i = dve.bn_stats(st[:, t, h, :], hm[:, t, h, :])
                    step(i)
                    for n in range(TT * HEADS):
                        i = dve.bn_aggr(hv[:, n, 0:2], st[:, n // HEADS, n % HEADS, :])
                    step(i)
                    dve.tensor_scalar(hv[:, :, 2], hv[:, :, 1], 1e-5, None, ALU.add).then_inc(asked, 1)
                    dve.wait_ge(given, 1)
                    step(dve.reciprocal(hv[:, :, 4], hv[:, :, 3]))
                    dve.wait_ge(o_gate, 1)
                    for n in range(TT * HEADS):
                        hh, gate = hm[:, n // HEADS, n % HEADS, :], o2[:, n // HEADS, n % HEADS * P:(n % HEADS + 1) * P]
                        dve.scalar_tensor_tensor(hh, hh, hv[:, n, 0:1], gate, ALU.subtract, ALU.mult).then_inc(centred, 1)
                    for n in range(TT * HEADS):
                        hh = hm[:, n // HEADS, n % HEADS, :]
                        dve.wait_ge(centred, n + 1)
                        i = dve.tensor_scalar(hh, hh, hv[:, n, 4:5], None, ALU.mult)
                    i.then_inc(ymr, 1)
                    for b in range(4):
                        dve.wait_ge(rnd, b + 1)
                        s = slice(8 + 2 * b, 10 + 2 * b)
                        dve.tensor_tensor(mix_lo[:, s, :], PS[:, b % 2, :].rearrange("p (k t) -> p k t", k=2),
                                          mix_hi[:, s, :].bitcast(F), ALU.subtract).then_inc(cp, 1)
        cell.close()

        with ExitStack() as ph:
            par = [buf2(f"parb{i}", [P, D], F, ph) for i in range(2)]
            par_in, acc_free, resid, asked, given, ready = (
                sem(x + "_4") for x in ("par_in", "acc_free", "resid", "asked", "given", "ready"))
            m0 = base["out2"]
            with stage() as blk:
                @blk.sync
                def _(sp):
                    load_slabs(sp, src_out2, base["out2"], NRAW, N_OUT2)
                    load_slabs(sp, src_wq, base["wq"], 0, NRAW)
                    sp.wait_ge(ready, 2)
                    sp.dma_start(h_dram, h_buf[:, :, :]).then_inc(h_stored, 16)

                @blk.gpsimd
                def _(pool):
                    clear_last_stage(pool)
                    for i, name in enumerate(("ln1_g", "ln1_b")):
                        pool.dma_start(par[i][:, :], bcast(io[name])).then_inc(par_in, 16)

                @blk.tensor
                def _(pe):
                    with loop(pe, 4, 2) as c:
                        for u in range(2):
                            pe.wait_ge(acc_free, c + (u + 1))
                            for g in range(8):
                                token_slab(pe, [PS[:, 2 * u + t, :] for t in range(TT)], c * 8, m0 + 8 * u + g, g, mix_hi, mix_lo)

                @blk.scalar
                def _(act):
                    with loop(act, N_OUT2, NRAW) as i:
                        for s in range(NRAW):
                            round_slab(act, i, m0 + s + 1)
                    for t in range(TT):
                        act.wait_ge(asked, t + 1)
                        act.activation(mv[:, t, 3:4], mv[:, t, 2:3], ACT.Sqrt).then_inc(given, 1)

                @blk.vector
                def _(dve):
                    step = chain(dve, "dve_out2")
                    dve.sem_inc(acc_free, 2)
                    with loop(dve, 4, 2) as c:
                        for u in range(2):
                            for g in range(8):
                                split_slab(dve, c * 8, m0 + 8 * u + g + 1)
                            wait_multiplied(dve, c * 8, m0 + 8 * u + 8)
                            for t in range(TT):
                                hh = h_buf[:, t, ds(c * 512 + u * 512, 512)]
                                i = dve.scalar_tensor_tensor(hh, hh, ALPHA, PS[:, 2 * u + t, :], ALU.mult, ALU.add)
                            i.then_inc(acc_free, 1)
                    dve.wait_ge(acc_free, 6)
                    dve.wait_ge(par_in, 32)
                    for t in range(TT):
                        norm_stats(dve, step, h_buf, t, asked)
                    for t in range(TT):
                        norm_apply(dve, step, h_buf, t, given, 0, par[0], par[1]).then_inc(ready, 1)
        second.close()

        top = ExitStack()
        ctx.enter_context(top)

        def buf3(name, shape, dt=F, where=top):
            return where.enter_context(nc.sbuf_tensor(name, shape, dt))
        pick_at = nc.sbuf_base
        pick = buf3("pick", [P, 3, T])
        hT = top.enter_context(ExitStack())
        h_hi_at = nc.sbuf_base
        h_hi = buf3("h2_hi", [P, KT, T], R, hT)
        h_lo = buf3("h2_lo", [P, KT, T], R, hT)

        wt_at = nc.sbuf_base
        wt = buf3("wt", [P, N_KEYS, T])

        def top_step(dve, k, src, n, tk, count):
            dve.wait_ge(tk, count)
            carry(dve)
            for t in range(TT):
                if k == 0:
                    i = dve.max(t8[:, t, 0:8], src[t])
                elif k == 1:
                    dve.max_index(i8[:, t, 0:8], t8[:, t, 0:8], src[t])
                    i = dve.match_replace(rest[:, t, 0:n], t8[:, t, 0:8], src[t], -3.0e38)
                elif k == 2:
                    i = dve.max(t8[:, t, 8:16], rest[:, t, 0:n])
                else:
                    i = dve.max_index(i8[:, t, 8:16], t8[:, t, 8:16], rest[:, t, 0:n])
            i.then_inc(tk, 1)

        with ExitStack() as ph:
            sv = nc.alloc_sbuf_tensor_at("sv", [P, TT, 2 * HEADS, TOPK], F, offset=pick_at)
            si = buf3("si", [P, TT, 2 * HEADS, TOPK], F, ph)
            gt = buf3("gt", [P, TT, HEADS, TOPK], F, ph)
            gs = buf3("gs", [P, TT, HEADS, 2], F, ph)
            eid = buf3("eid", [P, TT, 2, HEADS, TOPK], F, ph)
            t8 = buf3("t8", [P, TT, TOPK], F, ph)
            i8 = buf3("i8", [P, TT, TOPK], U32, ph)
            eq = buf3("eq", [P, TT, 2, 256], F, ph)
            rest, cand = eq[:, :, 0, :], eq[:, :, 1, :]
            abu = buf3("abu", [P, TT, 2, TOPK], U32, ph)
            abf = buf3("abf", [P, TT, 2, TOPK], F, ph)

            keys = nc.alloc_sbuf_tensor_at("keys", [P, 2 * HEADS, N_KEYS], F, offset=wt_at)
            qp = nc.alloc_sbuf_tensor_at("qp", [P, 2, T], F, offset=wt_at + 2 * HEADS * N_KEYS * 4)
            tr, rnd, cp, keys_in, acc_free, s_done, s_free, tk = (
                sem(x + "_5") for x in ("tr", "rnd", "cp", "keys_in", "acc_free", "s_done", "s_free", "tk"))
            m0 = base["wq"]
            with stage() as blk:
                @blk.sync
                def _(sp):
                    sp.dma_start(keys[:, :, :], io["keys"]).then_inc(keys_in, 16)
                    load_slabs(sp, src_wq, base["wq"], NRAW, N_WQ)
                    load_slabs(sp, src_u, base["u"], 0, NRAW)

                @blk.gpsimd
                def _(pool):
                    clear_last_stage(pool)

                @blk.tensor
                def _(pe):
                    transpose_in(pe, h_buf, None, cp, tr, banks=(0, 1))
                    pe.wait_ge(cp, 8)

                    def query(reg, n):
                        r2 = None if reg is None else reg * 2
                        pe.wait_ge(acc_free, n + 1 if reg is None else reg + (n + 1))
                        for half in range(2):
                            feature_slab(pe, PS[:, 2 + n % 2, 0:T], r2, m0 + 2 * n + half, half, h_hi, h_lo, slice(0, T))

                    def score(reg, n):
                        pe.wait_ge(acc_free, n + 3 if reg is None else reg + (n + 3))
                        pe.wait_ge(s_free, n + 1 if reg is None else reg + (n + 1))
                        for t in range(TT):
                            last = pe.matmul(PS[:, 4 + n % 2, t * N_KEYS:(t + 1) * N_KEYS], qp[:, n % 2, t * P:(t + 1) * P],
                                             keys[:, n if reg is None else reg + n, :], start=True, stop=True)
                        last.then_inc(s_done, 1)
                    query(None, 0)
                    query(None, 1)
                    pe.wait_ge(keys_in, 16)
                    score(None, 0)
                    with loop(pe, 2 * HEADS - 2, 2) as j:
                        for u in range(2):
                            query(j, 2 + u)
                            score(j, 1 + u)
                    score(None, 2 * HEADS - 1)

                @blk.scalar
                def _(act):
                    transposed_round(act, tr, h_hi, rnd, banks=(0, 1))
                    act.sem_inc(acc_free, 2)
                    with loop(act, 2 * HEADS, 2) as j:
                        for u in range(2):
                            for s in range(2):
                                round_slab(act, j * 2, m0 + 2 * u + s + 1)
                            wait_multiplied(act, j * 2, m0 + 2 * u + 2)
                            act.activation(qp[:, u, :], PS[:, 2 + u, 0:T], ACT.Copy).then_inc(acc_free, 1)

                @blk.vector
                def _(dve):
                    transposed_split(dve, h_hi, h_lo, rnd, cp, banks=(0, 1))
                    dve.sem_inc(s_free, 2)
                    dve.sem_inc(tk, 1)
                    dve.wait_ge(h_stored, 16)
                    for s in range(4):
                        split_slab(dve, None, m0 + s + 1)

                    def rank(reg, n):
                        r2 = None if reg is None else reg * 2
                        done = 5 * n + 1 if reg is None else reg * 5 + (5 * n + 1)
                        src = [PS[:, 4 + n % 2, t * N_KEYS:(t + 1) * N_KEYS] for t in range(TT)]
                        if reg is not None:
                            split_slab(dve, r2, m0 + 2 * n + 5)
                        dve.wait_ge(s_done, n + 1 if reg is None else reg + (n + 1))
                        top_step(dve, 0, src, N_KEYS, tk, done)
                        top_step(dve, 1, src, N_KEYS, tk, done + 1)
                        if reg is not None:
                            split_slab(dve, r2, m0 + 2 * n + 6)
                        top_step(dve, 2, src, N_KEYS, tk, done + 2)
                        dve.sem_inc(s_free, 1)
                        top_step(dve, 3, src, N_KEYS, tk, done + 3)
                        dve.wait_ge(tk, done + 4)
                        at = n if reg is None else reg + n
                        dve.tensor_copy(sv[:, :, at, :], t8[:, :, :])
                        dve.tensor_copy(si[:, :, at, :], i8[:, :, :]).then_inc(tk, 1)
                    with loop(dve, 2 * HEADS - 2, 2) as j:
                        for u in range(2):
                            rank(j, u)
                    for n in range(2 * HEADS - 2, 2 * HEADS):
                        rank(None, n)
                    dve.wait_ge(tk, 5 * 2 * HEADS + 1)

            tk, sh, g_exp, g_ready, p_tr, acc_free = (
                sem(x + "_u") for x in ("tk", "sh", "g_exp", "g_ready", "p_tr", "acc_free"))
            m0 = base["u"]
            HEAD_SLABS = 8
            J1 = HEADS * HEAD_SLABS // 2
            J2 = J1 + 2
            with stage() as blk:
                @blk.sync
                def _(sp):
                    load_slabs(sp, src_u, base["u"], NRAW, N_U)
                    load_slabs(sp, src_v, base["v"], 0, NRAW)

                @blk.gpsimd
                def _(pool):
                    clear_last_stage(pool)

                @blk.tensor
                def _(pe):
                    def experts(reg, j):
                        pe.wait_ge(acc_free, j + 1 if reg is None else reg + (j + 1))
                        r2 = None if reg is None else reg * 2
                        for half in range(2):
                            feature_slab(pe, PS[:, j % 2, 0:T], r2, m0 + 2 * j + half, half, h_hi, h_lo, slice(0, T))
                    with loop(pe, J1, 2) as j:
                        for u in range(2):
                            experts(j, u)
                    for j in range(J1, J2):
                        experts(None, j)
                    pe.wait_ge(g_ready, 1)
                    for a in range(3):
                        for t in range(TT):
                            src = gt[:, t, :, :] if a == 2 else eid[:, t, a, :, :]
                            last = pe.transpose(PS[:, 2 + a, t * P:(t + 1) * P], src.rearrange("p h k -> p (h k)"), ident)
                    last.then_inc(p_tr, 1)
                    with loop(pe, N_KEYS - J2, 2) as j:
                        for u in range(2):
                            experts(j, J2 + u)

                @blk.scalar
                def _(act):
                    def activate(reg, j):
                        r2 = None if reg is None else reg * 2
                        wait_multiplied(act, r2, m0 + 2 * j + 2)
                        act.activation(wt[:, j if reg is None else reg + j, :], PS[:, j % 2, 0:T], ACT.Gelu).then_inc(acc_free, 1)
                    act.preload_act_table(ACT.Gelu)
                    act.sem_inc(acc_free, 2)
                    with loop(act, J1, 2) as j:
                        for u in range(2):
                            for s in range(2):
                                round_slab(act, j * 2, m0 + 2 * u + s + 1)
                            activate(j, u)
                    for j in range(J1, J2):
                        for s in range(2):
                            round_slab(act, None, m0 + 2 * j + s + 1)
                        if j == J1:
                            act.wait_ge(sh, 1)
                            act.activation(gt[:, :, :, :], gt[:, :, :, :], ACT.Exp).then_inc(g_exp, 1)
                        activate(None, j)
                    act.wait_ge(p_tr, 1)
                    act.activation(pick[:, :, :], PS[:, 2:5, 0:T], ACT.Copy)
                    with loop(act, N_KEYS - J2, 2) as j:
                        for u in range(2):
                            for s in range(2):
                                round_slab(act, j * 2, m0 + 2 * (J2 + u) + s + 1)
                            activate(j, J2 + u)

                @blk.vector
                def _(dve):
                    step = chain(dve, "dve_top")
                    per = 10
                    iota16 = cst[:, C_IOTA:C_IOTA + TOPK]
                    src = [cand[:, t, :] for t in range(TT)]
                    both = [(t, half) for t in range(TT) for half in range(2)]

                    def square(t, half):
                        return eq[:, t, half, :].rearrange("p (k a) -> p k a", k=TOPK)
                    dve.sem_inc(tk, 1)
                    with loop(dve, HEADS) as h:
                        def written(k):
                            dve.wait_ge(tk, h * per + (k + 1))
                        def split(s):
                            split_slab(dve, h * HEAD_SLABS, m0 + s + 1)
                        written(0)
                        for t in range(TT):
                            s0 = sv[:, t, h * 2, :][:, :, None].broadcast_to([P, TOPK, TOPK])
                            s1 = sv[:, t, h * 2 + 1, :][:, None, :].broadcast_to([P, TOPK, TOPK])
                            i = dve.tensor_tensor(cand[:, t, :].rearrange("p (a b) -> p a b", a=TOPK), s0, s1, ALU.add)
                        i.then_inc(tk, 1)
                        split(0)
                        top_step(dve, 0, src, 256, tk, h * per + 2)
                        split(1)
                        top_step(dve, 1, src, 256, tk, h * per + 3)
                        split(2)
                        top_step(dve, 2, src, 256, tk, h * per + 4)
                        top_step(dve, 3, src, 256, tk, h * per + 5)
                        split(3)
                        written(5)
                        dve.tensor_copy(gt[:, :, h, :], t8[:, :, :])
                        dve.tensor_scalar(abu[:, :, 0, :], i8[:, :, :], 4, None, ALU.logical_shift_right)
                        dve.tensor_scalar(abu[:, :, 1, :], i8[:, :, :], 15, None, ALU.bitwise_and).then_inc(tk, 1)
                        written(6)
                        dve.tensor_copy(abf[:, :, :, :], abu[:, :, :, :]).then_inc(tk, 1)
                        split(4)
                        written(7)
                        for t, half in both:
                            i = dve.tensor_tensor(square(t, half), abf[:, t, half, :][:, :, None].broadcast_to([P, TOPK, TOPK]),
                                                  iota16[:, None, :].broadcast_to([P, TOPK, TOPK]), ALU.is_equal)
                        i.then_inc(tk, 1)
                        split(5)
                        written(8)
                        for t, half in both:
                            key = si[:, t, h * 2 + half, :][:, None, :].broadcast_to([P, TOPK, TOPK])
                            i = dve.tensor_tensor(square(t, half), square(t, half), key, ALU.mult)
                        i.then_inc(tk, 1)
                        split(6)
                        written(9)
                        for t, half in both:
                            i = dve.tensor_reduce(eid[:, t, half, h, :], square(t, half), X, ALU.add)
                        i.then_inc(tk, 1)
                        split(7)
                    dve.wait_ge(tk, HEADS * per + 1)
                    step(dve.tensor_copy(gs[:, :, :, 0], gt[:, :, :, 0]))
                    for t in range(TT):
                        i = dve.tensor_tensor(gt[:, t, :, :], gt[:, t, :, :], gs[:, t, :, 0:1].broadcast_to([P, HEADS, TOPK]),
                                              ALU.subtract)
                    i.then_inc(sh, 1)
                    for s in range(2):
                        split_slab(dve, None, m0 + 2 * J1 + s + 1)
                    dve.wait_ge(g_exp, 1)
                    step(dve.tensor_reduce(gs[:, :, :, 0], gt[:, :, :, :], X, ALU.add))
                    step(dve.reciprocal(gs[:, :, :, 1], gs[:, :, :, 0]))
                    for t in range(TT):
                        i = dve.tensor_tensor(gt[:, t, :, :], gt[:, t, :, :], gs[:, t, :, 1:2].broadcast_to([P, HEADS, TOPK]),
                                              ALU.mult)
                    i.then_inc(g_ready, 1)
                    for s in range(2, 4):
                        split_slab(dve, None, m0 + 2 * J1 + s + 1)
                    with loop(dve, N_U - 2 * J2, NRAW) as i:
                        for s in range(NRAW):
                            split_slab(dve, i, m0 + 2 * J2 + s + 1)

        GT = 4
        with ExitStack() as ph:
            row_hot = buf3("row_hot", [P, 2, GT, N_KEYS], F, ph)
            col_hot = buf3("col_hot", [P, 2, GT, N_KEYS], F, ph)
            col_of = buf3("col_of", [P, 2, GT], F, ph)
            far = buf3("far", [P, 2, GT // 2, N_KEYS], F, ph)
            rows_made, cols_made, cols_made_act, dense, weighed, col_in, squared = (
                sem(x + "_g") for x in ("rows_made", "cols_made", "cols_made_act", "dense", "weighed", "col_in", "squared"))
            iota = cst[:, C_IOTA:C_IOTA + N_KEYS]
            NG = T // GT
            with stage() as blk:
                @blk.gpsimd
                def _(pool):
                    clear_last_stage(pool)
                    pool.sem_inc(dense, 2)
                    with loop(pool, NG, 2) as g:
                        for u in range(2):
                            pool.tensor_copy(col_of[:, u, :], pick[:, 1, ds(g * GT + u * GT, GT)]).then_inc(col_in, 1)
                            pool.wait_ge(dense, g + (u + 1))
                            pool.wait_ge(col_in, g + (u + 1))
                            carry(pool)
                            for t in range(GT // 2):
                                i = pool.tensor_scalar(col_hot[:, u, t, :], iota, col_of[:, u, t:t + 1], None, ALU.is_equal)
                            i.then_inc(cols_made, 1)

                @blk.scalar
                def _(act):
                    with loop(act, NG, 2) as g:
                        for u in range(2):
                            for t in range(GT // 2):
                                i = act.activation(far[:, u, t, :], iota, ACT.Square, scale=-1.0,
                                                   bias=pick[:, 1, ds(g * GT + (u * GT + GT // 2 + t), 1)])
                            i.then_inc(squared, 1)
                            act.wait_ge(dense, g + (u + 1))
                            act.wait_ge(squared, g + (u + 1))
                            act.activation(col_hot[:, u, GT // 2:, :], far[:, u, :, :], ACT.Relu, scale=-1.0, bias=1.0)\
                               .then_inc(cols_made_act, 1)

                @blk.vector
                def _(dve):
                    def rows(reg, n):
                        for t in range(GT):
                            at = n * GT + t
                            tok = slice(at, at + 1) if reg is None else ds(reg * GT + at, 1)
                            i = dve.tensor_scalar(row_hot[:, n % 2, t, :], iota, pick[:, 0, tok], pick[:, 2, tok],
                                                  ALU.is_equal, ALU.mult)
                        i.then_inc(rows_made, 1)

                    def multiply(reg, n):
                        dve.wait_ge(dense, n + 3 if reg is None else reg + (n + 3))
                        at = slice(n * GT, n * GT + GT) if reg is None else ds(reg * GT + n * GT, GT)
                        dve.tensor_tensor(wt[:, :, at], wt[:, :, at], PS[:, 2 + n % 2, :].rearrange("p (t j) -> p j t", t=GT),
                                          ALU.mult).then_inc(weighed, 1)
                    rows(None, 0)
                    rows(None, 1)
                    with loop(dve, NG - 2, 2) as g:
                        for u in range(2):
                            multiply(g, u)
                            rows(g, u + 2)
                    multiply(None, NG - 2)
                    multiply(None, NG - 1)

                @blk.tensor
                def _(pe):
                    pe.sem_inc(weighed, 2)
                    with loop(pe, NG, 2) as g:
                        for u in range(2):
                            pe.wait_ge(weighed, g + (u + 1))
                            pe.wait_ge(rows_made, g + (u + 1))
                            pe.wait_ge(cols_made, g + (u + 1))
                            pe.wait_ge(cols_made_act, g + (u + 1))
                            for t in range(GT):
                                last = pe.matmul(PS[:, 2 + u, t * N_KEYS:(t + 1) * N_KEYS], row_hot[:, u, t, :],
                                                 col_hot[:, u, t, :], start=True, stop=True)
                            last.then_inc(dense, 1)

        with ExitStack() as ph:
            wj_hi = [buf3(f"wj_hi{i}", [P, T], R, ph) for i in range(2)]
            wj_lo = [buf3(f"wj_lo{i}", [P, T], R, ph) for i in range(2)]
            hb = nc.alloc_sbuf_tensor_at("hb", [P, TT, D], F, offset=h_hi_at)
            par = [nc.alloc_sbuf_tensor_at(f"parc{i}", [P, D], F, offset=h_hi_at + (TT + i) * D * 4) for i in range(2)]
            wj_round, wj_split, late_in, ff_done, asked, given, ready, out_done = (
                sem(x + "_6") for x in ("wj_round", "wj_split", "late_in", "ff_done", "asked", "given", "ready", "out_done"))
            m0 = base["v"]
            with stage() as blk:
                @blk.sync
                def _(sp):
                    load_slabs(sp, src_v, base["v"], NRAW, N_V)
                    for t in range(TT):
                        sp.wait_ge(ready, t + 1)
                        sp.dma_start(io["out"][t * P:(t + 1) * P, :], hb[:, t, :]).then_inc(out_done, 16)
                    sp.wait_ge(out_done, 32)

                @blk.gpsimd
                def _(pool):
                    clear_last_stage(pool)
                    pool.wait_ge(h_stored, 16)
                    pool.dma_start(hb[:, :, :], h_dram).then_inc(late_in, 16)
                    for i, name in enumerate(("ln2_g", "ln2_b")):
                        pool.dma_start(par[i][:, :], bcast(io[name])).then_inc(late_in, 16)

                def split_weights(act, dve, j, u):
                    n = u if j is None else j + u
                    if act is not None:
                        wait_multiplied(act, None if j is None else j * 2, m0 - 4 + 2 * u + 2)
                        act.activation(wj_hi[u % 2][:, :], wt[:, n, :], ACT.Copy).then_inc(wj_round, 1)
                    if dve is not None:
                        dve.wait_ge(wj_round, n + 1)
                        dve.tensor_tensor(wj_lo[u % 2][:, :], wt[:, n, :], wj_hi[u % 2][:, :].bitcast(F), ALU.subtract)\
                           .then_inc(wj_split, 1)

                @blk.scalar
                def _(act):
                    def pair(j, last):
                        for u in range(2):
                            split_weights(act, None, j, u)
                            for s in range(2):
                                if not (last and u == 1 and s == 1):
                                    round_slab(act, None if j is None else j * 2, m0 + 2 * u + s + 1)
                    with loop(act, N_KEYS - 2, 2) as j:
                        pair(j, False)
                    for u in range(2):
                        split_weights(act, None, None, N_KEYS - 2 + u)
                        for s in range(2 - u):
                            round_slab(act, None, m0 + 2 * (N_KEYS - 2 + u) + s + 1)
                    for t in range(TT):
                        act.wait_ge(asked, t + 1)
                        act.activation(mv[:, t, 3:4], mv[:, t, 2:3], ACT.Sqrt).then_inc(given, 1)

                @blk.vector
                def _(dve):
                    step = chain(dve, "dve_last")
                    with loop(dve, N_KEYS - 2, 2) as j:
                        for u in range(2):
                            split_weights(None, dve, j, u)
                            for s in range(2):
                                split_slab(dve, j * 2, m0 + 2 * u + s + 1)
                    for u in range(2):
                        split_weights(None, dve, None, N_KEYS - 2 + u)
                        for s in range(2 - u):
                            split_slab(dve, None, m0 + 2 * (N_KEYS - 2 + u) + s + 1)
                    dve.wait_ge(late_in, 48)
                    wait_multiplied(dve, None, m0 + N_V)
                    for t in range(TT):
                        for c in range(4):
                            hh = hb[:, t, c * 512:(c + 1) * 512]
                            i = dve.scalar_tensor_tensor(hh, hh, ALPHA, PS[:, 4 * t + c, :], ALU.mult, ALU.add)
                        step(i)
                        norm_stats(dve, step, hb, t, asked)
                    for t in range(TT):
                        norm_apply(dve, step, hb, t, given, 0, par[0], par[1]).then_inc(ready, 1)

                @blk.tensor
                def _(pe):
                    def expert_slab(j, m, n, a, first, last_one):
                        if a == 0:
                            pe.wait_ge(wj_split, n + 1 if j is None else j + (n + 1))
                        for c in range(2):
                            pe.wait_ge(lo_ready, halves(None if j is None else j * 2, m) + (c + 1))
                            col = slice(c * 512, (c + 1) * 512)
                            for t in range(TT):
                                tok = slice(t * P, (t + 1) * P)
                                last = mm3(pe, PS[:, 4 * t + 2 * a + c, :], (wj_hi[n % 2][:, tok], wj_lo[n % 2][:, tok]),
                                           (w_hi[m % 2][:, col], w_lo[m % 2][:, col]), first, last_one)
                            last.then_inc(multiplied, 1)
                    for u in range(2):
                        for a in range(2):
                            expert_slab(None, m0 + 2 * u + a, u, a, u == 0, False)
                    with loop(pe, N_KEYS - 4, 2) as j:
                        for u in range(2):
                            for a in range(2):
                                expert_slab(j, m0 + 4 + 2 * u + a, 2 + u, a, False, False)
                    for n in range(N_KEYS - 2, N_KEYS):
                        for a in range(2):
                            expert_slab(None, m0 + 2 * n + a, n, a, False, n == N_KEYS - 1)
        top.close()


NAMES = ["x", "ctx", "c_cols", "consts", "mod_cols", "lam_in", "w_mod_s", "w_in_a", "w_in_b", "rpb_e", "subln_g",
         "w_out_s", "final_g", "ln_in_g", "ln_in_b", "w_in2_s", "conv_cols", "w_gate_cols", "b_gate", "mh_g", "w_out2_s",
         "ln1_g", "ln1_b", "wq_s", "keys", "u_s", "v", "ln2_g", "ln2_b"]


def constants():
    import numpy as np
    c = np.zeros((P, C_ALL), np.float32)
    p = np.arange(P)
    c[p, C_IDENT + p] = 1
    c[:, C_ONES:C_ONES + P] = 1
    c[:, C_TRI:C_TRI + P] = np.where(p[:, None] <= p[None, :], 0.0, MASKED)
    c[:, C_IOTA:C_IOTA + P] = p
    f = p % 64
    partner = np.where(p % 32 < 16, p + 16, p - 16)
    c[partner, C_PERM + p] = 1
    inv = (np.float32(10000.0) ** (-np.arange(16, dtype=np.float32) / np.float32(16))).astype(np.float32)
    t = np.arange(T)
    pos = np.where((f < 32)[:, None], (t // 64)[None, :], (t % 64)[None, :]).astype(np.float32)
    ang = pos * inv[p % 16][:, None]
    c[:, C_COS:C_COS + T] = np.cos(ang)
    c[:, C_SIN:C_SIN + T] = np.sin(ang) * np.where(p % 32 < 16, -1, 1)[:, None]
    j, col = (p % 64)[:, None], np.arange(64)[None, :]
    c0 = np.clip(j - 8, 0, 48)
    c[:, C_NAMASK:C_NAMASK + 64] = np.where((col >= c0) & (col < c0 + 16), 0.0, MASKED)
    c[np.arange(8), C_EYE8 + np.arange(8)] = 1
    return c


def feature_slabs(w):
    import numpy as np
    n = w.shape[1] // P
    return np.ascontiguousarray(w.reshape(2, 8, P, n, P).transpose(3, 0, 2, 1, 4)).reshape(2 * n, P, SLAB)


def token_slabs(w):
    import numpy as np
    n = w.shape[1] // 512
    return np.ascontiguousarray(w.reshape(8, 2, P, n, 512).transpose(3, 0, 2, 1, 4)).reshape(8 * n, P, SLAB)


def cols(v):
    return v.reshape(-1, P).T


def lay_out(i):
    import numpy as np
    w_in, w2 = i["w_in"][0], i["w_in_2"][0]
    pad = np.pad(i["rpb"][0], ((0, 0), (0, 0), (48, 48)))
    rpb_e = np.stack([pad[:, :, 63 - j:127 - j] for j in range(64)], axis=1).reshape(HEADS, 64, 15 * 64)
    half = lambda o: np.concatenate([feature_slabs(w_in[:, o:o + 2 * WA]), token_slabs(w_in[:, o + 2 * WA:o + 4 * WA])])
    conv = feature_slabs(w2[:, 0:3 * WA]).reshape(3, 8, 2, P, SLAB).transpose(1, 0, 2, 3, 4).reshape(48, P, SLAB)
    return {
        "x": i["x"][0], "ctx": i["ctx"][0],
        "c_cols": np.stack([cols(i["c"][0]), cols(i["c_ctx"])], axis=2),
        "consts": constants(),
        "mod_cols": np.concatenate([cols(i["b_mod"][0]), cols(i["norm_g"][0])], axis=1),
        "lam_in": np.concatenate([i["lam_q1"][0], i["lam_k1"][0], i["lam_q2"][0], i["lam_k2"][0]])[None],
        "w_mod_s": token_slabs(i["w_mod"][0]),
        "w_in_a": half(0), "w_in_b": half(4 * WA),
        "rpb_e": rpb_e, "subln_g": i["subln_g"],
        "w_out_s": token_slabs(i["w_out"][0]),
        "final_g": i["final_g"][None], "ln_in_g": i["ln_in_g_2"][None], "ln_in_b": i["ln_in_b_2"][None],
        "w_in2_s": np.concatenate([conv, feature_slabs(w2[:, 3 * WA:5 * WA]), token_slabs(w2[:, 5 * WA:7 * WA])]),
        "conv_cols": np.concatenate([cols(i["conv_w_2"][0, n]) for n in range(3)] + [cols(i["conv_b_2"][0])], axis=1),
        "w_gate_cols": w2[:, 7 * WA:].reshape(KT, P, 16).transpose(1, 0, 2).reshape(P, KT * 16),
        "b_gate": i["b_gate_2"], "mh_g": i["mh_norm_g_2"],
        "ln1_g": i["ln1_g_2"], "ln1_b": i["ln1_b_2"], "ln2_g": i["ln2_g_2"], "ln2_b": i["ln2_b_2"],
        "keys": i["peer_keys_2"][0].reshape(2 * HEADS, N_KEYS, P).transpose(2, 0, 1),
        "w_out2_s": token_slabs(i["w_out_2"][0]), "wq_s": feature_slabs(i["peer_wq_2"][0]),
        "u_s": np.ascontiguousarray(i["peer_u_2"][0].reshape(N_KEYS, N_KEYS, 2, 8, P).transpose(1, 2, 4, 3, 0)).reshape(2 * N_KEYS, P, SLAB),
        "v": i["peer_v_2"][0],
    }


def kernel(**inputs):
    import numpy as np
    import concourse.bacc as bacc
    from concourse.bass_utils import run_bass_kernel_spmd

    nc = bacc.Bacc("TRN2", target_bir_lowering=False, num_devices=1)
    laid = lay_out({k: np.asarray(v) for k, v in inputs.items()})
    arrays, io = {}, {}
    for name in NAMES:
        a = np.ascontiguousarray(laid[name])
        arrays[f"in_{name}"] = a
        io[name] = nc.dram_tensor(f"in_{name}", a.shape, mybir.dt.from_np(a.dtype), kind="ExternalInput").ap()
    io["out"] = nc.dram_tensor("out_0_dram", (T, D), mybir.dt.float32, kind="ExternalOutput").ap()
    peer_block_kernel(nc, io)
    r = run_bass_kernel_spmd(nc, [arrays], core_ids=[0])
    return r.results[0]["out_0_dram"].reshape(1, T, D)
```
